# Optimizing a Trainium2 kernel written in Bass

```python
import math
import jax
import jax.numpy as jnp
from jax import lax
import numpy as np

D_MODEL = 1024
BATCH = 1
SEQ = 1024
DEPTH = 2

GRID_W = 64
CTX_LEN = 256
RMS_EPS = 1e-6

DN_HEADS = 4
DN_DK = 128
DN_DV = 128
DN_CHUNK = 64
QKV_CONV = 3
SC_WIDTH = 512
SC_CONV = 3
DN_QK_W = DN_HEADS * DN_DK
DN_V_W = DN_HEADS * DN_DV
QKV_W = 2 * DN_QK_W + DN_V_W
C_GATE = QKV_W
C_ALPHA = C_GATE + DN_V_W
C_BETA = C_ALPHA + 2 * DN_HEADS
C_SC = C_BETA + 2 * DN_HEADS
IN0_COLS = C_SC + 3 * SC_WIDTH
MIX0_WIDTH = DN_V_W + SC_WIDTH
ATT_HEADS = 16
ATT_KV_HEADS = 4
GQA_GROUP = ATT_HEADS // ATT_KV_HEADS
ATT_HD = 64
WINDOW = 128
Q_BLOCK = 128
ROPE_BASE = 10000.0
IN1_COLS = (ATT_HEADS + 2 * ATT_KV_HEADS) * ATT_HD
MIX1_WIDTH = ATT_HEADS * ATT_HD
N_GROUPS = 4
EXPERTS_PER_GROUP = 8
N_EXPERTS = N_GROUPS * EXPERTS_PER_GROUP
TOP_K = 2
D_EXPERT = 512
MOE_BLOCK = 128

N_EVEN = (DEPTH + 1) // 2
N_ODD = DEPTH // 2

kernel_name = 'hybrid_deltanet_shortconv_swa_hmoe_prefix_dit'

F32 = jnp.float32

def rmsnorm(x, w):
    xf = x.astype(F32)
    y = xf * lax.rsqrt(jnp.mean(xf * xf, axis=-1, keepdims=True) + RMS_EPS)
    return (y * w.astype(F32)).astype(x.dtype)

def modulate(h, shift, scale):
    return h * (1.0 + scale) + shift

def l2norm(t):
    tf = t.astype(F32)
    return tf * lax.rsqrt(jnp.sum(tf * tf, axis=-1, keepdims=True) + RMS_EPS)

def dwconv_centred(x, w):
    taps = w.shape[0]
    p = taps // 2
    L = x.shape[1]
    xp = jnp.pad(x, ((0, 0), (p, p), (0, 0)))
    out = xp[:, 0:L] * w[0]
    for i in range(1, taps):
        out = out + xp[:, i:i + L] * w[i]
    return out

def gated_delta_rule(q, k, v, log_a, beta, s0):
    Bn, L, H, dk = q.shape
    dv = v.shape[-1]
    n = L // DN_CHUNK

    def to_chunks(t):
        t = t.astype(F32).reshape((Bn, n, DN_CHUNK, H) + t.shape[3:])
        return jnp.moveaxis(t, (1, 3), (0, 2))

    qc = to_chunks(q) * (dk ** -0.5)
    kc = to_chunks(k)
    vc = to_chunks(v)
    g = jnp.cumsum(to_chunks(log_a), axis=-1)
    bc = to_chunks(beta)
    idx = jnp.arange(DN_CHUNK)
    incl = idx[:, None] >= idx[None, :]
    strict = idx[:, None] > idx[None, :]
    decay = jnp.exp(jnp.where(incl, g[..., :, None] - g[..., None, :], -jnp.inf))
    kb = kc * bc[..., None]
    a_mat = jnp.where(strict, jnp.einsum('nbhid,nbhjd->nbhij', kb, kc) * decay, 0.0)
    eye = jnp.eye(DN_CHUNK, dtype=F32)
    t_mat = lax.linalg.triangular_solve(eye + a_mat, jnp.broadcast_to(eye, a_mat.shape),
                                        left_side=True, lower=True, unit_diagonal=True)
    u = jnp.einsum('nbhij,nbhjd->nbhid', t_mat, vc * bc[..., None])
    w = jnp.einsum('nbhij,nbhjd->nbhid', t_mat, kb * jnp.exp(g)[..., None])
    qk = jnp.where(incl, jnp.einsum('nbhid,nbhjd->nbhij', qc, kc) * decay, 0.0)
    q_dec = qc * jnp.exp(g)[..., None]
    k_dec = kc * jnp.exp(g[..., -1:] - g)[..., None]
    g_last = jnp.exp(g[..., -1])

    def step(s, inp):
        qd, kd, uc, wc, qkc, gl = inp
        v_new = uc - jnp.einsum('bhcd,bhde->bhce', wc, s)
        o = jnp.einsum('bhcd,bhde->bhce', qd, s) + jnp.einsum('bhij,bhje->bhie', qkc, v_new)
        s = s * gl[..., None, None] + jnp.einsum('bhcd,bhce->bhde', kd, v_new)
        return s, o

    s_fin, o = lax.scan(step, s0.astype(F32), (q_dec, k_dec, u, w, qk, g_last))
    o = jnp.moveaxis(o, (0, 2), (1, 3)).reshape(Bn, L, H, dv)
    return o, s_fin

def mixer_ab(a, s0_fwd, s0_bwd, w_in, conv_qkv, conv_sc, a_log, dt_bias, out_norm, w_out):
    B, L, _ = a.shape
    z = a @ w_in
    qkv, gate, a_in, b_in, sc = jnp.split(z, [C_GATE, C_ALPHA, C_BETA, C_SC], axis=-1)
    qkv = jax.nn.silu(dwconv_centred(qkv, conv_qkv))
    q, k, v = jnp.split(qkv, [DN_QK_W, 2 * DN_QK_W], axis=-1)
    q = l2norm(q.reshape(B, L, DN_HEADS, DN_DK))
    k = l2norm(k.reshape(B, L, DN_HEADS, DN_DK))
    v = v.reshape(B, L, DN_HEADS, DN_DV)
    log_a = -jnp.exp(a_log.astype(F32)) * jax.nn.softplus(
        a_in.astype(F32).reshape(B, L, 2, DN_HEADS) + dt_bias.astype(F32))
    beta = jax.nn.sigmoid(b_in.astype(F32)).reshape(B, L, 2, DN_HEADS)
    o_f, s_f = gated_delta_rule(q, k, v, log_a[:, :, 0], beta[:, :, 0], s0_fwd)
    rev = lambda t: jnp.flip(t, axis=1)
    o_b, s_b = gated_delta_rule(rev(q), rev(k), rev(v), rev(log_a[:, :, 1]), rev(beta[:, :, 1]), s0_bwd)
    o = (o_f + rev(o_b)).astype(a.dtype)
    o = rmsnorm(o, out_norm) * jax.nn.silu(gate.reshape(B, L, DN_HEADS, DN_DV))
    b_g, c_g, h_in = jnp.split(sc, 3, axis=-1)
    y_sc = b_g * dwconv_centred(c_g * h_in, conv_sc)
    y = jnp.concatenate([o.reshape(B, L, DN_V_W), y_sc], axis=-1) @ w_out
    return y, s_f, s_b

def axial_rope(t, rows, cols):
    half = t.shape[-1] // 2
    nf = half // 2
    inv = jnp.power(ROPE_BASE, -jnp.arange(nf, dtype=F32) / nf)
    bshape = (1, t.shape[1]) + (1,) * (t.ndim - 3) + (nf,)

    def rot(u, pos):
        ang = (pos.astype(F32)[:, None] * inv).reshape(bshape)
        cos, sin = jnp.cos(ang), jnp.sin(ang)
        u1, u2 = u[..., :nf].astype(F32), u[..., nf:].astype(F32)
        return jnp.concatenate([u1 * cos - u2 * sin, u1 * sin + u2 * cos], axis=-1)

    return jnp.concatenate([rot(t[..., :half], rows), rot(t[..., half:], cols)], axis=-1).astype(t.dtype)

def split_qkv(z):
    B, L, _ = z.shape
    q, k, v = jnp.split(z, [MIX1_WIDTH, MIX1_WIDTH + ATT_KV_HEADS * ATT_HD], axis=-1)
    return (q.reshape(B, L, ATT_KV_HEADS, GQA_GROUP, ATT_HD),
            k.reshape(B, L, ATT_KV_HEADS, ATT_HD),
            v.reshape(B, L, ATT_KV_HEADS, ATT_HD))

def sink_attend(q, k_parts, v_parts, masks, sink_g):
    scale = ATT_HD ** -0.5
    logits = []
    for kp, m in zip(k_parts, masks):
        s = jnp.einsum('bqkgd,bskd->bkgqs', q, kp).astype(F32) * scale
        if m is not None:
            s = jnp.where(m, s, -jnp.inf)
        logits.append(s)
    B, Q = q.shape[:2]
    sink_col = jnp.broadcast_to(sink_g.astype(F32)[None, :, :, None, None], (B, ATT_KV_HEADS, GQA_GROUP, Q, 1))
    p = jax.nn.softmax(jnp.concatenate(logits + [sink_col], axis=-1), axis=-1)
    out = None
    off = 0
    for vp in v_parts:
        n = vp.shape[1]
        term = jnp.einsum('bkgqs,bskd->bqkgd', p[..., off:off + n].astype(vp.dtype), vp)
        out = term if out is None else out + term
        off += n
    return out

def mixer_c(a_lat, a_ctx, rows, cols, w_in, sink, w_out, ctx_out):
    B, L, _ = a_lat.shape
    Lc = a_ctx.shape[1]
    sink_g = sink.reshape(ATT_KV_HEADS, GQA_GROUP)
    q, k, v = split_qkv(a_lat @ w_in)
    qc, kc, vc = split_qkv(a_ctx @ w_in)
    q = axial_rope(q, rows, cols)
    k = axial_rope(k, rows, cols)
    pad = ((0, 0), (WINDOW, WINDOW), (0, 0), (0, 0))
    kp = jnp.pad(k, pad)
    vp = jnp.pad(v, pad)
    span = Q_BLOCK + 2 * WINDOW
    offs_q = jnp.arange(Q_BLOCK)
    offs_k = jnp.arange(span) - WINDOW

    def block(start):
        qb = lax.dynamic_slice_in_dim(q, start, Q_BLOCK, axis=1)
        kb = lax.dynamic_slice_in_dim(kp, start, span, axis=1)
        vb = lax.dynamic_slice_in_dim(vp, start, span, axis=1)
        qpos = start + offs_q
        kpos = start + offs_k
        valid = ((jnp.abs(qpos[:, None] - kpos[None, :]) <= WINDOW)
                 & (kpos[None, :] >= 0) & (kpos[None, :] < L))
        return sink_attend(qb, (kb, kc), (vb, vc), (valid, None), sink_g)

    o = lax.map(block, jnp.arange(L // Q_BLOCK) * Q_BLOCK)
    y_lat = jnp.moveaxis(o, 0, 1).reshape(B, L, MIX1_WIDTH) @ w_out
    if not ctx_out:
        return y_lat, None
    oc = sink_attend(qc, (kc,), (vc,), (None,), sink_g)
    y_ctx = oc.reshape(B, Lc, MIX1_WIDTH) @ w_out
    return y_lat, y_ctx

def expert_ffn_sorted(x, expert_id, weights, w1, w3, w2):
    T, D = x.shape
    A = T * TOP_K
    e_flat = expert_id.reshape(A)
    tok = jnp.repeat(jnp.arange(T, dtype=jnp.int32), TOP_K)
    order = jnp.argsort(e_flat)
    e_sorted = e_flat[order]
    tok_sorted = tok[order]
    counts = jnp.zeros((N_EXPERTS,), jnp.int32).at[e_flat].add(1)
    padded = ((counts + MOE_BLOCK - 1) // MOE_BLOCK) * MOE_BLOCK
    start = jnp.cumsum(counts) - counts
    pend = jnp.cumsum(padded)
    pstart = pend - padded
    dest = pstart[e_sorted] + (jnp.arange(A, dtype=jnp.int32) - start[e_sorted])
    n_blocks = -(-A // MOE_BLOCK) + N_EXPERTS
    rows_total = n_blocks * MOE_BLOCK
    buf = jnp.zeros((rows_total, D), x.dtype).at[dest].set(x[tok_sorted])
    blk_start = jnp.arange(n_blocks, dtype=jnp.int32) * MOE_BLOCK
    blk_expert = jnp.minimum(jnp.searchsorted(pend, blk_start, side='right'), N_EXPERTS - 1)

    def run(args):
        xb, e = args
        h = jax.nn.silu(xb @ w1[e]) * (xb @ w3[e])
        return h @ w2[e]

    y = lax.map(run, (buf.reshape(n_blocks, MOE_BLOCK, D), blk_expert)).reshape(rows_total, D)
    contrib = y[dest] * weights.reshape(A)[order][:, None].astype(y.dtype)
    return jnp.zeros((T, D), x.dtype).at[tok_sorted].add(contrib)

def hier_moe(x, w_group, w_expert, w1, w3, w2):
    T = x.shape[0]
    g_logits = (x @ w_group).astype(F32)
    g_prob = jax.nn.softmax(g_logits, axis=-1)
    g_sel = jnp.argmax(g_logits, axis=-1).astype(jnp.int32)
    p_group = jnp.take_along_axis(g_prob, g_sel[:, None], axis=-1)
    e_logits = (x @ w_expert).astype(F32).reshape(T, N_GROUPS, EXPERTS_PER_GROUP)
    e_in = jnp.take_along_axis(e_logits, g_sel[:, None, None], axis=1)[:, 0]
    top_p, top_i = lax.top_k(jax.nn.softmax(e_in, axis=-1), TOP_K)
    weights = p_group * top_p / jnp.sum(top_p, axis=-1, keepdims=True)
    expert_id = g_sel[:, None] * EXPERTS_PER_GROUP + top_i.astype(jnp.int32)
    return expert_ffn_sorted(x, expert_id, weights, w1, w3, w2)

def setup_inputs(seed: int = 0) -> dict:
    key = jax.random.key(seed)
    ks = jax.random.split(key, 24)
    D = D_MODEL

    def nrm(k, shape, fan):
        return jax.random.normal(k, shape, F32) * (fan ** -0.5)

    def std(k, shape):
        return jax.random.normal(k, shape, F32)

    dt = jnp.exp(jax.random.uniform(ks[13], (N_EVEN, 2, DN_HEADS), F32,
                                    minval=math.log(1e-3), maxval=math.log(1e-1)))
    return {
        'x': std(ks[0], (BATCH, SEQ, D)),
        'c': std(ks[1], (BATCH, D)),
        'ctx': std(ks[2], (BATCH, CTX_LEN, D)),
        'c_ctx': std(ks[3], (D,)),
        'ada_w': nrm(ks[4], (DEPTH, D, 6 * D), D),
        'ada_b': 0.02 * std(ks[5], (DEPTH, 6 * D)),
        'norm_mix': 1.0 + 0.1 * std(ks[6], (DEPTH, D)),
        'norm_ffn': 1.0 + 0.1 * std(ks[7], (DEPTH, D)),
        'norm_final': 1.0 + 0.1 * std(ks[8], (D,)),
        'ab_w_in': nrm(ks[9], (N_EVEN, D, IN0_COLS), D),
        'ab_conv_qkv': nrm(ks[10], (N_EVEN, QKV_CONV, QKV_W), QKV_CONV),
        'ab_conv_sc': nrm(ks[11], (N_EVEN, SC_CONV, SC_WIDTH), SC_CONV),
        'ab_a_log': jnp.log(jax.random.uniform(ks[12], (N_EVEN, 2, DN_HEADS), F32, minval=1.0, maxval=16.0)),
        'ab_dt_bias': dt + jnp.log(-jnp.expm1(-dt)),
        'ab_out_norm': 1.0 + 0.1 * std(ks[14], (N_EVEN, DN_DV)),
        'ab_w_out': nrm(ks[15], (N_EVEN, MIX0_WIDTH, D), MIX0_WIDTH),
        'at_w_in': nrm(ks[16], (N_ODD, D, IN1_COLS), D),
        'at_sink': 0.5 * std(ks[17], (N_ODD, ATT_HEADS)),
        'at_w_out': nrm(ks[18], (N_ODD, MIX1_WIDTH, D), MIX1_WIDTH),
        'moe_w_group': nrm(ks[19], (DEPTH, D, N_GROUPS), D),
        'moe_w_expert': nrm(ks[20], (DEPTH, D, N_EXPERTS), D),
        'moe_w1': nrm(ks[21], (DEPTH, N_EXPERTS, D, D_EXPERT), D),
        'moe_w3': nrm(ks[22], (DEPTH, N_EXPERTS, D, D_EXPERT), D),
        'moe_w2': nrm(ks[23], (DEPTH, N_EXPERTS, D_EXPERT, D), D_EXPERT),
    }

def reference(x, c, ctx, c_ctx, ada_w, ada_b, norm_mix, norm_ffn, norm_final,
              ab_w_in, ab_conv_qkv, ab_conv_sc, ab_a_log, ab_dt_bias, ab_out_norm, ab_w_out,
              at_w_in, at_sink, at_w_out,
              moe_w_group, moe_w_expert, moe_w1, moe_w3, moe_w2):
    B, L, D = x.shape
    Lc = ctx.shape[1]
    n_rows = L // GRID_W
    rows = jnp.repeat(jnp.arange(n_rows, dtype=jnp.int32), GRID_W)
    cols = jnp.tile(jnp.arange(GRID_W, dtype=jnp.int32), n_rows)
    s_zero = jnp.zeros((B, DN_HEADS, DN_DK, DN_DV), F32)

    h_lat, h_ctx = x, ctx
    sc_lat = jax.nn.silu(c)
    sc_ctx = jax.nn.silu(c_ctx)
    for l in range(DEPTH):
        last = l == DEPTH - 1
        i = l // 2
        mod_lat = (sc_lat @ ada_w[l] + ada_b[l])[:, None, :]
        mod_ctx = sc_ctx @ ada_w[l] + ada_b[l]
        sh1, s1, g1, sh2, s2, g2 = jnp.split(mod_lat, 6, axis=-1)
        csh1, cs1, cg1, csh2, cs2, cg2 = jnp.split(mod_ctx, 6, axis=-1)

        a_lat = modulate(rmsnorm(h_lat, norm_mix[l]), sh1, s1)
        a_ctx = modulate(rmsnorm(h_ctx, norm_mix[l]), csh1, cs1)
        if l % 2 == 0:
            y_ctx, s_f, s_b = mixer_ab(a_ctx, s_zero, s_zero, ab_w_in[i], ab_conv_qkv[i], ab_conv_sc[i],
                                       ab_a_log[i], ab_dt_bias[i], ab_out_norm[i], ab_w_out[i])
            y_lat, _, _ = mixer_ab(a_lat, s_f, s_b, ab_w_in[i], ab_conv_qkv[i], ab_conv_sc[i],
                                   ab_a_log[i], ab_dt_bias[i], ab_out_norm[i], ab_w_out[i])
        else:
            y_lat, y_ctx = mixer_c(a_lat, a_ctx, rows, cols, at_w_in[i], at_sink[i], at_w_out[i],
                                   not last)
        h_lat = h_lat + g1 * y_lat

        f_lat = modulate(rmsnorm(h_lat, norm_ffn[l]), sh2, s2)
        if last:
            out = hier_moe(f_lat.reshape(B * L, D), moe_w_group[l], moe_w_expert[l],
                           moe_w1[l], moe_w3[l], moe_w2[l])
            h_lat = h_lat + g2 * out.reshape(B, L, D)
        else:
            h_ctx = h_ctx + cg1 * y_ctx
            f_ctx = modulate(rmsnorm(h_ctx, norm_ffn[l]), csh2, cs2)
            tokens = jnp.concatenate([f_ctx.reshape(B * Lc, D), f_lat.reshape(B * L, D)], axis=0)
            out = hier_moe(tokens, moe_w_group[l], moe_w_expert[l], moe_w1[l], moe_w3[l], moe_w2[l])
            h_ctx = h_ctx + cg2 * out[:B * Lc].reshape(B, Lc, D)
            h_lat = h_lat + g2 * out[B * Lc:].reshape(B, L, D)
    return rmsnorm(h_lat, norm_final)


_drawn_inputs = setup_inputs


def setup_inputs(seed=0):
    import zlib

    import numpy as np

    out = dict(_drawn_inputs(seed))
    spreads = {}
    factors = {'at_sink': 8.0}
    for name, (base, spread) in spreads.items():
        noise = np.random.default_rng([zlib.crc32(name.encode()), seed]).standard_normal(out[name].shape)
        drawn = base * np.exp(spread * noise) if base else spread * noise
        out[name] = jnp.asarray(drawn.astype(out[name].dtype))
    for name, factor in factors.items():
        out[name] = (out[name] * factor).astype(out[name].dtype)
    return out
```

```python
from contextlib import ExitStack, contextmanager

import numpy as np

import concourse.bass as bass
import concourse.mybir as mybir

F32 = mybir.dt.float32
I32 = mybir.dt.int32
U32 = mybir.dt.uint32
ACT = mybir.ActivationFunctionType
ALU = mybir.AluOpType
AX = mybir.AxisListType

P = 128
D = 1024
KC = D // P
SEQ, CTX = 1024, 256
TOK = SEQ + CTX
NT = TOK // P
CT = CTX // P
LT = SEQ // P
EPS = 1e-6
NH = 4
W0 = NH * P
ATT_H, ATT_KV, HD = 16, 4, 64
ATT_COLS = (ATT_H + 2 * ATT_KV) * HD
WIN = 128
GROUPS, PER = 4, 8
NE = GROUPS * PER
FF = 512
FC = FF // P
LEVELS = 7
MODS = 6
OVER = (2 * TOK - NE) // P
SLOTS = (NE + OVER + OVER % 2) * P
PADTOK = TOK + 4
LAT0 = CTX + 2
SPANS = ((0, CTX), (CTX, 512), (CTX + 512, 512))


class Steps:

    def __init__(self, eng, sem, per=0):
        self.eng, self.sem, self.per, self.base, self.n = eng, sem, per, 0, 0

    def at(self, i):
        self.base, self.n = i * self.per, 0

    def link(self, ins):
        self.n += 1
        ins.then_inc(self.sem, 1)
        self.eng.wait_ge(self.sem, self.base + self.n)

    def end(self):
        assert self.n == self.per, f"{self.n} links in a pass, not {self.per}"


class Kernel:

    def __init__(self, nc, dram):
        self.nc, self.dram, self.ids = nc, dram, 0
        self.scopes, self.sems = [], []

    @contextmanager
    def scope(self):
        with ExitStack() as stack:
            self.scopes.append(stack)
            self.sems.append([])
            yield stack
            self.scopes.pop()
        if sems := self.sems.pop():
            self.nc.clear_and_free_semaphores(sems)
            self.nc.all_engine_barrier()

    def sb(self, name, shape, dt=F32):
        self.ids += 1
        return self.scopes[-1].enter_context(self.nc.sbuf_tensor(f"{name}_{self.ids}", list(shape), dt))

    def sem(self, name):
        self.ids += 1
        self.sems[-1].append(self.nc.alloc_semaphore(f"{name}_{self.ids}"))
        return self.sems[-1][-1]

    def block(self):
        return self.scopes[-1].enter_context(self.nc.Block())


def ds(i, n):
    return bass.ds(i, n)


def modulation(k, l):
    nc, dr = k.nc, k.dram
    RING, NW = 4, 512
    NN = MODS * D // NW
    c = k.sb("c", [P, 2, KC])
    sc = k.sb("silu_c", [P, KC, 2])
    w = [k.sb(f"ada_w{u}", [P, KC, NW]) for u in range(RING)]
    rows = k.sb("rows", [2, NN, NW])
    bias = k.sb("bias", [2, NN, NW])
    norms = k.sb("norms", [2, 2, D])
    c_in, c_silu = k.sem("c_in"), k.sem("c_silu")
    w_in = [k.sem(f"ada_w_in{u}") for u in range(RING)]
    consts_in = k.sem("consts_in")
    row_ready = [k.sem(f"row_ready{u}") for u in range(RING)]
    row_taken = [k.sem(f"row_taken{u}") for u in range(RING)]
    rows_done, rows_out, h_in = k.sem("rows_done"), k.sem("rows_out"), k.sem("h_in")
    block = k.block()

    @block.sync
    def _(sp):
        sp.dma_start(c[:, 0, :], dr["c_ctx"].rearrange("(p j) -> p j", p=P)).then_inc(c_in, 16)
        sp.dma_start(c[:, 1, :], dr["c"].rearrange("a (p j) -> (a p) j", p=P)).then_inc(c_in, 16)
        for v in range(2):
            sp.dma_start(bias[v:v + 1].rearrange("v n w -> v (n w)"), dr["ada_b"][l:l + 1]).then_inc(consts_in, 16)
            sp.dma_start(norms[v:v + 1, 0, :], dr["norm_mix"][l:l + 1]).then_inc(consts_in, 16)
            sp.dma_start(norms[v:v + 1, 1, :], dr["norm_ffn"][l:l + 1]).then_inc(consts_in, 16)
        src = dr["ada_w"][l].rearrange("(p j) n -> p j n", p=P)
        for u in range(RING):
            sp.dma_start(w[u][:], src[:, :, u * NW:(u + 1) * NW]).then_inc(w_in[u], 16)
        with sp.Fori(1, NN // RING) as i:
            for u in range(RING):
                sp.wait_ge(row_ready[u], i)
                sp.dma_start(w[u][:], src[:, :, ds(i * (RING * NW) + u * NW, NW)]).then_inc(w_in[u], 16)
        sp.wait_ge(rows_done, 2)
        sp.dma_start(dr["mods"][l], rows[:].rearrange("v n w -> v (n w)")).then_inc(rows_out, 16)
        sp.wait_ge(rows_out, 16)

    if l == 0:
        @block.gpsimd
        def _(pool):
            pool.dma_start(k.H[:, 0:CT, :], dr["ctx"].rearrange("b (t p) d -> p (b t) d", p=P)).then_inc(h_in, 16)
            pool.dma_start(k.H[:, CT:NT, :], dr["x"].rearrange("b (t p) d -> p (b t) d", p=P)).then_inc(h_in, 16)
            pool.dma_start(k.eye[:], dr["const_eye"]).then_inc(h_in, 16)
            pool.dma_start(k.tri[:], dr["const_tri"].rearrange("d p n -> p d n")).then_inc(h_in, 16)
            pool.wait_ge(h_in, 64)

    @block.tensor
    def _(pe):
        pe.wait_ge(c_silu, 1)
        with pe.Fori(0, NN // RING) as i:
            for u in range(RING):
                pe.wait_ge(w_in[u], (i + 1) * 16)
                pe.wait_ge(row_taken[u], i)
                for j in range(KC):
                    mm = pe.matmul(k.bank[u][0:2, :], sc[:, j, :], w[u][:, j, :],
                                   start=(j == 0), stop=(j == KC - 1))
                mm.then_inc(row_ready[u], 1)

    @block.scalar
    def _(act):
        act.wait_ge(c_in, 32)
        nc.scalar.activation(sc[:].rearrange("p j v -> p v j"), c[:], ACT.Silu).then_inc(c_silu, 1)

    @block.vector
    def _(dve):
        dve.wait_ge(consts_in, 96)
        with dve.Fori(0, NN // RING) as i:
            for u in range(RING):
                dve.wait_ge(row_ready[u], i + 1)
                nc.vector.tensor_tensor(rows[:, ds(i * RING + u, 1), :].rearrange("v a w -> v (a w)"),
                                        k.bank[u][0:2, :],
                                        bias[:, ds(i * RING + u, 1), :].rearrange("v a w -> v (a w)"),
                                        ALU.add).then_inc(row_taken[u], 1)
        for u in range(RING):
            dve.wait_ge(row_taken[u], NN // RING)
        rv = rows[:].rearrange("v (m a) w -> v m (a w)", m=MODS)
        for which in range(2):
            nc.vector.scalar_tensor_tensor(out=rv[:, 1 + 3 * which, :], in0=rv[:, 1 + 3 * which, :], scalar=1.0,
                                           in1=norms[:, which, :], op0=ALU.add, op1=ALU.mult).then_inc(rows_done, 1)


def spread_row(k, eng, dst, l, v, m, done):
    row = k.dram["mods"][l, v:v + 1, m * D:(m + 1) * D]
    eng.dma_start(dst, row.to_broadcast([P, D])).then_inc(done, 16)


def norm_mod(k, l, which, first, aT=None, logits=None):
    nc, dr, H = k.nc, k.dram, k.H
    vs = (0, 1) if first == 0 else (1,)
    A = k.sb("scale_rows", [P, 2, D])
    S = k.sb("shift_rows", [P, 2, D])
    sq = k.sb("squares", [P, 2, D])
    ssq = k.sb("sumsq", [P, 2])
    rstd = k.sb("rstd", [P, 2])
    a = [k.sb(f"a{u}", [P, D]) for u in range(2)]
    rows_in, sumsq_ready, a_ready = k.sem("rows_in"), k.sem("sumsq_ready"), k.sem("a_ready")
    a_turned, aT_ready = k.sem("a_turned"), k.sem("aT_ready")
    a_stored = [k.sem(f"a_stored{u}") for u in range(2)]
    order, mean_ready, root_ready = k.sem("dve_order"), k.sem("mean_ready"), k.sem("root_ready")
    moe = logits is not None
    NL = GROUPS + NE
    if moe:
        wr = k.sb("w_route", [P, KC, NL])
        fT = k.sb("fT", [P, 2, KC, P])
        logits_ready, logits_taken = k.sem("logits_ready"), k.sem("logits_taken")
    block = k.block()

    def passes(eng, body):
        if first == 0:
            body(0, 0, 0)
        with eng.Fori(1, NT // 2) as i:
            body(i, i if first == 0 else i - 1, 1)

    @block.sync
    def _(sp):
        for v in vs:
            spread_row(k, sp, A[:, v, :], l, v, 1 + 3 * which, rows_in)
            spread_row(k, sp, S[:, v, :], l, v, 3 * which, rows_in)
        if moe:
            sp.dma_start(wr[:, :, 0:GROUPS],
                         dr["moe_w_group"][l].rearrange("(j p) n -> p j n", p=P)).then_inc(rows_in, 16)
            sp.dma_start(wr[:, :, GROUPS:],
                         dr["moe_w_expert"][l].rearrange("(j p) n -> p j n", p=P)).then_inc(rows_in, 16)

            def body(i, n, v):
                for u in range(2):
                    sp.wait_ge(a_ready, 2 * n + u + 1)
                    sp.dma_start(dr["moe_x"][ds(i * 2 * P + u * P, P), :], a[u][:]).then_inc(a_stored[u], 16)
            passes(sp, body)
            for u in range(2):
                sp.wait_ge(a_stored[u], 8 * (NT - first))

    @block.scalar
    def _(act):
        def body(i, n, v):
            act.wait_ge(a_ready, 2 * n)
            for u in range(2):
                nc.scalar.activation(sq[:, u, :], H[:, ds(i * 2 + u, 1), :].rearrange("p a d -> p (a d)"),
                                     ACT.Square, accum_out=ssq[:, u:u + 1]).then_inc(sumsq_ready, 1)
            for u in range(2):
                act.wait_ge(mean_ready, 2 * n + u + 1)
                nc.scalar.activation(rstd[:, u:u + 1], rstd[:, u:u + 1], ACT.Sqrt).then_inc(root_ready, 1)
            for u in range(2):
                act.wait_ge(a_turned, 2 + 2 * n + u + 1)
                if moe:
                    act.wait_ge(logits_ready, 2 + 2 * n + u - 1)
                for half in range(2):
                    src = k.bank[2 * u + half][:].rearrange("p (c q) -> p c q", c=4)
                    if moe:
                        dst = fT[:, u, 4 * half:4 * half + 4, :]
                    else:
                        dst = aT[:, 4 * half:4 * half + 4, ds(i * (2 * P) + u * P, P)]
                    nc.scalar.copy(dst, src).then_inc(aT_ready, 1)
        passes(act, body)

    @block.vector
    def _(dve):
        dve.wait_ge(rows_in, 16 * (2 * len(vs) + 2 * moe))
        st = Steps(dve, order, 4)

        def body(i, n, v):
            st.at(n)
            for u in range(2):
                r = rstd[:, u:u + 1]
                dve.wait_ge(sumsq_ready, 2 * n + u + 1)
                nc.vector.tensor_scalar(r, ssq[:, u:u + 1], 1.0 / D, EPS, ALU.mult, ALU.add).then_inc(mean_ready, 1)
                dve.wait_ge(root_ready, 2 * n + u + 1)
                st.link(nc.vector.reciprocal(r, r))
                dve.wait_ge(a_turned, 2 + 2 * n + u - 1)
                if moe:
                    dve.wait_ge(a_stored[u], n * 16)
                st.link(nc.vector.scalar_tensor_tensor(
                    out=a[u][:], in0=H[:, ds(i * 2 + u, 1), :].rearrange("p a d -> p (a d)"), scalar=r,
                    in1=A[:, v, :], op0=ALU.mult, op1=ALU.mult))
                nc.vector.tensor_tensor(a[u][:], a[u][:], S[:, v, :], ALU.add).then_inc(a_ready, 1)
            st.end()
            if moe:
                for u in range(2):
                    dve.wait_ge(logits_ready, 2 + 2 * n + u + 1)
                    nc.vector.tensor_copy(logits[:, ds(i * 2 + u - first, 1), :].rearrange("p a e -> p (a e)"),
                                          k.bank[4 + u][:, 0:NL]).then_inc(logits_taken, 1)
        passes(dve, body)

    @block.tensor
    def _(pe):
        pe.sem_inc(a_turned, 2)
        if moe:
            pe.sem_inc(logits_ready, 2)

        def body(i, n, v):
            pe.wait_ge(aT_ready, 4 * n)
            for u in range(2):
                pe.wait_ge(a_ready, 2 * n + u + 1)
                for c in range(KC):
                    t = pe.transpose(k.bank[2 * u + c // 4][:, (c % 4) * P:(c % 4 + 1) * P],
                                     a[u][:, c * P:(c + 1) * P], k.eye[:])
                t.then_inc(a_turned, 1)
            if moe:
                pe.wait_ge(logits_taken, 2 * n)
                for u in range(2):
                    pe.wait_ge(aT_ready, 4 * n + 2 * u + 2)
                    for c in range(KC):
                        mm = pe.matmul(k.bank[4 + u][:, 0:NL], fT[:, u, c, :], wr[:, c, :],
                                       start=(c == 0), stop=(c == KC - 1))
                    mm.then_inc(logits_ready, 1)
        passes(pe, body)


def project0(k, aT):
    nc, dr = k.nc, k.dram
    PARTS = 7
    QC, ALPHA = 3 * W0, 4 * W0
    SC = ALPHA + 4 * NH
    COLS = (0, W0, 2 * W0, QC, SC + W0, SC + 2 * W0, SC)
    w = [k.sb(f"w{j}", [P, KC, P]) for j in range(PARTS)]
    wab = k.sb("w_ab", [P, KC, 4 * NH])
    cq = k.sb("conv_qkv", [P, 3, 3 * NH])
    csc = k.sb("conv_sc", [P, 3, NH])
    x = k.sb("x_raw", [P, PADTOK])
    y = k.sb("y", [P, PADTOK])
    z = k.sb("z", [P, PADTOK])
    bt = k.sb("by_token", [P, NT, P])
    ones, zero = k.sb("ones", [P, P]), k.sb("zero", [P, D])
    zero_set, cleared = k.sem("zero_set"), k.sem("cleared")
    r = k.sb("inv_norm", [P, 2, 512])
    w_in = [k.sem(f"w_in{j}") for j in range(PARTS)]
    w_used = [k.sem(f"w_used{j}") for j in range(PARTS)]
    consts_in, ones_set, pads_set = k.sem("consts_in"), k.sem("ones_set"), k.sem("pads_set")
    z_ready = [k.sem(f"z_ready{s}") for s in range(2)]
    z_copied = [k.sem(f"z_copied{s}") for s in range(2)]
    z_gated = [k.sem(f"z_gated{s}") for s in range(2)]
    ab_ready, ab_taken = k.sem("ab_ready"), k.sem("ab_taken")
    conv_ready, silu_ready = k.sem("conv_ready"), k.sem("silu_ready")
    sq_ready, norm_ready, norm_taken = k.sem("sq_ready"), k.sem("norm_ready"), k.sem("norm_taken")
    y_ready, y_stored = k.sem("y_ready"), k.sem("y_stored")
    turn_taken, bt_stored = k.sem("turn_taken"), k.sem("bt_stored")
    order, root_ready = k.sem("dve_order"), k.sem("root_ready")
    block = k.block()

    def use(j):
        return j // 2

    CNT = (4, 3)
    COPIED = (3, 2)
    AUX = 12

    @block.sync
    def _(sp):
        sp.dma_start(wab[:], dr["ab_w_in"][0, :, ALPHA:SC].rearrange("(j p) n -> p j n", p=P)).then_inc(consts_in, 16)
        for t in range(3):
            sp.dma_start(cq[:, t, :], dr["ab_conv_qkv"][0, t].rearrange("(c p) -> p c", p=P),
                         allow_slow_non_contiguous=True).then_inc(consts_in, 16)
            sp.dma_start(csc[:, t, :], dr["ab_conv_sc"][0, t].rearrange("(c p) -> p c", p=P),
                         allow_slow_non_contiguous=True).then_inc(consts_in, 16)
        src = dr["ab_w_in"][0].rearrange("(j p) n -> p j n", p=P)
        for j in range(PARTS):
            sp.dma_start(w[j][:], src[:, :, COLS[j]:COLS[j] + P]).then_inc(w_in[j], 16)
        with sp.Fori(1, NH) as h:
            for j in range(PARTS):
                sp.wait_ge(z_ready[j % 2], (h - 1) * CNT[j % 2] + use(j) + 1)
                sp.dma_start(w[j][:], src[:, :, ds(h * P + COLS[j], P)]).then_inc(w_in[j], 16)

    def store_channels(eng, part, h):
        out = dr["heads"][part]
        eng.dma_start(out[0:CT, :, ds(h * P, P)].rearrange("t p n -> p t n"),
                      z[:, 0:CTX].rearrange("p (t n) -> p t n", n=P)).then_inc(y_stored, 16)
        eng.dma_start(out[CT:NT, :, ds(h * P, P)].rearrange("t p n -> p t n"),
                      z[:, LAT0:LAT0 + SEQ].rearrange("p (t n) -> p t n", n=P)).then_inc(y_stored, 16)

    @block.gpsimd
    def _(pool):
        nc.gpsimd.memset(ones[:], 1.0).then_inc(ones_set, 1)
        nc.gpsimd.memset(zero[:], 0.0).then_inc(zero_set, 1)
        pool.wait_ge(zero_set, 1)
        more = dr["moe_y"][NE * P:SLOTS, :].rearrange("(b p) d -> p b d", p=P)
        pool.dma_start(more, zero[:].unsqueeze(1).to_broadcast([P, SLOTS // P - NE, D])).then_inc(cleared, 16)
        with pool.Fori(0, NH) as h:
            for n, part in enumerate((0, 1)):
                pool.wait_ge(y_ready, h * 2 + n + 1)
                store_channels(pool, part, h)
            for n, part in enumerate((2, 3)):
                pool.wait_ge(turn_taken, h * 6 + 3 * n + 3)
                pool.dma_start(dr["heads"][part, :, :, ds(h * P, P)].rearrange("t p n -> p t n"),
                               bt[:]).then_inc(bt_stored, 16)
        pool.wait_ge(y_stored, NH * 64)
        pool.wait_ge(bt_stored, NH * 32)
        pool.wait_ge(cleared, 16)

    @block.tensor
    def _(pe):
        pe.wait_ge(consts_in, 16 * 7)
        pe.wait_ge(ones_set, 1)
        for t in range(NT):
            for j in range(KC):
                mm = pe.matmul(k.bank[7][:, t * 4 * NH:(t + 1) * 4 * NH], aT[:, j, t * P:(t + 1) * P], wab[:, j, :],
                               start=(j == 0), stop=(j == KC - 1))
        mm.then_inc(ab_ready, 1)
        pe.wait_ge(ab_taken, 1)

        def part(h, j):
            s = j % 2
            pe.wait_ge(w_in[j], (h + 1) * 16)
            pe.wait_ge(z_copied[s], h * COPIED[s] + use(j))
            pe.wait_ge(z_gated[s], h)
            for n, (at, width) in enumerate(SPANS):
                for c in range(KC):
                    mm = pe.matmul(k.bank[3 * s + n][:, 0:width], w[j][:, c, :], aT[:, c, at:at + width],
                                   start=(c == 0), stop=(c == KC - 1))
            mm.then_inc(z_ready[s], 1)

        def aux(h, m):
            pe.wait_ge(norm_taken, h * 6 + min(max(m - 1, 0), 6))
            pe.wait_ge(turn_taken, h * 6 + max(m - 7, 0))
            return k.bank[6 + m % 2]

        def norms(h, n):
            pe.wait_ge(sq_ready, h * 2 + n + 1)
            for s, (at, width) in enumerate(SPANS):
                at += 2 if s else 0
                pe.matmul(aux(h, 3 * n + s)[:, 0:width], ones[:], y[:, at:at + width],
                          start=True, stop=True).then_inc(norm_ready, 1)

        def turns(h, n):
            if n == 0:
                pe.wait_ge(y_ready, h * 2 + 2)
            else:
                pe.wait_ge(silu_ready, h * 3 + 3)
            for g in range(3):
                to = aux(h, 6 + 3 * n + g)
                for q in range(min(4, NT - 4 * g)):
                    t = 4 * g + q
                    at = t * P + (2 if t >= CT else 0)
                    mm = pe.transpose(to[:, q * P:(q + 1) * P], z[:, at:at + P], k.eye[:])
                mm.then_inc(norm_ready, 1)

        with pe.Fori(0, NH) as h:
            part(h, 0)
            part(h, 1)
            norms(h, 0)
            part(h, 2)
            norms(h, 1)
            part(h, 3)
            turns(h, 0)
            part(h, 4)
            turns(h, 1)
            part(h, 5)
            part(h, 6)

    @block.scalar
    def _(act):
        act.wait_ge(ab_ready, 1)
        nc.scalar.copy(k.ab[:].rearrange("p t n -> p (t n)"), k.bank[7][:, 0:NT * 4 * NH]).then_inc(ab_taken, 1)
        act.wait_ge(pads_set, 1)

        def raw(h, j, dst):
            s = j % 2
            act.wait_ge(z_ready[s], h * CNT[s] + use(j) + 1)
            for n, (at, width) in enumerate(SPANS):
                at += 3 if n else 1
                c = nc.scalar.copy(dst[:, at:at + width], k.bank[3 * s + n][:, 0:width])
            c.then_inc(z_copied[s], 1)

        def silu(h, n):
            act.wait_ge(conv_ready, h * 4 + n + 1)
            nc.scalar.activation(z[:, 0:PADTOK - 2], y[:, 0:PADTOK - 2], ACT.Silu).then_inc(silu_ready, 1)

        def square(h, n):
            act.wait_ge(silu_ready, h * 3 + n + 1)
            nc.scalar.activation(y[:, 0:PADTOK - 2], z[:, 0:PADTOK - 2], ACT.Square).then_inc(sq_ready, 1)
            for s, (_, width) in enumerate(SPANS):
                m = 3 * n + s
                act.wait_ge(norm_taken, h * 6 + m + 1)
                nc.scalar.activation(r[:, m % 2, 0:width], r[:, m % 2, 0:width], ACT.Sqrt).then_inc(root_ready, 1)

        def take_turns(h, n):
            act.wait_ge(bt_stored, h * 32 + 16 * n)
            for g in range(3):
                act.wait_ge(norm_ready, h * AUX + 6 + 3 * n + g + 1)
                tiles = min(4, NT - 4 * g)
                nc.scalar.copy(bt[:, 4 * g:4 * g + tiles, :].rearrange("p t n -> p (t n)"),
                               k.bank[6 + g % 2 if n == 0 else 7 - g % 2][:, 0:tiles * P]).then_inc(turn_taken, 1)

        with act.Fori(0, NH) as h:
            raw(h, 0, x)
            act.wait_ge(z_gated[1], h)
            silu(h, 0)
            square(h, 0)
            act.wait_ge(conv_ready, h * 4 + 1)
            raw(h, 1, x)
            act.wait_ge(y_stored, h * 64 + 32)
            silu(h, 1)
            square(h, 1)
            raw(h, 2, x)
            act.wait_ge(z_ready[1], h * CNT[1] + use(3) + 1)
            for m, (at, width) in enumerate(SPANS):
                c = nc.scalar.activation(k.gate[:, ds(h, 1), at:at + width].rearrange("p a n -> p (a n)"),
                                         k.bank[3 + m][:, 0:width], ACT.Silu)
            c.then_inc(z_copied[1], 1)
            take_turns(h, 0)
            act.wait_ge(y_stored, h * 64 + 64)
            silu(h, 2)
            take_turns(h, 1)
            raw(h, 4, z)

    @block.vector
    def _(dve):
        for at in (0, CTX + 1, PADTOK - 1):
            m = nc.vector.memset(x[:, at:at + (2 if at == CTX + 1 else 1)], 0.0)
        m.then_inc(pads_set, 1)
        dve.wait_ge(consts_in, 16 * 7)
        st = Steps(dve, order, 4 * 2 + 2 * 5)
        N = PADTOK - 2

        def conv(h, taps, col):
            c = taps[:, :, ds(h + col, 1)].rearrange("p t a -> p (t a)")
            st.link(nc.vector.tensor_scalar(y[:, 0:N], x[:, 0:N], c[:, 0:1], None, ALU.mult))
            st.link(nc.vector.scalar_tensor_tensor(out=y[:, 0:N], in0=x[:, 1:N + 1], scalar=c[:, 1:2],
                                                   in1=y[:, 0:N], op0=ALU.mult, op1=ALU.add))
            nc.vector.scalar_tensor_tensor(out=y[:, 0:N], in0=x[:, 2:N + 2], scalar=c[:, 2:3],
                                           in1=y[:, 0:N], op0=ALU.mult, op1=ALU.add).then_inc(conv_ready, 1)

        def normalise(h, n, scale):
            for s, (at, width) in enumerate(SPANS):
                at += 2 if s else 0
                m = 3 * n + s
                dve.wait_ge(norm_ready, h * AUX + m + 1)
                nc.vector.tensor_scalar(r[:, m % 2, 0:width], k.bank[6 + m % 2][:, 0:width], EPS, None,
                                        ALU.add).then_inc(norm_taken, 1)
                dve.wait_ge(root_ready, h * 6 + m + 1)
                st.link(nc.vector.reciprocal(r[:, m % 2, 0:width], r[:, m % 2, 0:width]))
                c = nc.vector.scalar_tensor_tensor(out=z[:, at:at + width], in0=z[:, at:at + width],
                                                   scalar=scale, in1=r[:, m % 2, 0:width], op0=ALU.mult, op1=ALU.mult)
                if s < 2:
                    st.link(c)
            c.then_inc(y_ready, 1)

        with dve.Fori(0, NH) as h:
            st.at(h)
            dve.wait_ge(z_copied[0], h * 3 + 1)
            conv(h, cq, 0)
            normalise(h, 0, P ** -0.5)
            dve.wait_ge(z_copied[1], h * 2 + 1)
            conv(h, cq, NH)
            normalise(h, 1, 1.0)
            dve.wait_ge(z_copied[0], h * 3 + 2)
            conv(h, cq, 2 * NH)
            dve.wait_ge(z_copied[0], h * 3 + 3)
            dve.wait_ge(z_ready[1], h * CNT[1] + 3)
            for n, (at, width) in enumerate(SPANS):
                at += 3 if n else 1
                c = nc.vector.tensor_tensor(x[:, at:at + width], z[:, at:at + width],
                                            k.bank[3 + n][:, 0:width], ALU.mult)
            c.then_inc(z_gated[1], 1)
            dve.wait_ge(z_gated[1], h + 1)
            dve.wait_ge(silu_ready, h * 3 + 3)
            conv(h, csc, 0)
            dve.wait_ge(conv_ready, h * 4 + 4)
            dve.wait_ge(z_ready[0], h * CNT[0] + 4)
            for n, (at, width) in enumerate(SPANS):
                c = nc.vector.tensor_tensor(k.short[:, ds(h, 1), at:at + width].rearrange("p a n -> p (a n)"),
                                            y[:, at + (2 if n else 0):at + (2 if n else 0) + width],
                                            k.bank[n][:, 0:width], ALU.mult)
            c.then_inc(z_gated[0], 1)
            st.end()


def delta_scan(k, oT):
    nc, dr = k.nc, k.dram
    R2 = range(2)
    merge = k.sb("merge", [P, 2, LEVELS, P])
    ones = k.sb("ones", [P, P])
    alog = k.sb("a_log", [P, 2 * NH])
    dtb = k.sb("dt_bias", [P, 2 * NH])
    ST = [P, NT, 2 * NH]
    la, beta, g, tot = k.sb("log_a", ST), k.sb("beta", ST), k.sb("g", ST), k.sb("g_total", ST)
    beg, kdec, egl, tmp = k.sb("beta_eg", ST), k.sb("k_decay", ST), k.sb("eg_total", ST), k.sb("tmp", ST)

    def per_dir(name):
        return [k.sb(f"{name}{d}", [P, NH, P]) for d in R2]

    KT, QT, K, V = per_dir("KT"), per_dir("QT"), per_dir("K"), per_dir("V")
    GU, BI, Dc, EG = per_dir("g_rows_in"), per_dir("b_rows_in"), per_dir("decay"), per_dir("eg_rows")
    Dm, DB, AT, KQ = per_dir("decay_masked"), per_dir("decay_beta"), per_dir("AT"), per_dir("KQ")
    T, TT, Pm, QTd = per_dir("T"), per_dir("TT"), per_dir("A_T_off"), per_dir("QT_decayed")
    VB, R, VN, VD, S = per_dir("V_beta"), per_dir("R"), per_dir("v_new"), per_dir("v_decayed"), per_dir("S")

    consts_in, ones_set, state_set, stats = k.sem("consts_in"), k.sem("ones_set"), k.sem("state_set"), k.sem("stats")
    prep_act, prep_pe, prep_order = k.sem("prep_act"), k.sem("prep_pe"), k.sem("prep_order")

    def sems(name):
        return [k.sem(f"{name}{d}") for d in R2]

    tile_in, rows_in = sems("tile_in"), sems("rows_in")
    g_rows, kk_ready, a_turned, p_ready, dt_ready = (sems(n) for n in ("g_rows", "kk_ready", "a_turned", "p_ready", "dt_ready"))
    ks_ready, vn_ready, o_ready, ds_ready = (sems(n) for n in ("ks_ready", "vn_ready", "o_ready", "ds_ready"))
    e_ready, at_ready, kq_ready, t_ready, pm_ready = (sems(n) for n in ("e_ready", "at_ready", "kq_ready", "t_ready", "pm_ready"))
    tt_ready, r_ready, vd_ready, o_added, s_ready = (sems(n) for n in ("tt_ready", "r_ready", "vd_ready", "o_added", "s_ready"))
    eg_ready, d_ready, vn_copied = (sems(n) for n in ("eg_ready", "d_ready", "vn_copied"))
    dm_ready, qtd_ready, vb_ready, tt0_ready, s_scaled = (sems(n) for n in ("dm_ready", "qtd_ready", "vb_ready", "tt0_ready", "s_scaled"))
    order, pool_order = k.sem("dve_order"), k.sem("pool_order")
    MERGES = LEVELS - 1
    bank = [[k.bank[4 * d + n][:].rearrange("p (h n) -> p h n", h=NH) for n in range(4)] for d in R2]
    flat = [[k.bank[4 * d + n] for n in range(4)] for d in R2]
    block = k.block()

    def passes(eng, body):
        with eng.Fori(0, CT) as s:
            body(s, (s, eng.snap(s * -1 + (CT - 1), min_val=0, max_val=CT - 1)))
        with eng.Fori(CT, NT) as s:
            body(s, (s, eng.snap(s * -1 + (NT + CT - 1), min_val=CT, max_val=NT - 1)))

    def stat(x, t, d):
        return (x[:, ds(t, 1), NH * d:NH * d + NH].rearrange("p a h -> p (a h)").unsqueeze(2)
                .to_broadcast([P, NH, P]))

    def all_heads(x):
        return x.unsqueeze(1).to_broadcast([P, NH, P])

    @block.sync
    def _(sp):
        sp.dma_start(merge[:], dr["const_merge"].rearrange("d l p n -> p d l n")).then_inc(consts_in, 16)
        sp.dma_start(alog[:], dr["ab_a_log"].rearrange("a d h -> a (d h)").to_broadcast([P, 2 * NH])).then_inc(consts_in, 16)
        sp.dma_start(dtb[:], dr["ab_dt_bias"].rearrange("a d h -> a (d h)").to_broadcast([P, 2 * NH])).then_inc(consts_in, 16)

        def body(s, tiles):
            for d in R2:
                sp.wait_ge(ds_ready[d], s)
                sp.wait_ge(qtd_ready[d], s)
                sp.wait_ge(vb_ready[d], s)
                for part, dst in enumerate((QT, KT, K, V)):
                    sp.dma_start(dst[d][:].rearrange("p h n -> p (h n)"),
                                 dr["heads"][part, ds(tiles[d], 1)].rearrange("a p n -> p (a n)")).then_inc(tile_in[d], 16)
        passes(sp, body)

    @block.gpsimd
    def _(pool):
        nc.gpsimd.memset(ones[:], 1.0).then_inc(ones_set, 1)
        nc.gpsimd.memset(oT[:], 0.0).then_inc(state_set, 1)
        for d in R2:
            nc.gpsimd.memset(S[d][:], 0.0).then_inc(state_set, 1)
        pool.wait_ge(stats, 1)

        def body(s, tiles):
            for d in R2:
                pool.wait_ge(g_rows[d], s)
                nc.gpsimd.tensor_tensor(GU[d][:], all_heads(k.tri[:, d, :]), stat(la, tiles[d], d), ALU.mult).then_inc(rows_in[d], 1)
                nc.gpsimd.tensor_tensor(BI[d][:], all_heads(k.eye[:]), stat(beta, tiles[d], d), ALU.mult).then_inc(rows_in[d], 1)
            for d in R2:
                pool.wait_ge(d_ready[d], s + 1)
                pool.wait_ge(kq_ready[d], s)
                nc.gpsimd.tensor_tensor(Dm[d][:], Dc[d][:], all_heads(k.tri[:, d, :]), ALU.mult).then_inc(dm_ready[d], 1)
            for d in R2:
                pool.wait_ge(at_ready[d], s + 1)
                pool.wait_ge(vn_ready[d], s)
                nc.gpsimd.tensor_tensor(TT[d][:], AT[d][:], all_heads(merge[:, 1 - d, 0, :]), ALU.mult).then_inc(pool_order, 1)
                pool.wait_ge(pool_order, s * 2 + d + 1)
                nc.gpsimd.tensor_tensor(TT[d][:], all_heads(k.eye[:]), TT[d][:], ALU.subtract).then_inc(tt0_ready[d], 1)
            for d in R2:
                pool.wait_ge(tile_in[d], (s + 1) * 64)
                pool.wait_ge(eg_ready[d], s + 1)
                pool.wait_ge(r_ready[d], s)
                pool.wait_ge(o_ready[d], s)
                nc.gpsimd.tensor_tensor(QTd[d][:], QT[d][:], EG[d][:], ALU.mult).then_inc(qtd_ready[d], 1)
                nc.gpsimd.tensor_tensor(VB[d][:], V[d][:], stat(beta, tiles[d], d), ALU.mult).then_inc(vb_ready[d], 1)
            for d in R2:
                pool.wait_ge(o_ready[d], s + 1)
                nc.gpsimd.tensor_tensor(S[d][:], S[d][:], stat(egl, tiles[d], d), ALU.mult).then_inc(s_scaled[d], 1)
        passes(pool, body)

    @block.scalar
    def _(act):
        act.wait_ge(prep_order, 1)
        nc.scalar.activation(tmp[:], la[:], ACT.Abs).then_inc(prep_act, 1)
        act.wait_ge(prep_act, 1)
        nc.scalar.activation(tmp[:], tmp[:], ACT.Exp, scale=-1.0).then_inc(prep_act, 1)
        act.wait_ge(prep_act, 2)
        nc.scalar.activation(tmp[:], tmp[:], ACT.Ln, bias=1.0).then_inc(prep_act, 1)
        nc.scalar.activation(beta[:], k.ab[:, :, 2 * NH:], ACT.Sigmoid).then_inc(prep_act, 1)
        act.wait_ge(consts_in, 48)
        nc.scalar.activation(alog[:], alog[:], ACT.Exp).then_inc(prep_act, 1)
        act.wait_ge(prep_order, 6)
        nc.scalar.activation(kdec[:], kdec[:], ACT.Exp).then_inc(prep_act, 1)
        nc.scalar.activation(egl[:], tot[:], ACT.Exp).then_inc(prep_act, 1)
        nc.scalar.activation(tmp[:], g[:], ACT.Exp).then_inc(prep_act, 1)

        def body(s, tiles):
            for d in R2:
                act.wait_ge(g_rows[d], s + 1)
                act.wait_ge(qtd_ready[d], s)
                nc.scalar.activation(EG[d][:], bank[d][0], ACT.Exp).then_inc(eg_ready[d], 1)
            for d in R2:
                act.wait_ge(e_ready[d], s + 1)
                nc.scalar.activation(Dc[d][:], Dc[d][:], ACT.Exp).then_inc(d_ready[d], 1)
            for d in R2:
                act.wait_ge(vn_ready[d], s + 1)
                act.wait_ge(o_ready[d], s)
                nc.scalar.copy(VN[d][:], bank[d][1]).then_inc(vn_copied[d], 1)
        passes(act, body)

    @block.vector
    def _(dve):
        dve.wait_ge(consts_in, 48)
        prep = Steps(dve, prep_order)
        bias = dtb[:].unsqueeze(1).to_broadcast(ST)
        prep.link(nc.vector.tensor_tensor(la[:], k.ab[:, :, 0:2 * NH], bias, ALU.add))
        dve.wait_ge(prep_act, 3)
        prep.link(nc.vector.scalar_tensor_tensor(out=la[:], in0=la[:], scalar=0.0, in1=tmp[:], op0=ALU.max, op1=ALU.add))
        dve.wait_ge(prep_act, 5)
        prep.link(nc.vector.scalar_tensor_tensor(out=la[:], in0=la[:], scalar=-1.0,
                                                 in1=alog[:].unsqueeze(1).to_broadcast(ST), op0=ALU.mult, op1=ALU.mult))
        dve.wait_ge(prep_pe, 1)
        for d in R2:
            prep_copy = nc.vector.tensor_copy(g[:, :, NH * d:NH * d + NH],
                                              flat[0][d][:, 0:NT * NH].rearrange("p (t h) -> p t h", t=NT))
            if d == 1:
                prep.link(prep_copy)
        prep.link(nc.vector.tensor_copy(tot[:], flat[0][2][:, 0:2 * NT * NH].rearrange("p (t h) -> p t h", t=NT)))
        prep.link(nc.vector.tensor_tensor(kdec[:], tot[:], g[:], ALU.subtract))
        dve.wait_ge(prep_act, 8)
        prep.link(nc.vector.tensor_tensor(beg[:], tmp[:], beta[:], ALU.mult))
        dve.sem_inc(stats, 1)
        dve.wait_ge(state_set, 3)
        st = Steps(dve, order, 2 * (1 + 1 + 1 + 1))

        def body(s, tiles):
            st.at(s)
            for d in R2:
                dve.wait_ge(eg_ready[d], s + 1)
                dve.wait_ge(dm_ready[d], s)
                st.link(nc.vector.tensor_tensor(Dc[d][:], bank[d][0], stat(g, tiles[d], d), ALU.subtract))
                nc.vector.tensor_scalar(Dc[d][:], Dc[d][:], 0.0, None, ALU.min).then_inc(e_ready[d], 1)
            for d in R2:
                dve.wait_ge(d_ready[d], s + 1)
                st.link(nc.vector.tensor_tensor(DB[d][:], Dc[d][:], bank[d][1], ALU.mult))
                dve.wait_ge(kk_ready[d], s + 1)
                nc.vector.tensor_tensor(AT[d][:], DB[d][:], bank[d][2], ALU.mult).then_inc(at_ready[d], 1)
                dve.wait_ge(dm_ready[d], s + 1)
                nc.vector.tensor_tensor(KQ[d][:], Dm[d][:], bank[d][3], ALU.mult).then_inc(kq_ready[d], 1)
            for d in R2:
                dve.wait_ge(a_turned[d], s + 1)
                st.link(nc.vector.tensor_tensor(T[d][:], bank[d][0], all_heads(merge[:, d, 0, :]), ALU.mult))
                nc.vector.tensor_tensor(T[d][:], all_heads(k.eye[:]), T[d][:], ALU.subtract).then_inc(t_ready[d], 1)
            for n in range(MERGES):
                for d in R2:
                    dve.wait_ge(p_ready[d], s * MERGES + n + 1)
                    nc.vector.tensor_tensor(Pm[d][:], bank[d][1], all_heads(merge[:, d, n + 1, :]),
                                            ALU.mult).then_inc(pm_ready[d], 1)
                for d in R2:
                    dve.wait_ge(dt_ready[d], s * MERGES + n + 1)
                    if n == 0:
                        dve.wait_ge(tt0_ready[d], s + 1)
                        dve.wait_ge(t_ready[d], s + 1)
                    else:
                        dve.wait_ge(tt_ready[d], s * MERGES + n)
                    if n < MERGES - 1:
                        nc.vector.tensor_tensor(T[d][:], T[d][:], bank[d][2], ALU.subtract)
                    nc.vector.tensor_tensor(TT[d][:], TT[d][:], bank[d][3], ALU.subtract).then_inc(tt_ready[d], 1)
            for d in R2:
                dve.wait_ge(ks_ready[d], s + 1)
                st.link(nc.vector.tensor_tensor(R[d][:], bank[d][0], stat(beg, tiles[d], d), ALU.mult))
                dve.wait_ge(vb_ready[d], s + 1)
                nc.vector.tensor_tensor(R[d][:], VB[d][:], R[d][:], ALU.subtract).then_inc(r_ready[d], 1)
            for d in R2:
                dve.wait_ge(vn_copied[d], s + 1)
                nc.vector.tensor_tensor(VD[d][:], bank[d][1], stat(kdec, tiles[d], d), ALU.mult).then_inc(vd_ready[d], 1)
            for d in R2:
                o = oT[:, :, ds(tiles[d] * P, P)]
                dve.wait_ge(o_ready[d], s + 1)
                dve.wait_ge(o_added[1 - d], s + d)
                nc.vector.tensor_tensor(o, o, bank[d][2], ALU.add).then_inc(o_added[d], 1)
                dve.wait_ge(ds_ready[d], s + 1)
                dve.wait_ge(s_scaled[d], s + 1)
                nc.vector.tensor_tensor(S[d][:], S[d][:], bank[d][3], ALU.add).then_inc(s_ready[d], 1)
            st.end()
        passes(dve, body)

    @block.tensor
    def _(pe):
        pe.wait_ge(ones_set, 1)
        pe.wait_ge(prep_order, 3)
        for d in R2:
            pe.matmul(flat[0][d][:, 0:NT * NH], k.tri[:, d, :], la[:, :, NH * d:NH * d + NH], start=True, stop=True)
        pe.matmul(flat[0][2][:, 0:2 * NT * NH], ones[:], la[:].rearrange("p t h -> p (t h)"),
                  start=True, stop=True).then_inc(prep_pe, 1)
        pe.wait_ge(stats, 1)
        pe.wait_ge(state_set, 3)

        def heads(to, lhs, rhs, start=True, stop=True):
            for h in range(NH):
                mm = pe.matmul(to[:, h, :], lhs[:, h, :], rhs[:, h, :], start=start, stop=stop)
            return mm

        def body(s, tiles):
            for d in R2:
                pe.wait_ge(rows_in[d], 2 * s + 2)
                pe.wait_ge(r_ready[d], s)
                pe.wait_ge(vd_ready[d], s)
                pe.wait_ge(vn_copied[d], s)
                pe.matmul(flat[d][0][:], ones[:], GU[d][:].rearrange("p h n -> p (h n)"), start=True, stop=True)
                pe.matmul(flat[d][1][:], ones[:], BI[d][:].rearrange("p h n -> p (h n)"), start=True,
                          stop=True).then_inc(g_rows[d], 1)
            for d in R2:
                pe.wait_ge(tile_in[d], (s + 1) * 64)
                pe.wait_ge(o_added[d], s)
                pe.wait_ge(s_ready[d], s)
                heads(bank[d][2], KT[d], KT[d])
                heads(bank[d][3], KT[d], QT[d]).then_inc(kk_ready[d], 1)
            for d in R2:
                pe.wait_ge(at_ready[d], s + 1)
                pe.wait_ge(eg_ready[d], s + 1)
                for h in range(NH):
                    mm = pe.transpose(bank[d][0][:, h, :], AT[d][:, h, :], k.eye[:])
                mm.then_inc(a_turned[d], 1)
            for n in range(MERGES):
                for d in R2:
                    if n == 0:
                        pe.wait_ge(t_ready[d], s + 1)
                    else:
                        pe.wait_ge(tt_ready[d], s * MERGES + n)
                    heads(bank[d][1], AT[d], T[d]).then_inc(p_ready[d], 1)
                for d in R2:
                    pe.wait_ge(pm_ready[d], s * MERGES + n + 1)
                    if n == 0:
                        pe.wait_ge(tt0_ready[d], s + 1)
                        pe.wait_ge(kq_ready[d], s + 1)
                    if n < MERGES - 1:
                        heads(bank[d][2], TT[d], Pm[d])
                    heads(bank[d][3], Pm[d], TT[d]).then_inc(dt_ready[d], 1)
            for d in R2:
                pe.wait_ge(s_ready[d], s)
                heads(bank[d][0], KT[d], S[d]).then_inc(ks_ready[d], 1)
            for d in R2:
                pe.wait_ge(r_ready[d], s + 1)
                pe.wait_ge(tt_ready[d], (s + 1) * MERGES)
                heads(bank[d][1], TT[d], R[d]).then_inc(vn_ready[d], 1)
            for d in R2:
                pe.wait_ge(vn_copied[d], s + 1)
                pe.wait_ge(qtd_ready[d], s + 1)
                for h in range(NH):
                    pe.matmul(bank[d][2][:, h, :], S[d][:, h, :], QTd[d][:, h, :], start=True, stop=False)
                    mm = pe.matmul(bank[d][2][:, h, :], VN[d][:, h, :], KQ[d][:, h, :], start=False, stop=True)
                mm.then_inc(o_ready[d], 1)
            for d in R2:
                pe.wait_ge(vd_ready[d], s + 1)
                heads(bank[d][3], K[d], VD[d]).then_inc(ds_ready[d], 1)
        passes(pe, body)


def gate_heads(k, oT):
    nc, dr = k.nc, k.dram
    ones, wn = k.sb("ones", [P, P]), k.sb("out_norm", [P, 1])
    sq, r = k.sb("squares", [P, 3, 512]), k.sb("rstd", [P, 3, 512])
    w_in, ones_set, sq_ready, sum_ready = k.sem("w_in"), k.sem("ones_set"), k.sem("sq_ready"), k.sem("sum_ready")
    mean_ready, root_ready, gated, order = k.sem("mean_ready"), k.sem("root_ready"), k.sem("gated"), k.sem("dve_order")
    block = k.block()

    def span(x, h, at, width):
        return x[:, ds(h, 1), at:at + width].rearrange("p a n -> p (a n)")

    @block.sync
    def _(sp):
        sp.dma_start(wn[:], dr["ab_out_norm"].rearrange("a p -> p a")).then_inc(w_in, 16)

    @block.gpsimd
    def _(pool):
        nc.gpsimd.memset(ones[:], 1.0).then_inc(ones_set, 1)

    @block.scalar
    def _(act):
        with act.Fori(0, NH) as h:
            for n, (at, width) in enumerate(SPANS):
                act.wait_ge(sum_ready, h * 3)
                nc.scalar.activation(sq[:, n, 0:width], span(oT, h, at, width), ACT.Square).then_inc(sq_ready, 1)
            for n, (at, width) in enumerate(SPANS):
                act.wait_ge(mean_ready, h * 3 + n + 1)
                nc.scalar.activation(r[:, n, 0:width], r[:, n, 0:width], ACT.Sqrt).then_inc(root_ready, 1)

    @block.tensor
    def _(pe):
        pe.wait_ge(ones_set, 1)
        with pe.Fori(0, NH) as h:
            for n, (at, width) in enumerate(SPANS):
                pe.wait_ge(sq_ready, h * 3 + n + 1)
                pe.wait_ge(mean_ready, h * 3)
                pe.matmul(k.bank[n][:, 0:width], ones[:], sq[:, n, 0:width], start=True, stop=True).then_inc(sum_ready, 1)

    @block.vector
    def _(dve):
        dve.wait_ge(w_in, 16)
        st = Steps(dve, order, 6)
        with dve.Fori(0, NH) as h:
            st.at(h)
            for n, (at, width) in enumerate(SPANS):
                dve.wait_ge(sum_ready, h * 3 + n + 1)
                dve.wait_ge(gated, h * 3)
                nc.vector.tensor_scalar(r[:, n, 0:width], k.bank[n][:, 0:width], 1.0 / P, EPS, ALU.mult,
                                        ALU.add).then_inc(mean_ready, 1)
            for n, (at, width) in enumerate(SPANS):
                dve.wait_ge(root_ready, h * 3 + n + 1)
                st.link(nc.vector.reciprocal(r[:, n, 0:width], r[:, n, 0:width]))
                o = span(oT, h, at, width)
                st.link(nc.vector.scalar_tensor_tensor(out=o, in0=o, scalar=wn[:], in1=r[:, n, 0:width],
                                                       op0=ALU.mult, op1=ALU.mult))
                nc.vector.tensor_tensor(o, o, span(k.gate, h, at, width), ALU.mult).then_inc(gated, 1)
            st.end()


def project_out(k, l, first, lhs, w_name):
    nc, dr = k.nc, k.dram
    w, g = k.sb("w_out", [P, KC, D]), k.sb("gate_rows", [P, 2, D])
    y = k.sb("y", [P, 2, D])
    w_in, g_in, y_ready, y_scaled, h_added = k.sem("w_in"), k.sem("g_in"), k.sem("y_ready"), k.sem("y_scaled"), k.sem("h_added")
    block = k.block()
    tiles = range(first, NT)

    @block.sync
    def _(sp):
        for half in range(2):
            sp.dma_start(w[:, :, half * 512:(half + 1) * 512],
                         dr[w_name][0, :, half * 512:(half + 1) * 512].rearrange("(j p) n -> p j n", p=P)).then_inc(w_in, 16)
        for v in range(2):
            spread_row(k, sp, g[:, v, :], l, v, 2, g_in)

    @block.tensor
    def _(pe):
        pe.wait_ge(w_in, 32)
        for n, t in enumerate(tiles):
            if n >= 2:
                pe.wait_ge(y_scaled, 2 * n - 2)
            for half in range(2):
                for c in range(KC):
                    mm = pe.matmul(k.bank[2 * (n % 2) + half][:], lhs(c, t), w[:, c, half * 512:(half + 1) * 512],
                                   start=(c == 0), stop=(c == KC - 1))
                mm.then_inc(y_ready, 1)

    @block.vector
    def _(dve):
        dve.wait_ge(g_in, 32)
        for n, t in enumerate(tiles):
            if n >= 2:
                dve.wait_ge(h_added, n - 1)
            for half in range(2):
                dve.wait_ge(y_ready, 2 * n + half + 1)
                nc.vector.tensor_tensor(y[:, n % 2, half * 512:(half + 1) * 512], k.bank[2 * (n % 2) + half][:],
                                        g[:, 0 if t < CT else 1, half * 512:(half + 1) * 512],
                                        ALU.mult).then_inc(y_scaled, 1)

    @block.gpsimd
    def _(pool):
        for n, t in enumerate(tiles):
            pool.wait_ge(y_scaled, 2 * n + 2)
            nc.gpsimd.tensor_tensor(k.H[:, t, :], k.H[:, t, :], y[:, n % 2, :], ALU.add).then_inc(h_added, 1)


def route(k, first, logits, slots, wts, table):
    nc, dr = k.nc, k.dram
    T = NT - first
    ramp = k.sb("ramp", [P, P])
    late = k.sb("ramp_plus_128", [P, P])
    ones, strict = k.sb("ones", [P, P]), k.sb("strict", [P, P])
    gmax, gi, gsum = k.sb("gmax", [P, T]), k.sb("gi", [P, T]), k.sb("gsum", [P, T])
    gx, gc, gh = k.sb("g_shifted", [P, T, GROUPS]), k.sb("g_cand", [P, T, GROUPS]), k.sb("g_hot", [P, T, GROUPS])
    ex = k.sb("in_group", [P, T, PER])
    big = k.sb("big", [P, T, GROUPS, PER])
    em, ei, ec = k.sb("e_max", [P, 2, T]), k.sb("e_index", [P, T]), k.sb("e_cand", [P, T, PER])
    eh = k.sb("e_hot", [P, 2, T, PER])
    hot = k.sb("hot", [P, 2, T, NE])
    cnt, pos, run = k.sb("chosen", [P, T, NE]), k.sb("position", [P, T, NE]), k.sb("running", [P, NE])
    more, incl, excl = k.sb("more_blocks", [P, NE]), k.sb("more_upto", [P, NE]), k.sb("more_before", [P, NE])
    over, home, thresholds = k.sb("over", [P, NE, 9]), k.sb("home", [P, NE]), k.sb("thresholds", [P, 9])
    whose, ratio, inv = k.sb("whose", [P, OVER + 1, NE]), k.sb("ratio", [P, T]), k.sb("inv", [P, T])
    sf, tf = k.sb("slots_f32", [P, 2, T]), k.sb("table_f32", [P, OVER + 2])
    tok, zero = k.sb("token", [P, T], I32), k.sb("no_token", [P, SLOTS // P], I32)
    c_in, order, exps, counted, tokens = k.sem("c_in"), k.sem("order"), k.sem("exps"), k.sem("counted"), k.sem("tokens")
    shifted, ratio_set, hot_ready = k.sem("shifted"), k.sem("ratio_set"), k.sem("hot_ready")
    cleared, slots_ready, scattered, consts = k.sem("cleared"), k.sem("slots_ready"), k.sem("scattered"), k.sem("consts")
    block = k.block()

    @block.sync
    def _(sp):
        sp.dma_start(ramp[:], dr["const_ramp"].to_broadcast([P, P])).then_inc(c_in, 16)

    @block.gpsimd
    def _(pool):
        nc.gpsimd.memset(ones[:], 1.0).then_inc(consts, 1)
        nc.gpsimd.tensor_tensor(strict[:], k.tri[:, 0, :], k.eye[:], ALU.subtract).then_inc(consts, 1)
        nc.gpsimd.iota(tok[:], [[P, T]], base=first * P, channel_multiplier=1).then_inc(tokens, 1)
        nc.gpsimd.memset(zero[:], first * P).then_inc(tokens, 1)
        pool.wait_ge(tokens, 2)
        pool.dma_start(dr["slot_token"].rearrange("(p b) a -> p (b a)", p=P), zero[:]).then_inc(cleared, 16)
        pool.wait_ge(cleared, 16)
        pool.wait_ge(slots_ready, 1)
        for t in range(T):
            for c in range(2):
                pool.indirect_dma_start(dr["slot_token"], bass.IndirectOffsetOnAxis(ap=slots[:, c, t:t + 1], axis=0),
                                        tok[:, t:t + 1], None).then_inc(scattered, 16)
        pool.wait_ge(scattered, 32 * T)

    @block.scalar
    def _(act):
        act.wait_ge(shifted, 1)
        nc.scalar.activation(gx[:], gx[:], ACT.Exp).then_inc(exps, 1)
        act.wait_ge(ratio_set, 1)
        nc.scalar.activation(ratio[:], ratio[:], ACT.Exp).then_inc(exps, 1)

    @block.tensor
    def _(pe):
        pe.wait_ge(consts, 2)
        pe.wait_ge(hot_ready, 1)
        flat = cnt[:].rearrange("p t e -> p (t e)")
        pe.matmul(k.bank[0][:, 0:T * NE], strict[:], flat, start=True, stop=True)
        pe.matmul(k.bank[1][:, 0:T * NE], ones[:], flat, start=True, stop=True).then_inc(counted, 1)

    @block.vector
    def _(dve):
        V = nc.vector
        st = Steps(dve, order)
        G, E = logits[:, :, 0:GROUPS], logits[:, :, GROUPS:].rearrange("p t (g e) -> p t g e", g=GROUPS)

        def cols(x, n):
            return x.unsqueeze(2).to_broadcast([P, T, n])

        def rows(x, n):
            return x[:, 0:n].unsqueeze(1).to_broadcast([P, T, n])

        def first_of(values, best, cand, index, is_it, n):
            st.link(V.tensor_tensor(cand, values, cols(best, n), ALU.is_equal))
            st.link(V.scalar_tensor_tensor(out=cand, in0=cand, scalar=-float(P), in1=rows(late, n), op0=ALU.mult, op1=ALU.add))
            st.link(V.tensor_reduce(index, cand, AX.X, ALU.min))
            st.link(V.tensor_tensor(is_it, rows(ramp, n), cols(index, n), ALU.is_equal))

        dve.wait_ge(c_in, 16)
        st.link(V.tensor_scalar(late[:], ramp[:], float(P), None, ALU.add))
        st.link(V.tensor_reduce(gmax[:], G, AX.X, ALU.max))
        st.link(V.tensor_tensor(gx[:], G, cols(gmax[:], GROUPS), ALU.subtract))
        dve.sem_inc(shifted, 1)
        first_of(G, gmax[:], gc[:], gi[:], gh[:], GROUPS)
        st.link(V.tensor_tensor(big[:], E, gh[:].unsqueeze(3).to_broadcast([P, T, GROUPS, PER]), ALU.mult))
        st.link(V.tensor_reduce(ex[:], big[:].rearrange("p t g e -> p t e g"), AX.X, ALU.add))
        for c in range(2):
            if c:
                st.link(V.scalar_tensor_tensor(out=ex[:], in0=eh[:, 0], scalar=-1e30, in1=ex[:], op0=ALU.mult, op1=ALU.add))
            st.link(V.tensor_reduce(em[:, c], ex[:], AX.X, ALU.max))
            if c:
                st.link(V.tensor_tensor(ratio[:], em[:, 1], em[:, 0], ALU.subtract))
                dve.sem_inc(ratio_set, 1)
            first_of(ex[:], em[:, c], ec[:], ei[:], eh[:, c], PER)
        for c in range(2):
            st.link(V.tensor_tensor(hot[:, c].rearrange("p t (g e) -> p t g e", g=GROUPS),
                                    gh[:].unsqueeze(3).to_broadcast([P, T, GROUPS, PER]),
                                    eh[:, c].unsqueeze(2).to_broadcast([P, T, GROUPS, PER]), ALU.mult))
        st.link(V.tensor_tensor(cnt[:], hot[:, 0], hot[:, 1], ALU.add))
        dve.sem_inc(hot_ready, 1)

        dve.wait_ge(exps, 2)
        st.link(V.tensor_reduce(gsum[:], gx[:], AX.X, ALU.add))
        st.link(V.reciprocal(gsum[:], gsum[:]))
        st.link(V.tensor_scalar(inv[:], ratio[:], 1.0, None, ALU.add))
        st.link(V.reciprocal(inv[:], inv[:]))
        st.link(V.tensor_tensor(wts[:, 0], gsum[:], inv[:], ALU.mult))
        st.link(V.tensor_tensor(wts[:, 1], wts[:, 0], ratio[:], ALU.mult))

        dve.wait_ge(counted, 1)
        st.link(V.memset(run[:], 0.0))
        for t in range(T):
            st.link(V.tensor_tensor(pos[:, t], k.bank[0][:, t * NE:(t + 1) * NE], run[:], ALU.add))
            st.link(V.tensor_tensor(run[:], run[:], k.bank[1][:, t * NE:(t + 1) * NE], ALU.add))
        st.link(V.tensor_scalar(thresholds[:], ramp[:, 1:10], float(P), None, ALU.mult))
        st.link(V.tensor_tensor(over[:], run[:].unsqueeze(2).to_broadcast([P, NE, 9]),
                                thresholds[:].unsqueeze(1).to_broadcast([P, NE, 9]), ALU.is_gt))
        st.link(V.tensor_reduce(more[:], over[:], AX.X, ALU.add))
        st.link(V.tensor_tensor_scan(incl[:], ones[:, 0:NE], more[:], 0.0, ALU.mult, ALU.add))
        st.link(V.tensor_tensor(excl[:], incl[:], more[:], ALU.subtract))
        st.link(V.tensor_scalar(home[:], ramp[:, 0:NE], float(P), None, ALU.mult))
        st.link(V.tensor_scalar(excl[:], excl[:], float(P), float(NE * P - P), ALU.mult, ALU.add))
        st.link(V.tensor_tensor(excl[:], excl[:], home[:], ALU.subtract))
        b = big[:].rearrange("p t g e -> p t (g e)")
        st.link(V.tensor_scalar(b, pos[:], float(P), None, ALU.is_ge))
        st.link(V.tensor_tensor(b, b, excl[:].unsqueeze(1).to_broadcast([P, T, NE]), ALU.mult))
        st.link(V.tensor_tensor(pos[:], pos[:], home[:].unsqueeze(1).to_broadcast([P, T, NE]), ALU.add))
        st.link(V.tensor_tensor(pos[:], pos[:], b, ALU.add))
        for c in range(2):
            st.link(V.tensor_tensor(b, hot[:, c], pos[:], ALU.mult))
            st.link(V.tensor_reduce(sf[:, c], b, AX.X, ALU.add))
        V.tensor_copy(slots[:].rearrange("p c t -> p (c t)"), sf[:].rearrange("p c t -> p (c t)")).then_inc(slots_ready, 1)
        st.link(V.tensor_tensor(whose[:], incl[:].unsqueeze(1).to_broadcast([P, OVER + 1, NE]),
                                ramp[:, 0:OVER + 1].unsqueeze(2).to_broadcast([P, OVER + 1, NE]), ALU.is_le))
        st.link(V.tensor_copy(tf[:, 0:1], incl[:, NE - 1:NE]))
        st.link(V.tensor_reduce(tf[:, 1:], whose[:], AX.X, ALU.add))
        st.link(V.tensor_scalar(tf[:, 1:], tf[:, 1:], float(NE - 1), None, ALU.min))
        st.link(V.tensor_copy(table[:], tf[:]))


def experts(k, l, table):
    nc, dr = k.nc, k.dram
    R2 = range(2)
    w1 = [k.sb(f"w1_{u}", [P, KC, FF]) for u in R2]
    w3 = [k.sb(f"w3_{u}", [P, KC, FF]) for u in R2]
    w2 = [k.sb(f"w2_{u}", [P, FC, D]) for u in R2]
    idx = k.sb("idx", [P, SLOTS // P], I32)
    one = [k.sb(f"idx_block{u}", [P, 1], I32) for u in R2]
    x, xT = [k.sb(f"x{u}", [P, D]) for u in R2], [k.sb(f"xT{u}", [P, KC, P]) for u in R2]
    hs, hh = [k.sb(f"silu{u}", [P, FF]) for u in R2], [k.sb(f"h{u}", [P, FF]) for u in R2]
    hT, y = [k.sb(f"hT{u}", [P, FC, P]) for u in R2], [k.sb(f"y{u}", [P, D]) for u in R2]
    idx_in, gather_due, all_stored = k.sem("idx_in"), k.sem("gather_due"), k.sem("all_stored")

    def sems(name):
        return [k.sem(f"{name}{u}") for u in R2]

    w13_in, w2_in, idx_ready, x_in = sems("w13_in"), sems("w2_in"), sems("idx_ready"), sems("x_in")
    x_turned, xT_ready, up_ready, silu_ready = sems("x_turned"), sems("xT_ready"), sems("up_ready"), sems("silu_ready")
    h_ready, h_turned, hT_ready, y_mm, y_ready, y_stored = (sems(n) for n in ("h_ready", "h_turned", "hT_ready", "y_mm", "y_ready", "y_stored"))
    MAIN = NE // 2
    block = k.block()

    def passes(eng, body):
        with eng.Fori(0, MAIN) as i:
            body(i, i * 2, lambda u: i * 2 + u)
        count = eng.value_load(table[0:1, 0:1], min_val=0, max_val=OVER)
        with eng.Fori(0, (OVER + 1) // 2) as j:
            with eng.If(j * 2 < count):
                body(j + MAIN, j * 2 + NE,
                     lambda u: eng.value_load(table[0:1, ds(j * 2 + (1 + u), 1)], min_val=0, max_val=NE - 1))
        return count

    @block.sync
    def _(sp):
        def body(n, b, owner):
            for u in R2:
                e = owner(u)
                sp.wait_ge(up_ready[u], n)
                sp.dma_start(w1[u][:], dr["moe_w1"][l, ds(e, 1)].rearrange("a (p j) n -> p (a j) n", p=P)).then_inc(w13_in[u], 16)
                sp.dma_start(w3[u][:], dr["moe_w3"][l, ds(e, 1)].rearrange("a (p j) n -> p (a j) n", p=P)).then_inc(w13_in[u], 16)
                sp.wait_ge(y_mm[u], n)
                sp.dma_start(w2[u][:], dr["moe_w2"][l, ds(e, 1)].rearrange("a (p j) n -> p (a j) n", p=P)).then_inc(w2_in[u], 16)
        passes(sp, body)

    @block.gpsimd
    def _(pool):
        with nc.allow_non_contiguous_dma(reason="slots of a block over partitions"):
            pool.dma_start(idx[:], dr["slot_token"].rearrange("(b p) a -> p (b a)", p=P)).then_inc(idx_in, 16)
        pool.wait_ge(idx_in, 16)

        def body(n, b, owner):
            for u in R2:
                pool.wait_ge(x_in[u], n * 16)
                nc.gpsimd.tensor_copy(one[u][:], idx[:, ds(b + u, 1)]).then_inc(idx_ready[u], 1)
                pool.wait_ge(x_turned[u], n)
                pool.wait_ge(idx_ready[u], n + 1)
                pool.sem_inc(gather_due, 1)
                pool.indirect_dma_start(x[u][:], None, dr["moe_x"],
                                        bass.IndirectOffsetOnAxis(ap=one[u][:, 0:1], axis=0)).then_inc(x_in[u], 16)
        passes(pool, body)

    X, UP, HT, Y = ((0, 1), (2, 3)), ((4, 5), (6, 7)), (0, 1), ((2, 3), (4, 5))

    @block.tensor
    def _(pe):
        def body(n, b, owner):
            for u in R2:
                pe.wait_ge(x_in[u], n * 16 + 16)
                if u == 0:
                    pe.wait_ge(hT_ready[0], n)
                    pe.wait_ge(hT_ready[1], n)
                else:
                    pe.wait_ge(y_ready[0], n)
                for c in range(KC):
                    t = pe.transpose(k.bank[X[u][c // 4]][:, (c % 4) * P:(c % 4 + 1) * P], x[u][:, c:D:KC], k.eye[:])
                t.then_inc(x_turned[u], 1)
            for u in R2:
                pe.wait_ge(xT_ready[u], n * 2 + 2)
                pe.wait_ge(w13_in[u], n * 32 + 32)
                if u == 0:
                    pe.wait_ge(y_ready[1], n)
                else:
                    pe.wait_ge(h_ready[1], n)
                for half, w in enumerate((w1[u], w3[u])):
                    for c in range(KC):
                        mm = pe.matmul(k.bank[UP[u][half]][:], xT[u][:, c, :], w[:, c, :], start=(c == 0), stop=(c == KC - 1))
                mm.then_inc(up_ready[u], 1)
            for u in R2:
                pe.wait_ge(h_ready[u], n + 1)
                if u == 1:
                    pe.wait_ge(xT_ready[1], n * 2 + 2)
                for c in range(FC):
                    t = pe.transpose(k.bank[HT[u]][:, c * P:(c + 1) * P], hh[u][:, c:FF:FC], k.eye[:])
                t.then_inc(h_turned[u], 1)
                pe.wait_ge(hT_ready[u], n + 1)
                pe.wait_ge(w2_in[u], n * 16 + 16)
                for half in range(2):
                    for c in range(FC):
                        mm = pe.matmul(k.bank[Y[u][half]][:], hT[u][:, c, :], w2[u][:, c, half * 512:(half + 1) * 512],
                                       start=(c == 0), stop=(c == FC - 1))
                mm.then_inc(y_mm[u], 1)
        passes(pe, body)

    @block.scalar
    def _(act):
        def body(n, b, owner):
            for u in R2:
                act.wait_ge(x_turned[u], n + 1)
                act.wait_ge(up_ready[u], n)
                for half in range(2):
                    nc.scalar.copy(xT[u][:, 4 * half:4 * half + 4, :],
                                   k.bank[X[u][half]][:].rearrange("p (c q) -> p c q", c=4)).then_inc(xT_ready[u], 1)
            for u in R2:
                act.wait_ge(up_ready[u], n + 1)
                act.wait_ge(h_ready[u], n)
                nc.scalar.activation(hs[u][:], k.bank[UP[u][0]][:], ACT.Silu).then_inc(silu_ready[u], 1)
            for u in R2:
                act.wait_ge(y_mm[u], n + 1)
                act.wait_ge(y_stored[u], n * 16)
                for half in range(2):
                    c = nc.scalar.copy(y[u][:, half * 512:(half + 1) * 512], k.bank[Y[u][half]][:])
                c.then_inc(y_ready[u], 1)
                act.wait_ge(y_ready[u], n + 1)
                act.dma_start(dr["moe_y"][ds(b * P + u * P, P), :], y[u][:]).then_inc(y_stored[u], 16)
        count = passes(act, body)
        for u in R2:
            act.wait_ge(y_stored[u], ((count + 1) // 2 + MAIN) * 16)
        act.sem_inc(all_stored, 1)

    @block.vector
    def _(dve):
        def body(n, b, owner):
            for u in R2:
                dve.wait_ge(silu_ready[u], n + 1)
                dve.wait_ge(h_turned[u], n)
                nc.vector.tensor_tensor(hh[u][:], hs[u][:], k.bank[UP[u][1]][:], ALU.mult).then_inc(h_ready[u], 1)
            for u in R2:
                dve.wait_ge(h_turned[u], n + 1)
                dve.wait_ge(y_mm[u], n)
                nc.vector.tensor_copy(hT[u][:].rearrange("p c q -> p (c q)"), k.bank[HT[u]][:]).then_inc(hT_ready[u], 1)
        passes(dve, body)


def combine(k, l, first, slots, wts):
    nc, dr = k.nc, k.dram
    R2 = range(2)
    T = NT - first
    g = k.sb("gate_rows", [P, 2, D])
    y = [[k.sb(f"y{u}{c}", [P, D]) for c in R2] for u in R2]
    s = [[k.sb(f"slot{u}{c}", [P, 1], I32) for c in R2] for u in R2]
    g_in, order, gather_due = k.sem("g_in"), k.sem("order"), k.sem("gather_due")
    y_in, copied, scaled, added = ([k.sem(f"{n}{u}") for u in R2] for n in ("y_in", "copied", "scaled", "added"))
    block = k.block()

    def passes(eng, body):
        if first == 0:
            body(0, 0, 0)
        with eng.Fori(1, NT // 2) as i:
            body(i, i if first == 0 else i - 1, 1)

    @block.sync
    def _(sp):
        for v in R2:
            spread_row(k, sp, g[:, v, :], l, v, 5, g_in)

    @block.gpsimd
    def _(pool):
        def body(i, n, v):
            for u in R2:
                pool.wait_ge(y_in[u], n * 32)
                for c in R2:
                    nc.gpsimd.tensor_copy(s[u][c][:], slots[:, c, ds(n * 2 + u, 1)]).then_inc(copied[u], 1)
                pool.wait_ge(added[u], n)
                pool.wait_ge(copied[u], n * 2 + 2)
                pool.sem_inc(gather_due, 1)
                for c in R2:
                    pool.indirect_dma_start(y[u][c][:], None, dr["moe_y"],
                                            bass.IndirectOffsetOnAxis(ap=s[u][c][:, 0:1], axis=0)).then_inc(y_in[u], 16)
        passes(pool, body)

    @block.scalar
    def _(act):
        def body(i, n, v):
            for u in R2:
                act.wait_ge(y_in[u], n * 32 + 32)
                nc.scalar.activation(y[u][0][:], y[u][0][:], ACT.Copy,
                                     scale=wts[:, 0, ds(n * 2 + u, 1)]).then_inc(scaled[u], 1)
        passes(act, body)

    @block.vector
    def _(dve):
        dve.wait_ge(g_in, 32)
        st = Steps(dve, order, 4)

        def body(i, n, v):
            st.at(n)
            for u in R2:
                dve.wait_ge(scaled[u], n + 1)
                st.link(nc.vector.scalar_tensor_tensor(out=y[u][1][:], in0=y[u][1][:], scalar=wts[:, 1, ds(n * 2 + u, 1)],
                                                       in1=y[u][0][:], op0=ALU.mult, op1=ALU.add))
                st.link(nc.vector.tensor_tensor(y[u][1][:], y[u][1][:], g[:, v, :], ALU.mult))
                h = k.H[:, ds(i * 2 + u, 1), :].rearrange("p a d -> p (a d)")
                nc.vector.tensor_tensor(h, h, y[u][1][:], ALU.add).then_inc(added[u], 1)
            st.end()
        passes(dve, body)


def moe(k, l, first):
    with k.scope():
        T = NT - first
        slots, wts = k.sb("slots", [P, 2, T], I32), k.sb("weights", [P, 2, T])
        table = k.sb("table", [P, OVER + 2], I32)
        with k.scope():
            logits = k.sb("logits", [P, T, GROUPS + NE])
            with k.scope():
                norm_mod(k, l, 1, first, logits=logits)
            with k.scope():
                route(k, first, logits, slots, wts, table)
        with k.scope():
            experts(k, l, table)
        with k.scope():
            combine(k, l, first, slots, wts)


def project1(k, aT):
    nc, dr = k.nc, k.dram
    R2 = range(2)
    QW, KW = ATT_H * HD, ATT_KV * HD
    RH = (QW + KW) // HD
    NF = HD // 4
    w = k.sb("w_in", [P, KC, ATT_COLS])
    rope = k.sb("rope", [P, LT, 2, 2, NF])
    z, rt = [k.sb(f"z{s}", [P, ATT_COLS]) for s in R2], [k.sb(f"rotated{s}", [P, RH, 2, 2, NF]) for s in R2]
    kd = [k.sb(f"k_twice{s}", [P, ATT_KV, 2, HD]) for s in R2]
    out = [k.sb(f"turned{s}", [P, 12, P]) for s in R2]
    t1, t2, t3, t4 = (k.sb(f"t{n}", [P, RH, 2, NF]) for n in range(4))
    pad = k.sb("zero", [P, ATT_KV * P])
    w_in, rope_in, z_ready, z_copied = k.sem("w_in"), k.sem("rope_in"), k.sem("z_ready"), k.sem("z_copied")
    first_ready, second_ready, kd_ready = k.sem("first_ready"), k.sem("second_ready"), k.sem("kd_ready")
    turned, taken, dve_order, pool_order = k.sem("turned"), k.sem("taken"), k.sem("dve_order"), k.sem("pool_order")
    stored, pad_set, padded = [k.sem(f"stored{s}") for s in R2], k.sem("pad_set"), k.sem("padded")
    block = k.block()

    def rounds(t):
        return t if t < CT else CT + 3 * (t - CT)

    def stores(t):
        return sum(48 if x >= CT else 32 for x in range(t % 2, t, 2))

    def place(t):
        return t - CT + 1 if t >= CT else LT + 2 + t

    @block.sync
    def _(sp):
        for g in (2, 0, 1):
            sp.dma_start(w[:, :, g * 512:(g + 1) * 512],
                         dr["at_w_in"][0, :, g * 512:(g + 1) * 512].rearrange("(j p) n -> p j n", p=P)).then_inc(w_in, 16)
        sp.dma_start(rope[:].rearrange("p t a b f -> p t (a b f)"),
                     dr["const_rope"].rearrange("(t p) a b f -> p t (a b f)", p=P)).then_inc(rope_in, 16)
        sp.wait_ge(pad_set, 1)
        for at in (0, LT + 1):
            sp.dma_start(dr["att_k"][at], pad[:]).then_inc(padded, 16)
            sp.dma_start(dr["att_v"][at], pad[:, 0:KW]).then_inc(padded, 16)
        for t in range(NT):
            s = t % 2
            sp.wait_ge(taken, rounds(t + 1))
            if t >= CT:
                sp.dma_start(dr["att_q"][t - CT], out[s][:, 0:8, :].rearrange("p c n -> p (c n)")).then_inc(stored[s], 16)
            sp.dma_start(dr["att_k"][place(t)], out[s][:, 8:12, :].rearrange("p c n -> p (c n)")).then_inc(stored[s], 16)
            sp.dma_start(dr["att_v"][place(t)], z[s][:, QW + KW:]).then_inc(stored[s], 16)
        for s in R2:
            sp.wait_ge(stored[s], stores(NT + s))
        sp.wait_ge(padded, 64)

    @block.tensor
    def _(pe):
        pe.wait_ge(w_in, 48)

        def project(t):
            s = t % 2
            if t >= 2:
                pe.wait_ge(z_copied, t - 1)
            for g in ((2,) if t < CT else (0, 1, 2)):
                for c in range(KC):
                    mm = pe.matmul(k.bank[3 * s + g][:], aT[:, c, t * P:(t + 1) * P], w[:, c, g * 512:(g + 1) * 512],
                                   start=(c == 0), stop=(c == KC - 1))
            mm.then_inc(z_ready, 1)

        def turn(t):
            s = t % 2
            pe.wait_ge(kd_ready, t + 1)
            for g in ((2,) if t < CT else (0, 1, 2)):
                r = rounds(t) + (g if t >= CT else 0)
                if r >= 2:
                    pe.wait_ge(taken, r - 1)
                for q in range(4):
                    c = 4 * g + q
                    src = (kd[s][:].rearrange("p h a d -> p (h a d)")[:, (c - 8) * P:(c - 7) * P] if g == 2 else
                           rt[s][:].rearrange("p h a b f -> p (h a b f)")[:, c * P:(c + 1) * P])
                    mm = pe.transpose(k.bank[6 + r % 2][:, q * P:(q + 1) * P], src, k.eye[:])
                mm.then_inc(turned, 1)

        for t in range(NT + 1):
            if t < NT:
                project(t)
            if t > 0:
                turn(t - 1)

    @block.scalar
    def _(act):
        for t in range(NT + 1):
            if t < NT:
                s = t % 2
                act.wait_ge(z_ready, t + 1)
                if t >= 2:
                    act.wait_ge(stored[s], stores(t))
                for g in ((2,) if t < CT else (0, 1, 2)):
                    c = nc.scalar.copy(z[s][:, g * 512:(g + 1) * 512], k.bank[3 * s + g][:])
                c.then_inc(z_copied, 1)
                if t < CT:
                    act.wait_ge(z_copied, t + 1)
                    keys = z[s][:, QW:QW + KW].rearrange("p (h d) -> p h d", h=ATT_KV)
                else:
                    act.wait_ge(first_ready, t - CT + 1)
                    act.wait_ge(second_ready, t - CT + 1)
                    keys = rt[s][:, ATT_H:, :, :, :].rearrange("p h a b f -> p h (a b f)")
                if t >= 2:
                    act.wait_ge(turned, rounds(t - 1))
                nc.scalar.copy(kd[s][:], keys.unsqueeze(2).to_broadcast([P, ATT_KV, 2, HD])).then_inc(kd_ready, 1)
            if t > 0:
                u = t - 1
                for g in ((2,) if u < CT else (0, 1, 2)):
                    r = rounds(u) + (g if u >= CT else 0)
                    act.wait_ge(turned, r + 1)
                    nc.scalar.copy(out[u % 2][:, 4 * g:4 * g + 4, :].rearrange("p c n -> p (c n)"),
                                   k.bank[6 + r % 2][:]).then_inc(taken, 1)

    def halves(t):
        s = t % 2
        u = z[s][:, 0:QW + KW].rearrange("p (h a b f) -> p h a b f", a=2, b=2, f=NF)
        cos, sin = (rope[:, t - CT, n].unsqueeze(1).to_broadcast([P, RH, 2, NF]) for n in R2)
        return u[:, :, :, 0, :], u[:, :, :, 1, :], cos, sin

    @block.vector
    def _(dve):
        dve.wait_ge(rope_in, 16)
        st = Steps(dve, dve_order)
        for t in range(CT, NT):
            dve.wait_ge(z_copied, t + 1)
            dve.wait_ge(turned, rounds(t - 1))
            a, b, cos, sin = halves(t)
            nc.vector.tensor_tensor(t1[:], a, cos, ALU.mult)
            st.link(nc.vector.tensor_tensor(t2[:], b, sin, ALU.mult))
            nc.vector.tensor_tensor(rt[t % 2][:, :, :, 0, :], t1[:], t2[:], ALU.subtract).then_inc(first_ready, 1)

    @block.gpsimd
    def _(pool):
        nc.gpsimd.memset(pad[:], 0.0).then_inc(pad_set, 1)
        pool.wait_ge(rope_in, 16)
        st = Steps(pool, pool_order)
        for t in range(CT, NT):
            pool.wait_ge(z_copied, t + 1)
            pool.wait_ge(turned, rounds(t - 1))
            a, b, cos, sin = halves(t)
            nc.gpsimd.tensor_tensor(t3[:], a, sin, ALU.mult)
            st.link(nc.gpsimd.tensor_tensor(t4[:], b, cos, ALU.mult))
            nc.gpsimd.tensor_tensor(rt[t % 2][:, :, :, 1, :], t3[:], t4[:], ALU.add).then_inc(second_ready, 1)


def attend(k, att):
    nc, dr = k.nc, k.dram
    R2 = range(2)
    W, C = 3 * P, CTX
    PAIRS, KVS = ATT_H // 2, ATT_KV
    M, KM = 2 * PAIRS, 2 * KVS
    PASSES = LT // 2
    SCALE = HD ** -0.5
    q, kw = [k.sb(f"q{u}", [P, PAIRS, P]) for u in R2], [k.sb(f"k_win{u}", [P, 3, KVS, P]) for u in R2]
    vw, band = [k.sb(f"v_win{u}", [P, 3, KVS * HD]) for u in R2], [k.sb(f"band{u}", [P, W]) for u in R2]
    kc, vc = k.sb("k_ctx", [P, KVS, C]), k.sb("v_ctx", [P, CT, KVS * HD])
    sink, sink8 = k.sb("sink", [P, ATT_H]), k.sb("sink_scaled", [P, ATT_H])
    sm, pr = [k.sb(f"masked{s}", [P, 2, W]) for s in R2], [k.sb(f"probs{s}", [P, 2, W + C]) for s in R2]
    pt = [k.sb(f"probsT{s}", [P, 5, 2, 2, P]) for s in R2]
    small = [{n: k.sb(f"{n}{s}", [P, 2]) for n in ("max_win", "max_ctx", "neg_max", "sum_win", "sum_ctx",
                                                      "sink_part", "den")} for s in R2]
    ctx_in, blk_in = k.sem("ctx_in"), [k.sem(f"blk_in{u}") for u in R2]
    ctx0_ready = k.sem("ctx0_ready")
    s_ready, max_ready, p_ready, order = k.sem("s_ready"), k.sem("max_ready"), k.sem("p_ready"), k.sem("dve_order")
    inv_ready, scaled0, scaled1, sink_set = k.sem("inv_ready"), k.sem("scaled0"), k.sem("scaled1"), k.sem("sink_set")
    turned, pt_act, pt_dve = k.sem("turned"), k.sem("pt_act"), k.sem("pt_dve")
    o_ready, o_taken, den_order = k.sem("o_ready"), k.sem("o_taken"), k.sem("den_order")
    block = k.block()

    def logit_banks(m):
        return [k.bank[3 * (m % 2) + n] for n in range(3)]

    def fill(m, r):
        return 7 * (m // 2) + 3 * (m % 2) + r

    def wait_fill(pe, n, f):
        g, x = (f - 2) // 7, (f - 2) % 7
        if f < 2:
            pe.wait_ge(pt_dve, n * M)
            pe.wait_ge(o_taken, n * KM)
        elif x == 6:
            pe.wait_ge(o_taken, n * KM + g + 1)
        elif x % 3 == 2:
            pe.wait_ge(pt_dve, n * M + 2 * g + x // 3 + 1)
        else:
            pe.wait_ge(pt_act, n * 2 * M + 4 * g + 2 * (x // 3) + x % 3 + 1)

    @block.sync
    def _(sp):
        for t in range(CT):
            sp.dma_start(kc[:, :, t * P:(t + 1) * P], dr["att_k"][LT + 2 + t].rearrange("p (h n) -> p h n", h=KVS)).then_inc(ctx_in, 16)
        sp.dma_start(vc[:], dr["att_v"][LT + 2:].rearrange("t p n -> p t n")).then_inc(ctx_in, 16)
        sp.dma_start(sink[:], dr["at_sink"].to_broadcast([P, ATT_H])).then_inc(ctx_in, 16)

        def load(b, u):
            sp.dma_start(q[u][:].rearrange("p c n -> p (c n)"), dr["att_q"][ds(b, 1)].rearrange("a p n -> p (a n)")).then_inc(blk_in[u], 16)
            sp.dma_start(kw[u][:].rearrange("p t h n -> p t (h n)"), dr["att_k"][ds(b, 3)].rearrange("t p n -> p t n")).then_inc(blk_in[u], 16)
            sp.dma_start(vw[u][:], dr["att_v"][ds(b, 3)].rearrange("t p n -> p t n")).then_inc(blk_in[u], 16)
            sp.dma_start(band[u][:], dr["const_band"][ds(b, 1)].rearrange("a p n -> p (a n)")).then_inc(blk_in[u], 16)

        for u in R2:
            load(u, u)
        with sp.Fori(1, PASSES) as i:
            for u in R2:
                sp.wait_ge(o_ready, (i - 1) * KM + (u + 1) * KVS)
                load(i * 2 + u, u)

    @block.tensor
    def _(pe):
        pe.wait_ge(ctx_in, 64)

        def scores(n, m):
            u, kv, c = m // PAIRS, (m % PAIRS) // 2, m % PAIRS
            b = logit_banks(m)
            pe.wait_ge(p_ready, n * M + m - 1 if m >= 2 else n * M)
            if m % PAIRS == 0:
                pe.wait_ge(blk_in[u], n * 64 + 64)
            for h in R2:
                on = slice(HD * h, HD * h + HD)
                pe.matmul(b[h][:, 0:W], q[u][on, c, :], kw[u][on, :, kv, :], start=True, stop=True)
                if h:
                    pe.wait_ge(ctx0_ready, n * M + m + 1)
                mm = pe.matmul(b[2][:, h * C:(h + 1) * C], q[u][on, c, :], kc[on, kv, :], start=True, stop=True)
                mm.then_inc(s_ready if h else ctx0_ready, 1)

        def turn(n, m):
            for r in range(3):
                f = fill(m, r)
                wait_fill(pe, n, f)
                for h in ((r,) if r < 2 else R2):
                    pe.wait_ge((scaled0, scaled1)[h], n * M + m + 1)
                    for c in (range(4) if r < 2 else (4,)):
                        at = c * P if r < 2 else h * P
                        mm = pe.transpose(k.bank[6 + f % 2][:, at:at + P], pr[m % 2][:, h, c * P:(c + 1) * P], k.eye[:])
                mm.then_inc(turned, 1)

        def output(n, m):
            g = m // 2
            u, kv = g // KVS, g % KVS
            f = fill(m, 3)
            wait_fill(pe, n, f)
            pe.wait_ge(pt_act, n * 2 * M + 2 * m + 2)
            pe.wait_ge(pt_dve, n * M + m + 1)
            to = k.bank[6 + f % 2]
            for h in R2:
                for c in range(5):
                    v = vw[u][:, c, kv * HD:(kv + 1) * HD] if c < 3 else vc[:, c - 3, kv * HD:(kv + 1) * HD]
                    mm = pe.matmul(to[HD * h:HD * h + HD, 0:2 * P], v, pt[g % 2][:, c, h, :, :],
                                   start=(c == 0), stop=(c == 4))
            mm.then_inc(o_ready, 1)

        with pe.Fori(0, PASSES) as n:
            scores(n, 0)
            for m in range(M):
                if m + 1 < M:
                    scores(n, m + 1)
                turn(n, m)
                if m % 2:
                    output(n, m)

    @block.scalar
    def _(act):
        act.wait_ge(ctx_in, 64)
        with act.Fori(0, PASSES) as n:
            for m in range(M):
                s, x = m % 2, small[m % 2]
                b = logit_banks(m)
                act.wait_ge(max_ready, n * M + m + 1)
                act.wait_ge(turned, 3 * (n * M) + 3 * (m - 1) if m >= 2 else n * (3 * M))
                act.wait_ge(inv_ready, n * M + m - 1 if m >= 2 else n * M)
                nc.scalar.activation(x["sink_part"][:], x["sink_part"][:], ACT.Exp)
                for h in R2:
                    nc.scalar.activation(pr[s][:, h, 0:W], sm[s][:, h, :], ACT.Exp, bias=x["neg_max"][:, h:h + 1],
                                         scale=SCALE, accum_out=x["sum_win"][:, h:h + 1])
                    e = nc.scalar.activation(pr[s][:, h, W:], b[2][:, h * C:(h + 1) * C], ACT.Exp,
                                             bias=x["neg_max"][:, h:h + 1], scale=SCALE, accum_out=x["sum_ctx"][:, h:h + 1])
                e.then_inc(p_ready, 1)
                for h in R2:
                    act.wait_ge(turned, n * (3 * M) + 3 * m + h + 1)
                    g = m // 2
                    if m % 2 == 0 and h == 0:
                        act.wait_ge(o_ready, n * KM + g - 1 if g >= 2 else n * KM)
                    nc.scalar.copy(pt[g % 2][:, 0:4, h, m % 2, :],
                                   k.bank[6 + fill(m, h) % 2][:].rearrange("p (c n) -> p c n", c=4)).then_inc(pt_act, 1)

    @block.gpsimd
    def _(pool):
        with pool.Fori(0, PASSES) as n:
            for m in range(M):
                pool.wait_ge(inv_ready, n * M + m + 1)
                nc.gpsimd.tensor_tensor(pr[m % 2][:, 0, :], pr[m % 2][:, 0, :],
                                        small[m % 2]["den"][:, 0:1].to_broadcast([P, W + C]), ALU.mult).then_inc(scaled0, 1)

    @block.vector
    def _(dve):
        V = nc.vector
        dve.wait_ge(ctx_in, 64)
        V.tensor_scalar(sink8[:], sink[:], 1.0 / SCALE, None, ALU.mult).then_inc(sink_set, 1)
        dve.wait_ge(sink_set, 1)
        st = Steps(dve, order, M * 4)

        def maxima(n, m):
            u, x, b = m // PAIRS, small[m % 2], logit_banks(m)
            if m % PAIRS == 0:
                dve.wait_ge(blk_in[u], n * 64 + 64)
            dve.wait_ge(s_ready, n * M + m + 1)
            heads = slice(2 * (m % PAIRS), 2 * (m % PAIRS) + 2)
            V.tensor_reduce(x["max_ctx"][:], b[2][:].rearrange("p (h n) -> p h n", h=2), AX.X, ALU.max)
            for h in R2:
                r = V.tensor_tensor_reduce(out=sm[m % 2][:, h, :], in0=b[h][:, 0:W], in1=band[u][:], scale=1.0,
                                           scalar=-3e38, op0=ALU.add, op1=ALU.max, accum_out=x["max_win"][:, h:h + 1])
            st.link(r)
            st.link(V.tensor_tensor(x["max_ctx"][:], x["max_ctx"][:], x["max_win"][:], ALU.max))
            st.link(V.tensor_tensor(x["max_ctx"][:], x["max_ctx"][:], sink8[:, heads], ALU.max))
            st.link(V.tensor_scalar(x["neg_max"][:], x["max_ctx"][:], -SCALE, None, ALU.mult))
            V.tensor_tensor(x["sink_part"][:], sink[:, heads], x["neg_max"][:], ALU.add).then_inc(max_ready, 1)

        def divide(n, m):
            x = small[m % 2]
            dve.wait_ge(p_ready, n * M + m + 1)
            V.tensor_tensor(x["den"][:], x["sum_win"][:], x["sum_ctx"][:], ALU.add).then_inc(den_order, 1)
            dve.wait_ge(den_order, (n * M + m) * 2 + 1)
            V.tensor_tensor(x["den"][:], x["den"][:], x["sink_part"][:], ALU.add).then_inc(den_order, 1)
            dve.wait_ge(den_order, (n * M + m) * 2 + 2)
            V.reciprocal(x["den"][:], x["den"][:]).then_inc(inv_ready, 1)
            dve.wait_ge(inv_ready, n * M + m + 1)
            V.tensor_scalar(pr[m % 2][:, 1, :], pr[m % 2][:, 1, :], x["den"][:, 1:2], None, ALU.mult).then_inc(scaled1, 1)

        with dve.Fori(0, PASSES) as n:
            st.at(n)
            maxima(n, 0)
            for m in range(M):
                g = m // 2
                u, kv = g // KVS, g % KVS
                divide(n, m)
                if m + 1 < M:
                    maxima(n, m + 1)
                dve.wait_ge(turned, n * (3 * M) + 3 * m + 3)
                if m % 2 == 0:
                    dve.wait_ge(o_ready, n * KM + g - 1 if g >= 2 else n * KM)
                V.tensor_copy(pt[g % 2][:, 4, :, m % 2, :],
                              k.bank[6 + fill(m, 2) % 2][:, 0:2 * P].rearrange("p (h n) -> p h n", h=2)).then_inc(pt_dve, 1)
                if m % 2:
                    dve.wait_ge(o_ready, n * KM + g + 1)
                    V.tensor_copy(att[:, 2 * kv:2 * kv + 2, ds(n * (2 * P) + u * P, P)],
                                  k.bank[6 + fill(m, 3) % 2][:, 0:2 * P].rearrange("p (c n) -> p c n", c=2)).then_inc(o_taken, 1)
            st.end()


def final_norm(k):
    nc, dr, H = k.nc, k.dram, k.H
    R2 = range(2)
    w = k.sb("norm_rows", [P, D])
    sq, y = k.sb("squares", [P, 2, D]), [k.sb(f"y{u}", [P, D]) for u in R2]
    r = k.sb("rstd", [P, 2])
    w_in, sum_ready, mean_ready, root_ready = k.sem("w_in"), k.sem("sum_ready"), k.sem("mean_ready"), k.sem("root_ready")
    y_ready, order = k.sem("y_ready"), k.sem("order")
    y_stored = [k.sem(f"y_stored{u}") for u in R2]
    block = k.block()

    @block.sync
    def _(sp):
        sp.dma_start(w[:], dr["norm_final"].rearrange("(a n) -> a n", a=1).to_broadcast([P, D])).then_inc(w_in, 16)
        out = dr["out"].rearrange("a t d -> (a t) d")
        with sp.Fori(0, LT // 2) as i:
            for u in R2:
                sp.wait_ge(y_ready, i * 2 + u + 1)
                sp.dma_start(out[ds(i * (2 * P) + u * P, P), :], y[u][:]).then_inc(y_stored[u], 16)
        for u in R2:
            sp.wait_ge(y_stored[u], 16 * (LT // 2))

    @block.scalar
    def _(act):
        with act.Fori(0, LT // 2) as i:
            act.wait_ge(y_ready, i * 2)
            for u in R2:
                nc.scalar.activation(sq[:, u, :], H[:, ds(i * 2 + (CT + u), 1), :].rearrange("p a d -> p (a d)"),
                                     ACT.Square, accum_out=r[:, u:u + 1]).then_inc(sum_ready, 1)
            for u in R2:
                act.wait_ge(mean_ready, i * 2 + u + 1)
                nc.scalar.activation(r[:, u:u + 1], r[:, u:u + 1], ACT.Sqrt).then_inc(root_ready, 1)

    @block.vector
    def _(dve):
        dve.wait_ge(w_in, 16)
        st = Steps(dve, order, 2)
        with dve.Fori(0, LT // 2) as i:
            st.at(i)
            for u in R2:
                f = r[:, u:u + 1]
                dve.wait_ge(sum_ready, i * 2 + u + 1)
                nc.vector.tensor_scalar(f, f, 1.0 / D, EPS, ALU.mult, ALU.add).then_inc(mean_ready, 1)
                dve.wait_ge(root_ready, i * 2 + u + 1)
                st.link(nc.vector.reciprocal(f, f))
                dve.wait_ge(y_stored[u], i * 16)
                nc.vector.scalar_tensor_tensor(out=y[u][:], in0=H[:, ds(i * 2 + (CT + u), 1), :].rearrange("p a d -> p (a d)"),
                                               scalar=f, in1=w[:], op0=ALU.mult, op1=ALU.mult).then_inc(y_ready, 1)
            st.end()


def constants():
    i = np.arange(P)
    tri = np.stack([i[:, None] <= i[None, :], i[:, None] >= i[None, :]]).astype(np.float32)
    merge = np.zeros((2, LEVELS, P, P), np.float32)
    for n in range(LEVELS):
        pair = (i[:, None] >> (n + 1)) == (i[None, :] >> (n + 1))
        for d, low in enumerate((i[:, None] > i[None, :], i[:, None] < i[None, :])):
            merge[d, n] = pair & low & ((i[:, None] >> n) != (i[None, :] >> n))
    nf = HD // 4
    inv = np.power(np.float32(10000.0), -np.arange(nf, dtype=np.float32) / np.float32(nf)).astype(np.float32)
    pos = np.arange(SEQ)
    angle = np.stack([(pos // 64).astype(np.float32)[:, None] * inv, (pos % 64).astype(np.float32)[:, None] * inv], 1)
    rope = np.stack([np.cos(angle), np.sin(angle)], 1).astype(np.float32)
    key = np.arange(3 * P)[None, :] - P
    near = np.abs(i[:, None] - key) <= WIN
    band = np.where(np.stack([near & (key >= 0)] + [near] * (LT - 2) + [near & (key < P)]), 0.0, -1e30).astype(np.float32)
    return {
        "const_eye": np.eye(P, dtype=np.float32),
        "const_tri": tri,
        "const_merge": merge,
        "const_rope": rope,
        "const_band": band,
        "const_ramp": np.arange(P, dtype=np.float32)[None, :],
    }


def build(nc, dram):
    k = Kernel(nc, dram)
    with k.scope():
        k.bank = [k.scopes[-1].enter_context(nc.psum_tensor(f"bank{b}", [P, 512], F32)) for b in range(8)]
        k.H = k.sb("H", [P, NT, D])
        k.eye = k.sb("eye", [P, P])
        k.tri = k.sb("tri", [P, 2, P])
        for l in range(2):
            with k.scope():
                modulation(k, l)
        with k.scope():
            k.gate = k.sb("gate", [P, NH, TOK])
            k.short = k.sb("short", [P, NH, TOK])
            k.ab = k.sb("ab", [P, NT, 4 * NH])
            with k.scope():
                aT = k.sb("aT", [P, KC, TOK])
                with k.scope():
                    norm_mod(k, 0, 0, 0, aT=aT)
                with k.scope():
                    project0(k, aT)
            with k.scope():
                oT = k.sb("oT", [P, NH, TOK])
                with k.scope():
                    delta_scan(k, oT)
                with k.scope():
                    gate_heads(k, oT)
                with k.scope():
                    project_out(k, 0, 0, lambda c, t: (oT if c < NH else k.short)[:, c % NH, t * P:(t + 1) * P],
                                "ab_w_out")
        moe(k, 0, 0)
        with k.scope():
            aT = k.sb("aT", [P, KC, TOK])
            with k.scope():
                norm_mod(k, 1, 0, 0, aT=aT)
            with k.scope():
                project1(k, aT)
        with k.scope():
            att = k.sb("att", [P, KC, SEQ])
            with k.scope():
                attend(k, att)
            with k.scope():
                project_out(k, 1, CT, lambda c, t: att[:, c, (t - CT) * P:(t - CT + 1) * P], "at_w_out")
        moe(k, 1, CT)
        with k.scope():
            final_norm(k)


INPUTS = ("x", "c", "ctx", "c_ctx", "ada_w", "ada_b", "norm_mix", "norm_ffn", "norm_final", "ab_w_in",
          "ab_conv_qkv", "ab_conv_sc", "ab_a_log", "ab_dt_bias", "ab_out_norm", "ab_w_out", "at_w_in",
          "at_sink", "at_w_out", "moe_w_group", "moe_w_expert", "moe_w1", "moe_w3", "moe_w2")


def kernel(**inputs):
    import concourse.bacc as bacc
    from concourse.bass_utils import run_bass_kernel_spmd

    nc = bacc.Bacc("TRN2", target_bir_lowering=False, num_devices=1)
    arrays, dram = {}, {}
    for name, a in [(n, np.ascontiguousarray(inputs[n])) for n in INPUTS] + list(constants().items()):
        arrays[f"in_{name}"] = a
        dram[name] = nc.dram_tensor(f"in_{name}", a.shape, mybir.dt.from_np(a.dtype), kind="ExternalInput").ap()
    for name, shape, dt in (
        ("mods", (2, 2, MODS * D), F32),
        ("heads", (4, NT, P, W0), F32),
        ("moe_x", (TOK, D), F32),
        ("att_q", (LT, P, ATT_H // 2 * P), F32),
        ("att_k", (NT + 2, P, ATT_KV * P), F32),
        ("att_v", (NT + 2, P, ATT_KV * HD), F32),
        ("moe_y", (SLOTS, D), F32),
        ("slot_token", (SLOTS, 1), I32),
    ):
        dram[name] = nc.dram_tensor(name, shape, dt).ap()
    dram["out"] = nc.dram_tensor("out", (1, SEQ, D), F32, kind="ExternalOutput").ap()
    build(nc, dram)
    r = run_bass_kernel_spmd(nc, [arrays], core_ids=[0])
    return r.results[0]["out"]
```

```python
from contextlib import ExitStack, contextmanager

import numpy as np

import concourse.bass as bass
import concourse.mybir as mybir

F32 = mybir.dt.float32
I32 = mybir.dt.int32
U32 = mybir.dt.uint32
ACT = mybir.ActivationFunctionType
ALU = mybir.AluOpType
AX = mybir.AxisListType

P = 128
D = 1024
KC = D // P
SEQ, CTX = 1024, 256
TOK = SEQ + CTX
NT = TOK // P
CT = CTX // P
LT = SEQ // P
EPS = 1e-6
NH = 4
W0 = NH * P
ATT_H, ATT_KV, HD = 16, 4, 64
ATT_COLS = (ATT_H + 2 * ATT_KV) * HD
WIN = 128
GROUPS, PER = 4, 8
NE = GROUPS * PER
FF = 512
FC = FF // P
LEVELS = 7
MODS = 6
UNIT = P // 2
MAXP = ((2 * TOK + NE * (UNIT - 1)) // UNIT + 1) // 2
SLOTS = MAXP * P
RING = 3
PRIME = 1
PADTOK = TOK + 4
LAT0 = CTX + 2
SPANS = ((0, CTX), (CTX, 512), (CTX + 512, 512))


class Steps:

    def __init__(self, eng, sem, per=0):
        self.eng, self.sem, self.per, self.base, self.n = eng, sem, per, 0, 0

    def at(self, i):
        self.base, self.n = i * self.per, 0

    def link(self, ins):
        self.n += 1
        ins.then_inc(self.sem, 1)
        self.eng.wait_ge(self.sem, self.base + self.n)

    def end(self):
        assert self.n == self.per, f"{self.n} links in a pass, not {self.per}"


class Kernel:

    def __init__(self, nc, dram):
        self.nc, self.dram, self.ids = nc, dram, 0
        self.scopes, self.sems, self.unprimed = [], [], []

    @contextmanager
    def scope(self):
        with ExitStack() as stack:
            self.scopes.append(stack)
            self.sems.append([])
            yield stack
            self.scopes.pop()
        if sems := self.sems.pop():
            self.nc.clear_and_free_semaphores(sems)

    def sb(self, name, shape, dt=F32):
        self.ids += 1
        return self.scopes[-1].enter_context(self.nc.sbuf_tensor(f"{name}_{self.ids}", list(shape), dt))

    def sem(self, name, primed=False):
        self.ids += 1
        sem = self.nc.alloc_semaphore(f"{name}_{self.ids}")
        self.sems[-1].append(sem)
        if primed:
            self.unprimed.append(sem)
        return sem

    def block(self):
        for sem in self.unprimed:
            self.nc.gpsimd.sem_inc(sem, PRIME)
        self.unprimed = []
        self.nc.all_engine_barrier()
        return self.scopes[-1].enter_context(self.nc.Block())


def ds(i, n):
    return bass.ds(i, n)


def modulation(k, l):
    nc, dr = k.nc, k.dram
    RING, NW = 4, 512
    NN = MODS * D // NW
    c = k.sb("c", [P, 2, KC])
    sc = k.sb("silu_c", [P, KC, 2])
    w = [k.sb(f"ada_w{u}", [P, KC, NW]) for u in range(RING)]
    rows = k.sb("rows", [2, NN, NW])
    bias = k.sb("bias", [2, NN, NW])
    norms = k.sb("norms", [2, 2, D])
    c_in, c_silu = k.sem("c_in"), k.sem("c_silu")
    w_in = [k.sem(f"ada_w_in{u}") for u in range(RING)]
    consts_in = k.sem("consts_in")
    row_ready = [k.sem(f"row_ready{u}") for u in range(RING)]
    row_taken = [k.sem(f"row_taken{u}") for u in range(RING)]
    rows_done, rows_out, h_in = k.sem("rows_done"), k.sem("rows_out"), k.sem("h_in")
    block = k.block()

    @block.sync
    def _(sp):
        sp.dma_start(c[:, 0, :], dr["c_ctx"].rearrange("(p j) -> p j", p=P)).then_inc(c_in, 16)
        sp.dma_start(c[:, 1, :], dr["c"].rearrange("a (p j) -> (a p) j", p=P)).then_inc(c_in, 16)
        for v in range(2):
            sp.dma_start(bias[v:v + 1].rearrange("v n w -> v (n w)"), dr["ada_b"][l:l + 1]).then_inc(consts_in, 16)
            sp.dma_start(norms[v:v + 1, 0, :], dr["norm_mix"][l:l + 1]).then_inc(consts_in, 16)
            sp.dma_start(norms[v:v + 1, 1, :], dr["norm_ffn"][l:l + 1]).then_inc(consts_in, 16)
        src = dr["ada_w"][l].rearrange("(p j) n -> p j n", p=P)
        for u in range(RING):
            sp.dma_start(w[u][:], src[:, :, u * NW:(u + 1) * NW]).then_inc(w_in[u], 16)
        with sp.Fori(1, NN // RING) as i:
            for u in range(RING):
                sp.wait_ge(row_ready[u], i)
                sp.dma_start(w[u][:], src[:, :, ds(i * (RING * NW) + u * NW, NW)]).then_inc(w_in[u], 16)
        sp.wait_ge(rows_done, 2)
        sp.dma_start(dr["mods"][l], rows[:].rearrange("v n w -> v (n w)")).then_inc(rows_out, 16)
        sp.wait_ge(rows_out, 16)

    if l == 0:
        @block.gpsimd
        def _(pool):
            pool.dma_start(k.H[:, 0:CT, :], dr["ctx"].rearrange("b (t p) d -> p (b t) d", p=P)).then_inc(h_in, 16)
            pool.dma_start(k.H[:, CT:NT, :], dr["x"].rearrange("b (t p) d -> p (b t) d", p=P)).then_inc(h_in, 16)
            pool.dma_start(k.eye[:], dr["const_eye"]).then_inc(h_in, 16)
            pool.dma_start(k.tri[:], dr["const_tri"].rearrange("d p n -> p d n")).then_inc(h_in, 16)
            pool.wait_ge(h_in, 64)

    @block.tensor
    def _(pe):
        pe.wait_ge(c_silu, 1)
        with pe.Fori(0, NN // RING) as i:
            for u in range(RING):
                pe.wait_ge(w_in[u], (i + 1) * 16)
                pe.wait_ge(row_taken[u], i)
                for j in range(KC):
                    mm = pe.matmul(k.bank[u][0:2, :], sc[:, j, :], w[u][:, j, :],
                                   start=(j == 0), stop=(j == KC - 1))
                mm.then_inc(row_ready[u], 1)

    @block.scalar
    def _(act):
        act.wait_ge(c_in, 32)
        nc.scalar.activation(sc[:].rearrange("p j v -> p v j"), c[:], ACT.Silu).then_inc(c_silu, 1)

    @block.vector
    def _(dve):
        dve.wait_ge(consts_in, 96)
        with dve.Fori(0, NN // RING) as i:
            for u in range(RING):
                dve.wait_ge(row_ready[u], i + 1)
                nc.vector.tensor_tensor(rows[:, ds(i * RING + u, 1), :].rearrange("v a w -> v (a w)"),
                                        k.bank[u][0:2, :],
                                        bias[:, ds(i * RING + u, 1), :].rearrange("v a w -> v (a w)"),
                                        ALU.add).then_inc(row_taken[u], 1)
        for u in range(RING):
            dve.wait_ge(row_taken[u], NN // RING)
        rv = rows[:].rearrange("v (m a) w -> v m (a w)", m=MODS)
        for which in range(2):
            nc.vector.scalar_tensor_tensor(out=rv[:, 1 + 3 * which, :], in0=rv[:, 1 + 3 * which, :], scalar=1.0,
                                           in1=norms[:, which, :], op0=ALU.add, op1=ALU.mult).then_inc(rows_done, 1)


def spread_row(k, eng, dst, l, v, m, done):
    row = k.dram["mods"][l, v:v + 1, m * D:(m + 1) * D]
    eng.dma_start(dst, row.to_broadcast([P, D])).then_inc(done, 16)


def norm_mod(k, l, which, first, aT=None, logits=None):
    nc, dr, H = k.nc, k.dram, k.H
    vs = (0, 1) if first == 0 else (1,)
    A = k.sb("scale_rows", [P, 2, D])
    S = k.sb("shift_rows", [P, 2, D])
    sq = k.sb("squares", [P, 2, D])
    ssq = k.sb("sumsq", [P, 2])
    rstd = k.sb("rstd", [P, 2])
    a = [k.sb(f"a{u}", [P, D]) for u in range(2)]
    rows_in, sumsq_ready, a_ready = k.sem("rows_in"), k.sem("sumsq_ready"), k.sem("a_ready")
    a_turned, aT_ready = k.sem("a_turned"), k.sem("aT_ready")
    a_stored = [k.sem(f"a_stored{u}") for u in range(2)]
    order, mean_ready, root_ready = k.sem("dve_order"), k.sem("mean_ready"), k.sem("root_ready")
    moe = logits is not None
    NL = GROUPS + NE
    if moe:
        wr = k.sb("w_route", [P, KC, NL])
        fT = k.sb("fT", [P, 2, KC, P])
        logits_ready, logits_taken = k.sem("logits_ready"), k.sem("logits_taken")
    block = k.block()

    def passes(eng, body):
        if first == 0:
            body(0, 0, 0)
        with eng.Fori(1, NT // 2) as i:
            body(i, i if first == 0 else i - 1, 1)

    @block.sync
    def _(sp):
        for v in vs:
            spread_row(k, sp, A[:, v, :], l, v, 1 + 3 * which, rows_in)
            spread_row(k, sp, S[:, v, :], l, v, 3 * which, rows_in)
        if moe:
            sp.dma_start(wr[:, :, 0:GROUPS],
                         dr["moe_w_group"][l].rearrange("(j p) n -> p j n", p=P)).then_inc(rows_in, 16)
            sp.dma_start(wr[:, :, GROUPS:],
                         dr["moe_w_expert"][l].rearrange("(j p) n -> p j n", p=P)).then_inc(rows_in, 16)

            def body(i, n, v):
                for u in range(2):
                    sp.wait_ge(a_ready, 2 * n + u + 1)
                    sp.dma_start(dr["moe_x"][ds(i * 2 * P + u * P, P), :], a[u][:]).then_inc(a_stored[u], 16)
            passes(sp, body)
            for u in range(2):
                sp.wait_ge(a_stored[u], 8 * (NT - first))

    @block.scalar
    def _(act):
        def body(i, n, v):
            act.wait_ge(a_ready, 2 * n)
            for u in range(2):
                nc.scalar.activation(sq[:, u, :], H[:, ds(i * 2 + u, 1), :].rearrange("p a d -> p (a d)"),
                                     ACT.Square, accum_out=ssq[:, u:u + 1]).then_inc(sumsq_ready, 1)
            for u in range(2):
                act.wait_ge(mean_ready, 2 * n + u + 1)
                nc.scalar.activation(rstd[:, u:u + 1], rstd[:, u:u + 1], ACT.Sqrt).then_inc(root_ready, 1)
            for u in range(2):
                act.wait_ge(a_turned, 2 + 2 * n + u + 1)
                if moe:
                    act.wait_ge(logits_ready, 2 + 2 * n + u - 1)
                for half in range(2):
                    src = k.bank[2 * u + half][:].rearrange("p (c q) -> p c q", c=4)
                    if moe:
                        dst = fT[:, u, 4 * half:4 * half + 4, :]
                    else:
                        dst = aT[:, 4 * half:4 * half + 4, ds(i * (2 * P) + u * P, P)]
                    nc.scalar.copy(dst, src).then_inc(aT_ready, 1)
        passes(act, body)

    @block.vector
    def _(dve):
        dve.wait_ge(rows_in, 16 * (2 * len(vs) + 2 * moe))
        st = Steps(dve, order, 4)

        def body(i, n, v):
            st.at(n)
            for u in range(2):
                r = rstd[:, u:u + 1]
                dve.wait_ge(sumsq_ready, 2 * n + u + 1)
                nc.vector.tensor_scalar(r, ssq[:, u:u + 1], 1.0 / D, EPS, ALU.mult, ALU.add).then_inc(mean_ready, 1)
                dve.wait_ge(root_ready, 2 * n + u + 1)
                st.link(nc.vector.reciprocal(r, r))
                dve.wait_ge(a_turned, 2 + 2 * n + u - 1)
                if moe:
                    dve.wait_ge(a_stored[u], n * 16)
                st.link(nc.vector.scalar_tensor_tensor(
                    out=a[u][:], in0=H[:, ds(i * 2 + u, 1), :].rearrange("p a d -> p (a d)"), scalar=r,
                    in1=A[:, v, :], op0=ALU.mult, op1=ALU.mult))
                nc.vector.tensor_tensor(a[u][:], a[u][:], S[:, v, :], ALU.add).then_inc(a_ready, 1)
            st.end()
            if moe:
                for u in range(2):
                    dve.wait_ge(logits_ready, 2 + 2 * n + u + 1)
                    nc.vector.tensor_copy(logits[:, ds(i * 2 + u - first, 1), :].rearrange("p a e -> p (a e)"),
                                          k.bank[4 + u][:, 0:NL]).then_inc(logits_taken, 1)
        passes(dve, body)

    @block.tensor
    def _(pe):
        pe.sem_inc(a_turned, 2)
        if moe:
            pe.sem_inc(logits_ready, 2)

        def body(i, n, v):
            pe.wait_ge(aT_ready, 4 * n)
            for u in range(2):
                pe.wait_ge(a_ready, 2 * n + u + 1)
                for c in range(KC):
                    t = pe.transpose(k.bank[2 * u + c // 4][:, (c % 4) * P:(c % 4 + 1) * P],
                                     a[u][:, c * P:(c + 1) * P], k.eye[:])
                t.then_inc(a_turned, 1)
            if moe:
                pe.wait_ge(logits_taken, 2 * n)
                for u in range(2):
                    pe.wait_ge(aT_ready, 4 * n + 2 * u + 2)
                    for c in range(KC):
                        mm = pe.matmul(k.bank[4 + u][:, 0:NL], fT[:, u, c, :], wr[:, c, :],
                                       start=(c == 0), stop=(c == KC - 1))
                    mm.then_inc(logits_ready, 1)
        passes(pe, body)


def project0(k, aT):
    nc, dr = k.nc, k.dram
    PARTS = 7
    QC, ALPHA = 3 * W0, 4 * W0
    SC = ALPHA + 4 * NH
    COLS = (0, W0, 2 * W0, QC, SC + W0, SC + 2 * W0, SC)
    w = [k.sb(f"w{j}", [P, KC, P]) for j in range(PARTS)]
    wab = k.sb("w_ab", [P, KC, 4 * NH])
    cq = k.sb("conv_qkv", [P, 3, 3 * NH])
    csc = k.sb("conv_sc", [P, 3, NH])
    x = k.sb("x_raw", [P, PADTOK])
    y = k.sb("y", [P, PADTOK])
    z = k.sb("z", [P, PADTOK])
    bt = k.sb("by_token", [P, NT, P])
    ones, zero = k.sb("ones", [P, P]), k.sb("zero", [P, D])
    zero_set, cleared = k.sem("zero_set"), k.sem("cleared")
    r = k.sb("inv_norm", [P, 2, 512])
    w_in = [k.sem(f"w_in{j}") for j in range(PARTS)]
    w_used = [k.sem(f"w_used{j}") for j in range(PARTS)]
    consts_in, ones_set, pads_set = k.sem("consts_in"), k.sem("ones_set"), k.sem("pads_set")
    z_ready = [k.sem(f"z_ready{s}") for s in range(2)]
    z_copied = [k.sem(f"z_copied{s}") for s in range(2)]
    z_gated = [k.sem(f"z_gated{s}") for s in range(2)]
    ab_ready, ab_taken = k.sem("ab_ready"), k.sem("ab_taken")
    conv_ready, silu_ready = k.sem("conv_ready"), k.sem("silu_ready")
    sq_ready, norm_ready, norm_taken = k.sem("sq_ready"), k.sem("norm_ready"), k.sem("norm_taken")
    y_ready, y_stored = k.sem("y_ready"), k.sem("y_stored")
    turn_taken, bt_stored = k.sem("turn_taken"), k.sem("bt_stored")
    order, root_ready = k.sem("dve_order"), k.sem("root_ready")
    block = k.block()

    def use(j):
        return j // 2

    CNT = (4, 3)
    COPIED = (3, 2)
    AUX = 12

    @block.sync
    def _(sp):
        sp.dma_start(wab[:], dr["ab_w_in"][0, :, ALPHA:SC].rearrange("(j p) n -> p j n", p=P)).then_inc(consts_in, 16)
        for t in range(3):
            sp.dma_start(cq[:, t, :], dr["ab_conv_qkv"][0, t].rearrange("(c p) -> p c", p=P),
                         allow_slow_non_contiguous=True).then_inc(consts_in, 16)
            sp.dma_start(csc[:, t, :], dr["ab_conv_sc"][0, t].rearrange("(c p) -> p c", p=P),
                         allow_slow_non_contiguous=True).then_inc(consts_in, 16)
        src = dr["ab_w_in"][0].rearrange("(j p) n -> p j n", p=P)
        for j in range(PARTS):
            sp.dma_start(w[j][:], src[:, :, COLS[j]:COLS[j] + P]).then_inc(w_in[j], 16)
        with sp.Fori(1, NH) as h:
            for j in range(PARTS):
                sp.wait_ge(z_ready[j % 2], (h - 1) * CNT[j % 2] + use(j) + 1)
                sp.dma_start(w[j][:], src[:, :, ds(h * P + COLS[j], P)]).then_inc(w_in[j], 16)

    def store_channels(eng, part, h):
        out = dr["heads"][part]
        eng.dma_start(out[0:CT, :, ds(h * P, P)].rearrange("t p n -> p t n"),
                      z[:, 0:CTX].rearrange("p (t n) -> p t n", n=P)).then_inc(y_stored, 16)
        eng.dma_start(out[CT:NT, :, ds(h * P, P)].rearrange("t p n -> p t n"),
                      z[:, LAT0:LAT0 + SEQ].rearrange("p (t n) -> p t n", n=P)).then_inc(y_stored, 16)

    @block.gpsimd
    def _(pool):
        nc.gpsimd.memset(ones[:], 1.0).then_inc(ones_set, 1)
        nc.gpsimd.memset(zero[:], 0.0).then_inc(zero_set, 1)
        pool.wait_ge(zero_set, 1)
        more = dr["moe_y"][2 * NT * P:SLOTS, :].rearrange("(b p) d -> p b d", p=P)
        pool.dma_start(more, zero[:].unsqueeze(1).to_broadcast([P, MAXP - 2 * NT, D])).then_inc(cleared, 16)
        with pool.Fori(0, NH) as h:
            for n, part in enumerate((0, 1)):
                pool.wait_ge(y_ready, h * 2 + n + 1)
                store_channels(pool, part, h)
            for n, part in enumerate((2, 3)):
                pool.wait_ge(turn_taken, h * 6 + 3 * n + 3)
                pool.dma_start(dr["heads"][part, :, :, ds(h * P, P)].rearrange("t p n -> p t n"),
                               bt[:]).then_inc(bt_stored, 16)
        pool.wait_ge(y_stored, NH * 64)
        pool.wait_ge(bt_stored, NH * 32)
        pool.wait_ge(cleared, 16)

    @block.tensor
    def _(pe):
        pe.wait_ge(consts_in, 16 * 7)
        pe.wait_ge(ones_set, 1)
        for t in range(NT):
            for j in range(KC):
                mm = pe.matmul(k.bank[7][:, t * 4 * NH:(t + 1) * 4 * NH], aT[:, j, t * P:(t + 1) * P], wab[:, j, :],
                               start=(j == 0), stop=(j == KC - 1))
        mm.then_inc(ab_ready, 1)
        pe.wait_ge(ab_taken, 1)

        def part(h, j):
            s = j % 2
            pe.wait_ge(w_in[j], (h + 1) * 16)
            pe.wait_ge(z_copied[s], h * COPIED[s] + use(j))
            pe.wait_ge(z_gated[s], h)
            for n, (at, width) in enumerate(SPANS):
                for c in range(KC):
                    mm = pe.matmul(k.bank[3 * s + n][:, 0:width], w[j][:, c, :], aT[:, c, at:at + width],
                                   start=(c == 0), stop=(c == KC - 1))
            mm.then_inc(z_ready[s], 1)

        def aux(h, m):
            pe.wait_ge(norm_taken, h * 6 + min(max(m - 1, 0), 6))
            pe.wait_ge(turn_taken, h * 6 + max(m - 7, 0))
            return k.bank[6 + m % 2]

        def norms(h, n):
            pe.wait_ge(sq_ready, h * 2 + n + 1)
            for s, (at, width) in enumerate(SPANS):
                at += 2 if s else 0
                pe.matmul(aux(h, 3 * n + s)[:, 0:width], ones[:], y[:, at:at + width],
                          start=True, stop=True).then_inc(norm_ready, 1)

        def turns(h, n):
            if n == 0:
                pe.wait_ge(y_ready, h * 2 + 2)
            else:
                pe.wait_ge(silu_ready, h * 3 + 3)
            for g in range(3):
                to = aux(h, 6 + 3 * n + g)
                for q in range(min(4, NT - 4 * g)):
                    t = 4 * g + q
                    at = t * P + (2 if t >= CT else 0)
                    mm = pe.transpose(to[:, q * P:(q + 1) * P], z[:, at:at + P], k.eye[:])
                mm.then_inc(norm_ready, 1)

        with pe.Fori(0, NH) as h:
            part(h, 0)
            part(h, 1)
            norms(h, 0)
            part(h, 2)
            norms(h, 1)
            part(h, 3)
            turns(h, 0)
            part(h, 4)
            turns(h, 1)
            part(h, 5)
            part(h, 6)

    @block.scalar
    def _(act):
        act.wait_ge(ab_ready, 1)
        nc.scalar.copy(k.ab[:].rearrange("p t n -> p (t n)"), k.bank[7][:, 0:NT * 4 * NH]).then_inc(ab_taken, 1)
        act.wait_ge(pads_set, 1)

        def raw(h, j, dst):
            s = j % 2
            act.wait_ge(z_ready[s], h * CNT[s] + use(j) + 1)
            for n, (at, width) in enumerate(SPANS):
                at += 3 if n else 1
                c = nc.scalar.copy(dst[:, at:at + width], k.bank[3 * s + n][:, 0:width])
            c.then_inc(z_copied[s], 1)

        def silu(h, n):
            act.wait_ge(conv_ready, h * 4 + n + 1)
            nc.scalar.activation(z[:, 0:PADTOK - 2], y[:, 0:PADTOK - 2], ACT.Silu).then_inc(silu_ready, 1)

        def square(h, n):
            act.wait_ge(silu_ready, h * 3 + n + 1)
            nc.scalar.activation(y[:, 0:PADTOK - 2], z[:, 0:PADTOK - 2], ACT.Square).then_inc(sq_ready, 1)
            for s, (_, width) in enumerate(SPANS):
                m = 3 * n + s
                act.wait_ge(norm_taken, h * 6 + m + 1)
                nc.scalar.activation(r[:, m % 2, 0:width], r[:, m % 2, 0:width], ACT.Sqrt).then_inc(root_ready, 1)

        def take_turns(h, n):
            act.wait_ge(bt_stored, h * 32 + 16 * n)
            for g in range(3):
                act.wait_ge(norm_ready, h * AUX + 6 + 3 * n + g + 1)
                tiles = min(4, NT - 4 * g)
                nc.scalar.copy(bt[:, 4 * g:4 * g + tiles, :].rearrange("p t n -> p (t n)"),
                               k.bank[6 + g % 2 if n == 0 else 7 - g % 2][:, 0:tiles * P]).then_inc(turn_taken, 1)

        with act.Fori(0, NH) as h:
            raw(h, 0, x)
            act.wait_ge(z_gated[1], h)
            silu(h, 0)
            square(h, 0)
            act.wait_ge(conv_ready, h * 4 + 1)
            raw(h, 1, x)
            act.wait_ge(y_stored, h * 64 + 32)
            silu(h, 1)
            square(h, 1)
            raw(h, 2, x)
            act.wait_ge(z_ready[1], h * CNT[1] + use(3) + 1)
            for m, (at, width) in enumerate(SPANS):
                c = nc.scalar.activation(k.gate[:, ds(h, 1), at:at + width].rearrange("p a n -> p (a n)"),
                                         k.bank[3 + m][:, 0:width], ACT.Silu)
            c.then_inc(z_copied[1], 1)
            take_turns(h, 0)
            act.wait_ge(y_stored, h * 64 + 64)
            silu(h, 2)
            take_turns(h, 1)
            raw(h, 4, z)

    @block.vector
    def _(dve):
        for at in (0, CTX + 1, PADTOK - 1):
            m = nc.vector.memset(x[:, at:at + (2 if at == CTX + 1 else 1)], 0.0)
        m.then_inc(pads_set, 1)
        dve.wait_ge(consts_in, 16 * 7)
        st = Steps(dve, order, 4 * 2 + 2 * 5)
        N = PADTOK - 2

        def conv(h, taps, col):
            c = taps[:, :, ds(h + col, 1)].rearrange("p t a -> p (t a)")
            st.link(nc.vector.tensor_scalar(y[:, 0:N], x[:, 0:N], c[:, 0:1], None, ALU.mult))
            st.link(nc.vector.scalar_tensor_tensor(out=y[:, 0:N], in0=x[:, 1:N + 1], scalar=c[:, 1:2],
                                                   in1=y[:, 0:N], op0=ALU.mult, op1=ALU.add))
            nc.vector.scalar_tensor_tensor(out=y[:, 0:N], in0=x[:, 2:N + 2], scalar=c[:, 2:3],
                                           in1=y[:, 0:N], op0=ALU.mult, op1=ALU.add).then_inc(conv_ready, 1)

        def normalise(h, n, scale):
            for s, (at, width) in enumerate(SPANS):
                at += 2 if s else 0
                m = 3 * n + s
                dve.wait_ge(norm_ready, h * AUX + m + 1)
                nc.vector.tensor_scalar(r[:, m % 2, 0:width], k.bank[6 + m % 2][:, 0:width], EPS, None,
                                        ALU.add).then_inc(norm_taken, 1)
                dve.wait_ge(root_ready, h * 6 + m + 1)
                st.link(nc.vector.reciprocal(r[:, m % 2, 0:width], r[:, m % 2, 0:width]))
                c = nc.vector.scalar_tensor_tensor(out=z[:, at:at + width], in0=z[:, at:at + width],
                                                   scalar=scale, in1=r[:, m % 2, 0:width], op0=ALU.mult, op1=ALU.mult)
                if s < 2:
                    st.link(c)
            c.then_inc(y_ready, 1)

        with dve.Fori(0, NH) as h:
            st.at(h)
            dve.wait_ge(z_copied[0], h * 3 + 1)
            conv(h, cq, 0)
            normalise(h, 0, P ** -0.5)
            dve.wait_ge(z_copied[1], h * 2 + 1)
            conv(h, cq, NH)
            normalise(h, 1, 1.0)
            dve.wait_ge(z_copied[0], h * 3 + 2)
            conv(h, cq, 2 * NH)
            dve.wait_ge(z_copied[0], h * 3 + 3)
            dve.wait_ge(z_ready[1], h * CNT[1] + 3)
            for n, (at, width) in enumerate(SPANS):
                at += 3 if n else 1
                c = nc.vector.tensor_tensor(x[:, at:at + width], z[:, at:at + width],
                                            k.bank[3 + n][:, 0:width], ALU.mult)
            c.then_inc(z_gated[1], 1)
            dve.wait_ge(z_gated[1], h + 1)
            dve.wait_ge(silu_ready, h * 3 + 3)
            conv(h, csc, 0)
            dve.wait_ge(conv_ready, h * 4 + 4)
            dve.wait_ge(z_ready[0], h * CNT[0] + 4)
            for n, (at, width) in enumerate(SPANS):
                c = nc.vector.tensor_tensor(k.short[:, ds(h, 1), at:at + width].rearrange("p a n -> p (a n)"),
                                            y[:, at + (2 if n else 0):at + (2 if n else 0) + width],
                                            k.bank[n][:, 0:width], ALU.mult)
            c.then_inc(z_gated[0], 1)
            st.end()


def delta_scan(k, oT):
    nc, dr = k.nc, k.dram
    R2 = range(2)
    merge = k.sb("merge", [P, 2, LEVELS, P])
    ones = k.sb("ones", [P, P])
    alog = k.sb("a_log", [P, 2 * NH])
    dtb = k.sb("dt_bias", [P, 2 * NH])
    ST = [P, NT, 2 * NH]
    la, beta, g, tot = k.sb("log_a", ST), k.sb("beta", ST), k.sb("g", ST), k.sb("g_total", ST)
    beg, kdec, egl, tmp = k.sb("beta_eg", ST), k.sb("k_decay", ST), k.sb("eg_total", ST), k.sb("tmp", ST)

    def per_dir(name):
        return [k.sb(f"{name}{d}", [P, NH, P]) for d in R2]

    KT, QT, K, V = per_dir("KT"), per_dir("QT"), per_dir("K"), per_dir("V")
    GU, BI, Dc, EG = per_dir("g_rows_in"), per_dir("b_rows_in"), per_dir("decay"), per_dir("eg_rows")
    Dm, DB, AT, KQ = per_dir("decay_masked"), per_dir("decay_beta"), per_dir("AT"), per_dir("KQ")
    T, TT, Pm, QTd = per_dir("T"), per_dir("TT"), per_dir("A_T_off"), per_dir("QT_decayed")
    VB, R, VN, VD, S = per_dir("V_beta"), per_dir("R"), per_dir("v_new"), per_dir("v_decayed"), per_dir("S")

    consts_in, ones_set, state_set, stats = k.sem("consts_in"), k.sem("ones_set"), k.sem("state_set"), k.sem("stats")
    prep_act, prep_pe, prep_order = k.sem("prep_act"), k.sem("prep_pe"), k.sem("prep_order")

    def sems(name):
        return [k.sem(f"{name}{d}") for d in R2]

    tile_in, rows_in = sems("tile_in"), sems("rows_in")
    g_rows, kk_ready, a_turned, p_ready, dt_ready = (sems(n) for n in ("g_rows", "kk_ready", "a_turned", "p_ready", "dt_ready"))
    ks_ready, vn_ready, o_ready, ds_ready = (sems(n) for n in ("ks_ready", "vn_ready", "o_ready", "ds_ready"))
    e_ready, at_ready, kq_ready, t_ready, pm_ready = (sems(n) for n in ("e_ready", "at_ready", "kq_ready", "t_ready", "pm_ready"))
    tt_ready, r_ready, vd_ready, o_added, s_ready = (sems(n) for n in ("tt_ready", "r_ready", "vd_ready", "o_added", "s_ready"))
    eg_ready, d_ready, vn_copied = (sems(n) for n in ("eg_ready", "d_ready", "vn_copied"))
    dm_ready, qtd_ready, vb_ready, tt0_ready, s_scaled = (sems(n) for n in ("dm_ready", "qtd_ready", "vb_ready", "tt0_ready", "s_scaled"))
    order, pool_order = k.sem("dve_order"), k.sem("pool_order")
    MERGES = LEVELS - 1
    bank = [[k.bank[4 * d + n][:].rearrange("p (h n) -> p h n", h=NH) for n in range(4)] for d in R2]
    flat = [[k.bank[4 * d + n] for n in range(4)] for d in R2]
    block = k.block()

    def passes(eng, body):
        with eng.Fori(0, CT) as s:
            body(s, (s, eng.snap(s * -1 + (CT - 1), min_val=0, max_val=CT - 1)))
        with eng.Fori(CT, NT) as s:
            body(s, (s, eng.snap(s * -1 + (NT + CT - 1), min_val=CT, max_val=NT - 1)))

    def stat(x, t, d):
        return (x[:, ds(t, 1), NH * d:NH * d + NH].rearrange("p a h -> p (a h)").unsqueeze(2)
                .to_broadcast([P, NH, P]))

    def all_heads(x):
        return x.unsqueeze(1).to_broadcast([P, NH, P])

    @block.sync
    def _(sp):
        sp.dma_start(merge[:], dr["const_merge"].rearrange("d l p n -> p d l n")).then_inc(consts_in, 16)
        sp.dma_start(alog[:], dr["ab_a_log"].rearrange("a d h -> a (d h)").to_broadcast([P, 2 * NH])).then_inc(consts_in, 16)
        sp.dma_start(dtb[:], dr["ab_dt_bias"].rearrange("a d h -> a (d h)").to_broadcast([P, 2 * NH])).then_inc(consts_in, 16)

        def body(s, tiles):
            for d in R2:
                sp.wait_ge(ds_ready[d], s)
                sp.wait_ge(qtd_ready[d], s)
                sp.wait_ge(vb_ready[d], s)
                for part, dst in enumerate((QT, KT, K, V)):
                    sp.dma_start(dst[d][:].rearrange("p h n -> p (h n)"),
                                 dr["heads"][part, ds(tiles[d], 1)].rearrange("a p n -> p (a n)")).then_inc(tile_in[d], 16)
        passes(sp, body)

    @block.gpsimd
    def _(pool):
        nc.gpsimd.memset(ones[:], 1.0).then_inc(ones_set, 1)
        nc.gpsimd.memset(oT[:], 0.0).then_inc(state_set, 1)
        for d in R2:
            nc.gpsimd.memset(S[d][:], 0.0).then_inc(state_set, 1)
        pool.wait_ge(stats, 1)

        def body(s, tiles):
            for d in R2:
                pool.wait_ge(g_rows[d], s)
                nc.gpsimd.tensor_tensor(GU[d][:], all_heads(k.tri[:, d, :]), stat(la, tiles[d], d), ALU.mult).then_inc(rows_in[d], 1)
                nc.gpsimd.tensor_tensor(BI[d][:], all_heads(k.eye[:]), stat(beta, tiles[d], d), ALU.mult).then_inc(rows_in[d], 1)
            for d in R2:
                pool.wait_ge(d_ready[d], s + 1)
                pool.wait_ge(kq_ready[d], s)
                nc.gpsimd.tensor_tensor(Dm[d][:], Dc[d][:], all_heads(k.tri[:, d, :]), ALU.mult).then_inc(dm_ready[d], 1)
            for d in R2:
                pool.wait_ge(at_ready[d], s + 1)
                pool.wait_ge(vn_ready[d], s)
                nc.gpsimd.tensor_tensor(TT[d][:], AT[d][:], all_heads(merge[:, 1 - d, 0, :]), ALU.mult).then_inc(pool_order, 1)
                pool.wait_ge(pool_order, s * 2 + d + 1)
                nc.gpsimd.tensor_tensor(TT[d][:], all_heads(k.eye[:]), TT[d][:], ALU.subtract).then_inc(tt0_ready[d], 1)
            for d in R2:
                pool.wait_ge(tile_in[d], (s + 1) * 64)
                pool.wait_ge(eg_ready[d], s + 1)
                pool.wait_ge(r_ready[d], s)
                pool.wait_ge(o_ready[d], s)
                nc.gpsimd.tensor_tensor(QTd[d][:], QT[d][:], EG[d][:], ALU.mult).then_inc(qtd_ready[d], 1)
                nc.gpsimd.tensor_tensor(VB[d][:], V[d][:], stat(beta, tiles[d], d), ALU.mult).then_inc(vb_ready[d], 1)
            for d in R2:
                pool.wait_ge(o_ready[d], s + 1)
                nc.gpsimd.tensor_tensor(S[d][:], S[d][:], stat(egl, tiles[d], d), ALU.mult).then_inc(s_scaled[d], 1)
        passes(pool, body)

    @block.scalar
    def _(act):
        act.wait_ge(prep_order, 1)
        nc.scalar.activation(tmp[:], la[:], ACT.Abs).then_inc(prep_act, 1)
        act.wait_ge(prep_act, 1)
        nc.scalar.activation(tmp[:], tmp[:], ACT.Exp, scale=-1.0).then_inc(prep_act, 1)
        act.wait_ge(prep_act, 2)
        nc.scalar.activation(tmp[:], tmp[:], ACT.Ln, bias=1.0).then_inc(prep_act, 1)
        nc.scalar.activation(beta[:], k.ab[:, :, 2 * NH:], ACT.Sigmoid).then_inc(prep_act, 1)
        act.wait_ge(consts_in, 48)
        nc.scalar.activation(alog[:], alog[:], ACT.Exp).then_inc(prep_act, 1)
        act.wait_ge(prep_order, 6)
        nc.scalar.activation(kdec[:], kdec[:], ACT.Exp).then_inc(prep_act, 1)
        nc.scalar.activation(egl[:], tot[:], ACT.Exp).then_inc(prep_act, 1)
        nc.scalar.activation(tmp[:], g[:], ACT.Exp).then_inc(prep_act, 1)

        def body(s, tiles):
            for d in R2:
                act.wait_ge(g_rows[d], s + 1)
                act.wait_ge(qtd_ready[d], s)
                nc.scalar.activation(EG[d][:], bank[d][0], ACT.Exp).then_inc(eg_ready[d], 1)
            for d in R2:
                act.wait_ge(e_ready[d], s + 1)
                nc.scalar.activation(Dc[d][:], Dc[d][:], ACT.Exp).then_inc(d_ready[d], 1)
            for d in R2:
                act.wait_ge(vn_ready[d], s + 1)
                act.wait_ge(o_ready[d], s)
                nc.scalar.copy(VN[d][:], bank[d][1]).then_inc(vn_copied[d], 1)
        passes(act, body)

    @block.vector
    def _(dve):
        dve.wait_ge(consts_in, 48)
        prep = Steps(dve, prep_order)
        bias = dtb[:].unsqueeze(1).to_broadcast(ST)
        prep.link(nc.vector.tensor_tensor(la[:], k.ab[:, :, 0:2 * NH], bias, ALU.add))
        dve.wait_ge(prep_act, 3)
        prep.link(nc.vector.scalar_tensor_tensor(out=la[:], in0=la[:], scalar=0.0, in1=tmp[:], op0=ALU.max, op1=ALU.add))
        dve.wait_ge(prep_act, 5)
        prep.link(nc.vector.scalar_tensor_tensor(out=la[:], in0=la[:], scalar=-1.0,
                                                 in1=alog[:].unsqueeze(1).to_broadcast(ST), op0=ALU.mult, op1=ALU.mult))
        dve.wait_ge(prep_pe, 1)
        for d in R2:
            prep_copy = nc.vector.tensor_copy(g[:, :, NH * d:NH * d + NH],
                                              flat[0][d][:, 0:NT * NH].rearrange("p (t h) -> p t h", t=NT))
            if d == 1:
                prep.link(prep_copy)
        prep.link(nc.vector.tensor_copy(tot[:], flat[0][2][:, 0:2 * NT * NH].rearrange("p (t h) -> p t h", t=NT)))
        prep.link(nc.vector.tensor_tensor(kdec[:], tot[:], g[:], ALU.subtract))
        dve.wait_ge(prep_act, 8)
        prep.link(nc.vector.tensor_tensor(beg[:], tmp[:], beta[:], ALU.mult))
        dve.sem_inc(stats, 1)
        dve.wait_ge(state_set, 3)
        st = Steps(dve, order, 2 * (1 + 1 + 1 + 1))

        def body(s, tiles):
            st.at(s)
            for d in R2:
                dve.wait_ge(eg_ready[d], s + 1)
                dve.wait_ge(dm_ready[d], s)
                st.link(nc.vector.tensor_tensor(Dc[d][:], bank[d][0], stat(g, tiles[d], d), ALU.subtract))
                nc.vector.tensor_scalar(Dc[d][:], Dc[d][:], 0.0, None, ALU.min).then_inc(e_ready[d], 1)
            for d in R2:
                dve.wait_ge(d_ready[d], s + 1)
                st.link(nc.vector.tensor_tensor(DB[d][:], Dc[d][:], bank[d][1], ALU.mult))
                dve.wait_ge(kk_ready[d], s + 1)
                nc.vector.tensor_tensor(AT[d][:], DB[d][:], bank[d][2], ALU.mult).then_inc(at_ready[d], 1)
                dve.wait_ge(dm_ready[d], s + 1)
                nc.vector.tensor_tensor(KQ[d][:], Dm[d][:], bank[d][3], ALU.mult).then_inc(kq_ready[d], 1)
            for d in R2:
                dve.wait_ge(a_turned[d], s + 1)
                st.link(nc.vector.tensor_tensor(T[d][:], bank[d][0], all_heads(merge[:, d, 0, :]), ALU.mult))
                nc.vector.tensor_tensor(T[d][:], all_heads(k.eye[:]), T[d][:], ALU.subtract).then_inc(t_ready[d], 1)
            for n in range(MERGES):
                for d in R2:
                    dve.wait_ge(p_ready[d], s * MERGES + n + 1)
                    nc.vector.tensor_tensor(Pm[d][:], bank[d][1], all_heads(merge[:, d, n + 1, :]),
                                            ALU.mult).then_inc(pm_ready[d], 1)
                for d in R2:
                    dve.wait_ge(dt_ready[d], s * MERGES + n + 1)
                    if n == 0:
                        dve.wait_ge(tt0_ready[d], s + 1)
                        dve.wait_ge(t_ready[d], s + 1)
                    else:
                        dve.wait_ge(tt_ready[d], s * MERGES + n)
                    if n < MERGES - 1:
                        nc.vector.tensor_tensor(T[d][:], T[d][:], bank[d][2], ALU.subtract)
                    nc.vector.tensor_tensor(TT[d][:], TT[d][:], bank[d][3], ALU.subtract).then_inc(tt_ready[d], 1)
            for d in R2:
                dve.wait_ge(ks_ready[d], s + 1)
                st.link(nc.vector.tensor_tensor(R[d][:], bank[d][0], stat(beg, tiles[d], d), ALU.mult))
                dve.wait_ge(vb_ready[d], s + 1)
                nc.vector.tensor_tensor(R[d][:], VB[d][:], R[d][:], ALU.subtract).then_inc(r_ready[d], 1)
            for d in R2:
                dve.wait_ge(vn_copied[d], s + 1)
                nc.vector.tensor_tensor(VD[d][:], bank[d][1], stat(kdec, tiles[d], d), ALU.mult).then_inc(vd_ready[d], 1)
            for d in R2:
                o = oT[:, :, ds(tiles[d] * P, P)]
                dve.wait_ge(o_ready[d], s + 1)
                dve.wait_ge(o_added[1 - d], s + d)
                nc.vector.tensor_tensor(o, o, bank[d][2], ALU.add).then_inc(o_added[d], 1)
                dve.wait_ge(ds_ready[d], s + 1)
                dve.wait_ge(s_scaled[d], s + 1)
                nc.vector.tensor_tensor(S[d][:], S[d][:], bank[d][3], ALU.add).then_inc(s_ready[d], 1)
            st.end()
        passes(dve, body)

    @block.tensor
    def _(pe):
        pe.wait_ge(ones_set, 1)
        pe.wait_ge(prep_order, 3)
        for d in R2:
            pe.matmul(flat[0][d][:, 0:NT * NH], k.tri[:, d, :], la[:, :, NH * d:NH * d + NH], start=True, stop=True)
        pe.matmul(flat[0][2][:, 0:2 * NT * NH], ones[:], la[:].rearrange("p t h -> p (t h)"),
                  start=True, stop=True).then_inc(prep_pe, 1)
        pe.wait_ge(stats, 1)
        pe.wait_ge(state_set, 3)

        def heads(to, lhs, rhs, start=True, stop=True):
            for h in range(NH):
                mm = pe.matmul(to[:, h, :], lhs[:, h, :], rhs[:, h, :], start=start, stop=stop)
            return mm

        def body(s, tiles):
            for d in R2:
                pe.wait_ge(rows_in[d], 2 * s + 2)
                pe.wait_ge(r_ready[d], s)
                pe.wait_ge(vd_ready[d], s)
                pe.wait_ge(vn_copied[d], s)
                pe.matmul(flat[d][0][:], ones[:], GU[d][:].rearrange("p h n -> p (h n)"), start=True, stop=True)
                pe.matmul(flat[d][1][:], ones[:], BI[d][:].rearrange("p h n -> p (h n)"), start=True,
                          stop=True).then_inc(g_rows[d], 1)
            for d in R2:
                pe.wait_ge(tile_in[d], (s + 1) * 64)
                pe.wait_ge(o_added[d], s)
                pe.wait_ge(s_ready[d], s)
                heads(bank[d][2], KT[d], KT[d])
                heads(bank[d][3], KT[d], QT[d]).then_inc(kk_ready[d], 1)
            for d in R2:
                pe.wait_ge(at_ready[d], s + 1)
                pe.wait_ge(eg_ready[d], s + 1)
                for h in range(NH):
                    mm = pe.transpose(bank[d][0][:, h, :], AT[d][:, h, :], k.eye[:])
                mm.then_inc(a_turned[d], 1)
            for n in range(MERGES):
                for d in R2:
                    if n == 0:
                        pe.wait_ge(t_ready[d], s + 1)
                    else:
                        pe.wait_ge(tt_ready[d], s * MERGES + n)
                    heads(bank[d][1], AT[d], T[d]).then_inc(p_ready[d], 1)
                for d in R2:
                    pe.wait_ge(pm_ready[d], s * MERGES + n + 1)
                    if n == 0:
                        pe.wait_ge(tt0_ready[d], s + 1)
                        pe.wait_ge(kq_ready[d], s + 1)
                    if n < MERGES - 1:
                        heads(bank[d][2], TT[d], Pm[d])
                    heads(bank[d][3], Pm[d], TT[d]).then_inc(dt_ready[d], 1)
            for d in R2:
                pe.wait_ge(s_ready[d], s)
                heads(bank[d][0], KT[d], S[d]).then_inc(ks_ready[d], 1)
            for d in R2:
                pe.wait_ge(r_ready[d], s + 1)
                pe.wait_ge(tt_ready[d], (s + 1) * MERGES)
                heads(bank[d][1], TT[d], R[d]).then_inc(vn_ready[d], 1)
            for d in R2:
                pe.wait_ge(vn_copied[d], s + 1)
                pe.wait_ge(qtd_ready[d], s + 1)
                for h in range(NH):
                    pe.matmul(bank[d][2][:, h, :], S[d][:, h, :], QTd[d][:, h, :], start=True, stop=False)
                    mm = pe.matmul(bank[d][2][:, h, :], VN[d][:, h, :], KQ[d][:, h, :], start=False, stop=True)
                mm.then_inc(o_ready[d], 1)
            for d in R2:
                pe.wait_ge(vd_ready[d], s + 1)
                heads(bank[d][3], K[d], VD[d]).then_inc(ds_ready[d], 1)
        passes(pe, body)


def gate_heads(k, oT):
    nc, dr = k.nc, k.dram
    ones, wn = k.sb("ones", [P, P]), k.sb("out_norm", [P, 1])
    sq, r = k.sb("squares", [P, 3, 512]), k.sb("rstd", [P, 3, 512])
    w_in, ones_set, sq_ready, sum_ready = k.sem("w_in"), k.sem("ones_set"), k.sem("sq_ready"), k.sem("sum_ready")
    mean_ready, root_ready, gated, order = k.sem("mean_ready"), k.sem("root_ready"), k.sem("gated"), k.sem("dve_order")
    block = k.block()

    def span(x, h, at, width):
        return x[:, ds(h, 1), at:at + width].rearrange("p a n -> p (a n)")

    @block.sync
    def _(sp):
        sp.dma_start(wn[:], dr["ab_out_norm"].rearrange("a p -> p a")).then_inc(w_in, 16)

    @block.gpsimd
    def _(pool):
        nc.gpsimd.memset(ones[:], 1.0).then_inc(ones_set, 1)

    @block.scalar
    def _(act):
        with act.Fori(0, NH) as h:
            for n, (at, width) in enumerate(SPANS):
                act.wait_ge(sum_ready, h * 3)
                nc.scalar.activation(sq[:, n, 0:width], span(oT, h, at, width), ACT.Square).then_inc(sq_ready, 1)
            for n, (at, width) in enumerate(SPANS):
                act.wait_ge(mean_ready, h * 3 + n + 1)
                nc.scalar.activation(r[:, n, 0:width], r[:, n, 0:width], ACT.Sqrt).then_inc(root_ready, 1)

    @block.tensor
    def _(pe):
        pe.wait_ge(ones_set, 1)
        with pe.Fori(0, NH) as h:
            for n, (at, width) in enumerate(SPANS):
                pe.wait_ge(sq_ready, h * 3 + n + 1)
                pe.wait_ge(mean_ready, h * 3)
                pe.matmul(k.bank[n][:, 0:width], ones[:], sq[:, n, 0:width], start=True, stop=True).then_inc(sum_ready, 1)

    @block.vector
    def _(dve):
        dve.wait_ge(w_in, 16)
        st = Steps(dve, order, 6)
        with dve.Fori(0, NH) as h:
            st.at(h)
            for n, (at, width) in enumerate(SPANS):
                dve.wait_ge(sum_ready, h * 3 + n + 1)
                dve.wait_ge(gated, h * 3)
                nc.vector.tensor_scalar(r[:, n, 0:width], k.bank[n][:, 0:width], 1.0 / P, EPS, ALU.mult,
                                        ALU.add).then_inc(mean_ready, 1)
            for n, (at, width) in enumerate(SPANS):
                dve.wait_ge(root_ready, h * 3 + n + 1)
                st.link(nc.vector.reciprocal(r[:, n, 0:width], r[:, n, 0:width]))
                o = span(oT, h, at, width)
                st.link(nc.vector.scalar_tensor_tensor(out=o, in0=o, scalar=wn[:], in1=r[:, n, 0:width],
                                                       op0=ALU.mult, op1=ALU.mult))
                nc.vector.tensor_tensor(o, o, span(k.gate, h, at, width), ALU.mult).then_inc(gated, 1)
            st.end()


def project_out(k, l, first, lhs, w_name):
    nc, dr = k.nc, k.dram
    w, g = k.sb("w_out", [P, KC, D]), k.sb("gate_rows", [P, 2, D])
    y = k.sb("y", [P, 2, D])
    w_in, g_in, y_ready, y_scaled, h_added = k.sem("w_in"), k.sem("g_in"), k.sem("y_ready"), k.sem("y_scaled"), k.sem("h_added")
    block = k.block()
    tiles = range(first, NT)

    @block.sync
    def _(sp):
        for half in range(2):
            sp.dma_start(w[:, :, half * 512:(half + 1) * 512],
                         dr[w_name][0, :, half * 512:(half + 1) * 512].rearrange("(j p) n -> p j n", p=P)).then_inc(w_in, 16)
        for v in range(2):
            spread_row(k, sp, g[:, v, :], l, v, 2, g_in)

    @block.tensor
    def _(pe):
        pe.wait_ge(w_in, 32)
        for n, t in enumerate(tiles):
            if n >= 2:
                pe.wait_ge(y_scaled, 2 * n - 2)
            for half in range(2):
                for c in range(KC):
                    mm = pe.matmul(k.bank[2 * (n % 2) + half][:], lhs(c, t), w[:, c, half * 512:(half + 1) * 512],
                                   start=(c == 0), stop=(c == KC - 1))
                mm.then_inc(y_ready, 1)

    @block.vector
    def _(dve):
        dve.wait_ge(g_in, 32)
        for n, t in enumerate(tiles):
            if n >= 2:
                dve.wait_ge(h_added, n - 1)
            for half in range(2):
                dve.wait_ge(y_ready, 2 * n + half + 1)
                nc.vector.tensor_tensor(y[:, n % 2, half * 512:(half + 1) * 512], k.bank[2 * (n % 2) + half][:],
                                        g[:, 0 if t < CT else 1, half * 512:(half + 1) * 512],
                                        ALU.mult).then_inc(y_scaled, 1)

    @block.gpsimd
    def _(pool):
        for n, t in enumerate(tiles):
            pool.wait_ge(y_scaled, 2 * n + 2)
            nc.gpsimd.tensor_tensor(k.H[:, t, :], k.H[:, t, :], y[:, n % 2, :], ALU.add).then_inc(h_added, 1)


class Table:
    BLOCKS, LAST, ACTIVE = 0, 1, 2
    EXPERT = 3
    BLOCKS_UPTO = EXPERT + NE
    OF_BLOCK = BLOCKS_UPTO + NE
    PER = 2 + RING
    SIZE = OF_BLOCK + PER * (MAXP + 1)


def route(k, first, logits, slots, wts, table):
    nc, dr = k.nc, k.dram
    T = NT - first
    ramp = k.sb("ramp", [P, P])
    late = k.sb("ramp_plus_128", [P, P])
    ones, strict = k.sb("ones", [P, P]), k.sb("strict", [P, P])
    gmax, gi, gsum = k.sb("gmax", [P, T]), k.sb("gi", [P, T]), k.sb("gsum", [P, T])
    gx, gc, gh = k.sb("g_shifted", [P, T, GROUPS]), k.sb("g_cand", [P, T, GROUPS]), k.sb("g_hot", [P, T, GROUPS])
    ex = k.sb("in_group", [P, T, PER])
    big = k.sb("big", [P, T, GROUPS, PER])
    em, ei, ec = k.sb("e_max", [P, 2, T]), k.sb("e_index", [P, T]), k.sb("e_cand", [P, T, PER])
    eh = k.sb("e_hot", [P, 2, T, PER])
    hot = k.sb("hot", [P, 2, T, NE])
    cnt, pos, run = k.sb("chosen", [P, T, NE]), k.sb("position", [P, T, NE]), k.sb("running", [P, NE])
    MOST = TOK // UNIT
    U = 2 * (MAXP + 1)
    units, incl, excl = k.sb("units", [P, NE]), k.sb("units_upto", [P, NE]), k.sb("units_before", [P, NE])
    over, thresholds = k.sb("over", [P, NE, MOST]), k.sb("thresholds", [P, MOST])
    active, rank_upto, rank = k.sb("active", [P, NE]), k.sb("active_upto", [P, NE]), k.sb("active_before", [P, NE])
    far, last = k.sb("units_upto_if_active", [P, NE]), k.sb("last_rank", [P, 1])
    cmp, owner = k.sb("compare", [P, U, NE]), k.sb("owner_rank", [P, U])
    triple, rounds = k.sb("multiples_of_ring", [P, NE // RING + 1]), k.sb("rounds", [P, RING, U])
    last_unit, thresholds2 = k.sb("units_upto_rank", [P, NE]), k.sb("even_numbers", [P, MAXP])
    blocks_of = k.sb("blocks_of", [P, NE, MAXP])
    ratio, inv = k.sb("ratio", [P, T]), k.sb("inv", [P, T])
    sf, tf = k.sb("slots_f32", [P, 2, T]), k.sb("table_f32", [P, Table.SIZE])
    tok, zero = k.sb("token", [P, T], I32), k.sb("no_token", [P, MAXP + 1], I32)
    c_in, order, exps, counted, tokens = k.sem("c_in"), k.sem("order"), k.sem("exps"), k.sem("counted"), k.sem("tokens")
    shifted, ratio_set, hot_ready = k.sem("shifted"), k.sem("ratio_set"), k.sem("hot_ready")
    cleared, slots_ready, scattered, consts = k.sem("cleared"), k.sem("slots_ready"), k.sem("scattered"), k.sem("consts")
    block = k.block()

    @block.sync
    def _(sp):
        sp.dma_start(ramp[:], dr["const_ramp"].to_broadcast([P, P])).then_inc(c_in, 16)

    @block.gpsimd
    def _(pool):
        nc.gpsimd.memset(ones[:], 1.0).then_inc(consts, 1)
        nc.gpsimd.tensor_tensor(strict[:], k.tri[:, 0, :], k.eye[:], ALU.subtract).then_inc(consts, 1)
        nc.gpsimd.iota(tok[:], [[P, T]], base=first * P, channel_multiplier=1).then_inc(tokens, 1)
        nc.gpsimd.memset(zero[:], first * P).then_inc(tokens, 1)
        pool.wait_ge(tokens, 2)
        pool.dma_start(dr["slot_token"].rearrange("(p b) a -> p (b a)", p=P), zero[:]).then_inc(cleared, 16)
        pool.wait_ge(cleared, 16)
        pool.wait_ge(slots_ready, 1)
        for t in range(T):
            for c in range(2):
                pool.indirect_dma_start(dr["slot_token"], bass.IndirectOffsetOnAxis(ap=slots[:, c, t:t + 1], axis=0),
                                        tok[:, t:t + 1], None).then_inc(scattered, 16)
        pool.wait_ge(scattered, 32 * T)

    @block.scalar
    def _(act):
        act.wait_ge(shifted, 1)
        nc.scalar.activation(gx[:], gx[:], ACT.Exp).then_inc(exps, 1)
        act.wait_ge(ratio_set, 1)
        nc.scalar.activation(ratio[:], ratio[:], ACT.Exp).then_inc(exps, 1)

    @block.tensor
    def _(pe):
        pe.wait_ge(consts, 2)
        pe.wait_ge(hot_ready, 1)
        flat = cnt[:].rearrange("p t e -> p (t e)")
        pe.matmul(k.bank[0][:, 0:T * NE], strict[:], flat, start=True, stop=True)
        pe.matmul(k.bank[1][:, 0:T * NE], ones[:], flat, start=True, stop=True).then_inc(counted, 1)

    @block.vector
    def _(dve):
        V = nc.vector
        st = Steps(dve, order)
        G, E = logits[:, :, 0:GROUPS], logits[:, :, GROUPS:].rearrange("p t (g e) -> p t g e", g=GROUPS)

        def cols(x, n):
            return x.unsqueeze(2).to_broadcast([P, T, n])

        def rows(x, n):
            return x[:, 0:n].unsqueeze(1).to_broadcast([P, T, n])

        def first_of(values, best, cand, index, is_it, n):
            st.link(V.tensor_tensor(cand, values, cols(best, n), ALU.is_equal))
            st.link(V.scalar_tensor_tensor(out=cand, in0=cand, scalar=-float(P), in1=rows(late, n), op0=ALU.mult, op1=ALU.add))
            st.link(V.tensor_reduce(index, cand, AX.X, ALU.min))
            st.link(V.tensor_tensor(is_it, rows(ramp, n), cols(index, n), ALU.is_equal))

        dve.wait_ge(c_in, 16)
        st.link(V.tensor_scalar(late[:], ramp[:], float(P), None, ALU.add))
        st.link(V.tensor_reduce(gmax[:], G, AX.X, ALU.max))
        st.link(V.tensor_tensor(gx[:], G, cols(gmax[:], GROUPS), ALU.subtract))
        dve.sem_inc(shifted, 1)
        first_of(G, gmax[:], gc[:], gi[:], gh[:], GROUPS)
        st.link(V.tensor_tensor(big[:], E, gh[:].unsqueeze(3).to_broadcast([P, T, GROUPS, PER]), ALU.mult))
        st.link(V.tensor_reduce(ex[:], big[:].rearrange("p t g e -> p t e g"), AX.X, ALU.add))
        for c in range(2):
            if c:
                st.link(V.scalar_tensor_tensor(out=ex[:], in0=eh[:, 0], scalar=-1e30, in1=ex[:], op0=ALU.mult, op1=ALU.add))
            st.link(V.tensor_reduce(em[:, c], ex[:], AX.X, ALU.max))
            if c:
                st.link(V.tensor_tensor(ratio[:], em[:, 1], em[:, 0], ALU.subtract))
                dve.sem_inc(ratio_set, 1)
            first_of(ex[:], em[:, c], ec[:], ei[:], eh[:, c], PER)
        for c in range(2):
            st.link(V.tensor_tensor(hot[:, c].rearrange("p t (g e) -> p t g e", g=GROUPS),
                                    gh[:].unsqueeze(3).to_broadcast([P, T, GROUPS, PER]),
                                    eh[:, c].unsqueeze(2).to_broadcast([P, T, GROUPS, PER]), ALU.mult))
        st.link(V.tensor_tensor(cnt[:], hot[:, 0], hot[:, 1], ALU.add))
        dve.sem_inc(hot_ready, 1)

        dve.wait_ge(exps, 2)
        st.link(V.tensor_reduce(gsum[:], gx[:], AX.X, ALU.add))
        st.link(V.reciprocal(gsum[:], gsum[:]))
        st.link(V.tensor_scalar(inv[:], ratio[:], 1.0, None, ALU.add))
        st.link(V.reciprocal(inv[:], inv[:]))
        st.link(V.tensor_tensor(wts[:, 0], gsum[:], inv[:], ALU.mult))
        st.link(V.tensor_tensor(wts[:, 1], wts[:, 0], ratio[:], ALU.mult))

        dve.wait_ge(counted, 1)
        st.link(V.memset(run[:], 0.0))
        for t in range(T):
            st.link(V.tensor_tensor(pos[:, t], k.bank[0][:, t * NE:(t + 1) * NE], run[:], ALU.add))
            st.link(V.tensor_tensor(run[:], run[:], k.bank[1][:, t * NE:(t + 1) * NE], ALU.add))
        st.link(V.tensor_scalar(thresholds[:], ramp[:, 0:MOST], float(UNIT), None, ALU.mult))
        st.link(V.tensor_tensor(over[:], run[:].unsqueeze(2).to_broadcast([P, NE, MOST]),
                                thresholds[:].unsqueeze(1).to_broadcast([P, NE, MOST]), ALU.is_gt))
        st.link(V.tensor_reduce(units[:], over[:], AX.X, ALU.add))
        st.link(V.tensor_tensor_scan(incl[:], ones[:, 0:NE], units[:], 0.0, ALU.mult, ALU.add))
        st.link(V.tensor_tensor(excl[:], incl[:], units[:], ALU.subtract))
        st.link(V.tensor_scalar(excl[:], excl[:], float(UNIT), None, ALU.mult))
        st.link(V.tensor_tensor(pos[:], pos[:], excl[:].unsqueeze(1).to_broadcast([P, T, NE]), ALU.add))
        b = big[:].rearrange("p t g e -> p t (g e)")
        for c in range(2):
            st.link(V.tensor_tensor(b, hot[:, c], pos[:], ALU.mult))
            st.link(V.tensor_reduce(sf[:, c], b, AX.X, ALU.add))
        V.tensor_copy(slots[:].rearrange("p c t -> p (c t)"), sf[:].rearrange("p c t -> p (c t)")).then_inc(slots_ready, 1)

        st.link(V.tensor_scalar(active[:], units[:], 1.0, None, ALU.min))
        st.link(V.tensor_tensor_scan(rank_upto[:], ones[:, 0:NE], active[:], 0.0, ALU.mult, ALU.add))
        st.link(V.tensor_tensor(rank[:], rank_upto[:], active[:], ALU.subtract))
        R = slice(0, NE)
        by_rank = ramp[:, R].unsqueeze(2).to_broadcast([P, NE, NE])
        st.link(V.tensor_tensor(cmp[:, R], rank_upto[:].unsqueeze(1).to_broadcast([P, NE, NE]), by_rank, ALU.is_le))
        st.link(V.tensor_reduce(tf[:, Table.EXPERT:Table.EXPERT + NE], cmp[:, R], AX.X, ALU.add))
        st.link(V.tensor_scalar(tf[:, Table.EXPERT:Table.EXPERT + NE], tf[:, Table.EXPERT:Table.EXPERT + NE],
                                float(NE - 1), None, ALU.min))
        st.link(V.tensor_tensor(cmp[:, R], rank[:].unsqueeze(1).to_broadcast([P, NE, NE]), by_rank, ALU.is_le))
        st.link(V.tensor_tensor(cmp[:, R], cmp[:, R], units[:].unsqueeze(1).to_broadcast([P, NE, NE]), ALU.mult))
        st.link(V.tensor_reduce(last_unit[:], cmp[:, R], AX.X, ALU.add))
        st.link(V.tensor_scalar(thresholds2[:], ramp[:, 0:MAXP], 2.0, None, ALU.mult))
        st.link(V.tensor_tensor(blocks_of[:], last_unit[:].unsqueeze(2).to_broadcast([P, NE, MAXP]),
                                thresholds2[:].unsqueeze(1).to_broadcast([P, NE, MAXP]), ALU.is_gt))
        st.link(V.tensor_reduce(tf[:, Table.BLOCKS_UPTO:Table.BLOCKS_UPTO + NE], blocks_of[:], AX.X, ALU.add))
        st.link(V.tensor_copy(tf[:, Table.BLOCKS:Table.BLOCKS + 1], tf[:, Table.BLOCKS_UPTO + NE - 1:Table.BLOCKS_UPTO + NE]))
        st.link(V.tensor_scalar(tf[:, Table.LAST:Table.LAST + 1], tf[:, Table.BLOCKS:Table.BLOCKS + 1], -1.0, None, ALU.add))
        st.link(V.tensor_copy(tf[:, Table.ACTIVE:Table.ACTIVE + 1], rank_upto[:, NE - 1:NE]))
        st.link(V.tensor_scalar(far[:], active[:], -float(2 * U), float(2 * U), ALU.mult, ALU.add))
        st.link(V.tensor_tensor(far[:], far[:], incl[:], ALU.add))
        st.link(V.tensor_tensor(cmp[:], far[:].unsqueeze(1).to_broadcast([P, U, NE]),
                                ramp[:, 0:U].unsqueeze(2).to_broadcast([P, U, NE]), ALU.is_le))
        st.link(V.tensor_reduce(owner[:], cmp[:], AX.X, ALU.add))
        st.link(V.tensor_scalar(last[:], rank_upto[:, NE - 1:NE], -1.0, None, ALU.add))
        st.link(V.tensor_scalar(owner[:], owner[:], last[:, 0:1], None, ALU.min))
        NR = NE // RING + 1
        st.link(V.tensor_scalar(triple[:], ramp[:, 0:NR], float(RING), None, ALU.mult))
        for r in range(RING):
            if r:
                st.link(V.tensor_scalar(triple[:], triple[:], 1.0, None, ALU.add))
            st.link(V.tensor_tensor(cmp[:, :, 0:NR], owner[:].unsqueeze(2).to_broadcast([P, U, NR]),
                                    triple[:].unsqueeze(1).to_broadcast([P, U, NR]), ALU.is_ge))
            st.link(V.tensor_reduce(rounds[:, r], cmp[:, :, 0:NR], AX.X, ALU.add))
        per = tf[:, Table.OF_BLOCK:].rearrange("p (b n) -> p b n", n=Table.PER)
        st.link(V.scalar_tensor_tensor(out=owner[:], in0=rounds[:, 0], scalar=-float(RING), in1=owner[:], op0=ALU.mult, op1=ALU.add))
        st.link(V.tensor_scalar(per[:, :, 0:2], owner[:].rearrange("p (b u) -> p b u", u=2), float(RING), None, ALU.add))
        for r in range(RING):
            st.link(V.tensor_copy(per[:, :, 2 + r], rounds[:, r, 1:U:2]))
        st.link(V.tensor_copy(table[:], tf[:]))


def experts(k, l, first, table):
    nc, dr = k.nc, k.dram
    R2, RR = range(2), range(RING)
    LEAST = 2 * (NT - first)
    w13 = k.sb("w13", [P, RING, 2, KC * FF])
    w2 = k.sb("w2", [P, RING, FC * D])
    idx, one = k.sb("idx", [P, MAXP + 1], I32), k.sb("idx_block", [P, 1], I32)
    x, xT = k.sb("x", [P, D]), k.sb("xT", [P, KC, P])
    h, hT, y = k.sb("h", [P, FF]), k.sb("hT", [P, FC, P]), k.sb("y", [P, D])
    idx_in, gather_due, all_stored = k.sem("idx_in"), k.sem("gather_due"), k.sem("all_stored")
    w13_in, w2_in = [k.sem(f"w13_in{r}", True) for r in RR], [k.sem(f"w2_in{r}", True) for r in RR]
    idx_ready, x_in, x_turned = k.sem("idx_ready"), k.sem("x_in"), k.sem("x_turned")
    xT_act, xT_dve = k.sem("xT_act"), k.sem("xT_dve")
    xw1_ready, up_ready, silu_ready = k.sem("xw1_ready"), k.sem("up_ready"), k.sem("silu_ready")
    h_ready, h_turned, hT_ready = k.sem("h_ready"), k.sem("h_turned"), k.sem("hT_ready")
    y0_mm, y_mm, y_dve, y_act, y_stored = (k.sem(n, True) for n in ("y0_mm", "y_mm", "y_dve", "y_act", "y_stored"))
    block = k.block()

    def passes(eng, body):
        with eng.Fori(1, LEAST) as j:
            body(j)
        count = eng.value_load(table[0:1, Table.BLOCKS:Table.BLOCKS + 1], min_val=LEAST, max_val=MAXP)
        with eng.Fori(LEAST, MAXP) as j:
            with eng.If(j < count):
                body(j)
        return eng.value_load(table[0:1, Table.LAST:Table.LAST + 1], min_val=LEAST - 1, max_val=MAXP - 1)

    @block.sync
    def _(sp):
        def entry(base, m, lo, hi):
            return sp.value_load(table[0:1, ds(m + base, 1)], min_val=lo, max_val=hi)

        def load13(m, r, wait=True):
            e = entry(Table.EXPERT, m, 0, NE - 1)
            if wait:
                sp.wait_ge(up_ready, entry(Table.BLOCKS_UPTO, m - RING, 1, MAXP))
            for half, name in enumerate(("moe_w1", "moe_w3")):
                sp.dma_start(w13[:, r, half, :], dr[name][l, ds(e, 1)].rearrange("a (p j) n -> p (a j n)", p=P)).then_inc(w13_in[r], 16)

        def load2(m, r, wait=True):
            e = entry(Table.EXPERT, m, 0, NE - 1)
            if wait:
                sp.wait_ge(y_mm, entry(Table.BLOCKS_UPTO, m - RING, 1, MAXP) + PRIME)
            sp.dma_start(w2[:, r, :], dr["moe_w2"][l, ds(e, 1)].rearrange("a (p j) n -> p (a j n)", p=P)).then_inc(w2_in[r], 16)

        active = sp.value_load(table[0:1, Table.ACTIVE:Table.ACTIVE + 1], min_val=1, max_val=NE)
        load13(0, 0, wait=False)
        for m in range(RING):
            with sp.If(active > m + 1):
                load13(m + 1, (m + 1) % RING, wait=m + 1 >= RING)
            with sp.If(active > m):
                load2(m, m, wait=False)
        with sp.Fori(1, NE // RING + 1) as i:
            for r in RR:
                with sp.If(i * RING + (r + 1) < active):
                    load13(i * RING + (r + 1), (r + 1) % RING)
                with sp.If(i * RING + r < active):
                    load2(i * RING + r, r)

    @block.gpsimd
    def _(pool):
        with nc.allow_non_contiguous_dma(reason="slots of a block over partitions"):
            pool.dma_start(idx[:], dr["slot_token"].rearrange("(b p) a -> p (b a)", p=P)).then_inc(idx_in, 16)
        pool.wait_ge(idx_in, 16)

        def gather(j):
            if not isinstance(j, int) or j:
                pool.wait_ge(x_in, j * 16)
            nc.gpsimd.tensor_copy(one[:], idx[:, ds(j, 1)]).then_inc(idx_ready, 1)
            if not isinstance(j, int) or j:
                pool.wait_ge(x_turned, j)
            pool.wait_ge(idx_ready, j + 1)
            pool.sem_inc(gather_due, 1)
            pool.indirect_dma_start(x[:], None, dr["moe_x"],
                                    bass.IndirectOffsetOnAxis(ap=one[:, 0:1], axis=0)).then_inc(x_in, 16)
        gather(0)
        gather(1)
        passes(pool, lambda j: gather(j + 1))

    X, UP, HT, Y = (0, 1), (2, 3), 4, (5, 6)

    @block.tensor
    def _(pe):
        def entry(j, n, hi):
            return pe.value_load(table[0:1, ds(j * Table.PER + (Table.OF_BLOCK + n), 1)], min_val=0, max_val=hi)

        def by_buffer(buf, products):
            for r in RR:
                with pe.If(buf == r):
                    products(r)

        def turn_x(j):
            pe.wait_ge(x_in, j * 16 + 16)
            if not isinstance(j, int) or j:
                pe.wait_ge(xT_act, j)
                pe.wait_ge(xT_dve, j)
            for c in range(KC):
                t = pe.transpose(k.bank[X[c // 4]][:, (c % 4) * P:(c % 4 + 1) * P], x[:, c:D:KC], k.eye[:])
            t.then_inc(x_turned, 1)

        def turn_h(j):
            pe.wait_ge(h_ready, j + 1)
            for c in range(FC):
                t = pe.transpose(k.bank[HT][:, c * P:(c + 1) * P], h[:, c:FF:FC], k.eye[:])
            t.then_inc(h_turned, 1)

        def up(j):
            buf = [entry(j, u, RING - 1) for u in R2]
            loads = [entry(j, 2 + r, NE) for r in RR]
            pe.wait_ge(xT_act, j + 1)
            pe.wait_ge(xT_dve, j + 1)
            for r in RR:
                pe.wait_ge(w13_in[r], loads[r] * 32 + PRIME)

            def products(r):
                for half in R2:
                    for c in range(KC):
                        for u in R2:
                            mm = pe.matmul(k.bank[UP[half]][u * UNIT:(u + 1) * UNIT, :], xT[:, c, u * UNIT:(u + 1) * UNIT],
                                           w13[:, r if u else ds(buf[0], 1), half, c * FF:(c + 1) * FF].rearrange(
                                               "p n -> p n" if u else "p a n -> p (a n)"),
                                           start=(c == 0), stop=(c == KC - 1))
                    mm.then_inc((xw1_ready, up_ready)[half], 1)
            by_buffer(buf[1], products)

        def down(j):
            buf = [entry(j, u, RING - 1) for u in R2]
            loads = [entry(j, 2 + r, NE) for r in RR]
            pe.wait_ge(hT_ready, j + 1)
            pe.wait_ge(y_dve, j + PRIME)
            pe.wait_ge(y_act, j + PRIME)
            for r in RR:
                pe.wait_ge(w2_in[r], loads[r] * 16 + PRIME)

            def products(r):
                for half in R2:
                    for c in range(FC):
                        for u in R2:
                            at = c * D + half * 512
                            mm = pe.matmul(k.bank[Y[half]][u * UNIT:(u + 1) * UNIT, :], hT[:, c, u * UNIT:(u + 1) * UNIT],
                                           w2[:, r if u else ds(buf[0], 1), at:at + 512].rearrange(
                                               "p n -> p n" if u else "p a n -> p (a n)"),
                                           start=(c == 0), stop=(c == FC - 1))
                    mm.then_inc((y0_mm, y_mm)[half], 1)
            by_buffer(buf[1], products)

        turn_x(0)
        turn_x(1)
        up(0)

        def body(j):
            turn_x(j + 1)
            turn_h(j - 1)
            up(j)
            down(j - 1)
        last = passes(pe, body)
        turn_h(last)
        down(last)

    def copy_xT(half):
        return xT[:, 4 * half:4 * half + 4, :], k.bank[X[half]][:].rearrange("p (c q) -> p c q", c=4)

    @block.scalar
    def _(act):
        def first(j):
            act.wait_ge(xw1_ready, j + 1)
            if not isinstance(j, int):
                act.wait_ge(h_turned, j)
            nc.scalar.activation(h[:], k.bank[UP[0]][:], ACT.Silu).then_inc(silu_ready, 1)
            turned(j + 1)

        def turned(j):
            act.wait_ge(x_turned, j + 1)
            if not isinstance(j, int) or j:
                act.wait_ge(up_ready, j)
            nc.scalar.copy(*copy_xT(0)).then_inc(xT_act, 1)

        def second(j):
            act.wait_ge(y_mm, j + 1 + PRIME)
            act.wait_ge(y_stored, j * 16 + PRIME)
            nc.scalar.copy(y[:, 512:], k.bank[Y[1]][:]).then_inc(y_act, 1)
            act.wait_ge(y_act, j + 1 + PRIME)
            act.wait_ge(y_dve, j + 1 + PRIME)
            act.dma_start(dr["moe_y"][ds(j * P, P), :], y[:]).then_inc(y_stored, 16)

        turned(0)
        first(0)

        def body(j):
            first(j)
            second(j - 1)
        last = passes(act, body)
        second(last)
        act.wait_ge(y_stored, last * 16 + (16 + PRIME))
        act.sem_inc(all_stored, 1)

    @block.vector
    def _(dve):
        def turned(j):
            dve.wait_ge(x_turned, j + 1)
            if not isinstance(j, int) or j:
                dve.wait_ge(up_ready, j)
            nc.vector.tensor_copy(*copy_xT(1)).then_inc(xT_dve, 1)

        def first(j):
            dve.wait_ge(silu_ready, j + 1)
            dve.wait_ge(up_ready, j + 1)
            nc.vector.tensor_tensor(h[:], h[:], k.bank[UP[1]][:], ALU.mult).then_inc(h_ready, 1)
            turned(j + 1)

        def copy_hT(j):
            dve.wait_ge(h_turned, j + 1)
            dve.wait_ge(y_mm, j + PRIME)
            nc.vector.tensor_copy(hT[:].rearrange("p c q -> p (c q)"), k.bank[HT][:]).then_inc(hT_ready, 1)

        def second(j):
            dve.wait_ge(y0_mm, j + 1 + PRIME)
            dve.wait_ge(y_stored, j * 16 + PRIME)
            nc.vector.tensor_copy(y[:, 0:512], k.bank[Y[0]][:]).then_inc(y_dve, 1)

        turned(0)
        first(0)

        def body(j):
            copy_hT(j - 1)
            first(j)
            second(j - 1)
        last = passes(dve, body)
        copy_hT(last)
        second(last)


def combine(k, l, first, slots, wts):
    nc, dr = k.nc, k.dram
    R2 = range(2)
    T = NT - first
    g = k.sb("gate_rows", [P, 2, D])
    y = [[k.sb(f"y{u}{c}", [P, D]) for c in R2] for u in R2]
    s = [[k.sb(f"slot{u}{c}", [P, 1], I32) for c in R2] for u in R2]
    g_in, order, gather_due = k.sem("g_in"), k.sem("order"), k.sem("gather_due")
    y_in, copied, scaled, added = ([k.sem(f"{n}{u}") for u in R2] for n in ("y_in", "copied", "scaled", "added"))
    block = k.block()

    def passes(eng, body):
        if first == 0:
            body(0, 0, 0)
        with eng.Fori(1, NT // 2) as i:
            body(i, i if first == 0 else i - 1, 1)

    @block.sync
    def _(sp):
        for v in R2:
            spread_row(k, sp, g[:, v, :], l, v, 5, g_in)

    @block.gpsimd
    def _(pool):
        def body(i, n, v):
            for u in R2:
                pool.wait_ge(y_in[u], n * 32)
                for c in R2:
                    nc.gpsimd.tensor_copy(s[u][c][:], slots[:, c, ds(n * 2 + u, 1)]).then_inc(copied[u], 1)
                pool.wait_ge(added[u], n)
                pool.wait_ge(copied[u], n * 2 + 2)
                pool.sem_inc(gather_due, 1)
                for c in R2:
                    pool.indirect_dma_start(y[u][c][:], None, dr["moe_y"],
                                            bass.IndirectOffsetOnAxis(ap=s[u][c][:, 0:1], axis=0)).then_inc(y_in[u], 16)
        passes(pool, body)

    @block.scalar
    def _(act):
        def body(i, n, v):
            for u in R2:
                act.wait_ge(y_in[u], n * 32 + 32)
                nc.scalar.activation(y[u][0][:], y[u][0][:], ACT.Copy,
                                     scale=wts[:, 0, ds(n * 2 + u, 1)]).then_inc(scaled[u], 1)
        passes(act, body)

    @block.vector
    def _(dve):
        dve.wait_ge(g_in, 32)
        st = Steps(dve, order, 4)

        def body(i, n, v):
            st.at(n)
            for u in R2:
                dve.wait_ge(scaled[u], n + 1)
                st.link(nc.vector.scalar_tensor_tensor(out=y[u][1][:], in0=y[u][1][:], scalar=wts[:, 1, ds(n * 2 + u, 1)],
                                                       in1=y[u][0][:], op0=ALU.mult, op1=ALU.add))
                st.link(nc.vector.tensor_tensor(y[u][1][:], y[u][1][:], g[:, v, :], ALU.mult))
                h = k.H[:, ds(i * 2 + u, 1), :].rearrange("p a d -> p (a d)")
                nc.vector.tensor_tensor(h, h, y[u][1][:], ALU.add).then_inc(added[u], 1)
            st.end()
        passes(dve, body)


def moe(k, l, first):
    with k.scope():
        T = NT - first
        slots, wts = k.sb("slots", [P, 2, T], I32), k.sb("weights", [P, 2, T])
        table = k.sb("table", [P, Table.SIZE], I32)
        with k.scope():
            logits = k.sb("logits", [P, T, GROUPS + NE])
            with k.scope():
                norm_mod(k, l, 1, first, logits=logits)
            with k.scope():
                route(k, first, logits, slots, wts, table)
        with k.scope():
            experts(k, l, first, table)
        with k.scope():
            combine(k, l, first, slots, wts)


def project1(k, aT):
    nc, dr = k.nc, k.dram
    R2 = range(2)
    QW, KW = ATT_H * HD, ATT_KV * HD
    RH = (QW + KW) // HD
    NF = HD // 4
    w = k.sb("w_in", [P, KC, ATT_COLS])
    rope = k.sb("rope", [P, LT, 2, 2, NF])
    z, rt = [k.sb(f"z{s}", [P, ATT_COLS]) for s in R2], [k.sb(f"rotated{s}", [P, RH, 2, 2, NF]) for s in R2]
    kd = [k.sb(f"k_twice{s}", [P, ATT_KV, 2, HD]) for s in R2]
    out = [k.sb(f"turned{s}", [P, 12, P]) for s in R2]
    t1, t2, t3, t4 = (k.sb(f"t{n}", [P, RH, 2, NF]) for n in range(4))
    pad = k.sb("zero", [P, ATT_KV * P])
    w_in, rope_in, z_ready, z_copied = k.sem("w_in"), k.sem("rope_in"), k.sem("z_ready"), k.sem("z_copied")
    first_ready, second_ready, kd_ready = k.sem("first_ready"), k.sem("second_ready"), k.sem("kd_ready")
    turned, taken, dve_order, pool_order = k.sem("turned"), k.sem("taken"), k.sem("dve_order"), k.sem("pool_order")
    stored, pad_set, padded = [k.sem(f"stored{s}") for s in R2], k.sem("pad_set"), k.sem("padded")
    block = k.block()

    def rounds(t):
        return t if t < CT else CT + 3 * (t - CT)

    def stores(t):
        return sum(48 if x >= CT else 32 for x in range(t % 2, t, 2))

    def place(t):
        return t - CT + 1 if t >= CT else LT + 2 + t

    @block.sync
    def _(sp):
        for g in (2, 0, 1):
            sp.dma_start(w[:, :, g * 512:(g + 1) * 512],
                         dr["at_w_in"][0, :, g * 512:(g + 1) * 512].rearrange("(j p) n -> p j n", p=P)).then_inc(w_in, 16)
        sp.dma_start(rope[:].rearrange("p t a b f -> p t (a b f)"),
                     dr["const_rope"].rearrange("(t p) a b f -> p t (a b f)", p=P)).then_inc(rope_in, 16)
        sp.wait_ge(pad_set, 1)
        for at in (0, LT + 1):
            sp.dma_start(dr["att_k"][at], pad[:]).then_inc(padded, 16)
            sp.dma_start(dr["att_v"][at], pad[:, 0:KW]).then_inc(padded, 16)
        for t in range(NT):
            s = t % 2
            sp.wait_ge(taken, rounds(t + 1))
            if t >= CT:
                sp.dma_start(dr["att_q"][t - CT], out[s][:, 0:8, :].rearrange("p c n -> p (c n)")).then_inc(stored[s], 16)
            sp.dma_start(dr["att_k"][place(t)], out[s][:, 8:12, :].rearrange("p c n -> p (c n)")).then_inc(stored[s], 16)
            sp.dma_start(dr["att_v"][place(t)], z[s][:, QW + KW:]).then_inc(stored[s], 16)
        for s in R2:
            sp.wait_ge(stored[s], stores(NT + s))
        sp.wait_ge(padded, 64)

    @block.tensor
    def _(pe):
        pe.wait_ge(w_in, 48)

        def project(t):
            s = t % 2
            if t >= 2:
                pe.wait_ge(z_copied, t - 1)
            for g in ((2,) if t < CT else (0, 1, 2)):
                for c in range(KC):
                    mm = pe.matmul(k.bank[3 * s + g][:], aT[:, c, t * P:(t + 1) * P], w[:, c, g * 512:(g + 1) * 512],
                                   start=(c == 0), stop=(c == KC - 1))
            mm.then_inc(z_ready, 1)

        def turn(t):
            s = t % 2
            pe.wait_ge(kd_ready, t + 1)
            for g in ((2,) if t < CT else (0, 1, 2)):
                r = rounds(t) + (g if t >= CT else 0)
                if r >= 2:
                    pe.wait_ge(taken, r - 1)
                for q in range(4):
                    c = 4 * g + q
                    src = (kd[s][:].rearrange("p h a d -> p (h a d)")[:, (c - 8) * P:(c - 7) * P] if g == 2 else
                           rt[s][:].rearrange("p h a b f -> p (h a b f)")[:, c * P:(c + 1) * P])
                    mm = pe.transpose(k.bank[6 + r % 2][:, q * P:(q + 1) * P], src, k.eye[:])
                mm.then_inc(turned, 1)

        for t in range(NT + 1):
            if t < NT:
                project(t)
            if t > 0:
                turn(t - 1)

    @block.scalar
    def _(act):
        for t in range(NT + 1):
            if t < NT:
                s = t % 2
                act.wait_ge(z_ready, t + 1)
                if t >= 2:
                    act.wait_ge(stored[s], stores(t))
                for g in ((2,) if t < CT else (0, 1, 2)):
                    c = nc.scalar.copy(z[s][:, g * 512:(g + 1) * 512], k.bank[3 * s + g][:])
                c.then_inc(z_copied, 1)
                if t < CT:
                    act.wait_ge(z_copied, t + 1)
                    keys = z[s][:, QW:QW + KW].rearrange("p (h d) -> p h d", h=ATT_KV)
                else:
                    act.wait_ge(first_ready, t - CT + 1)
                    act.wait_ge(second_ready, t - CT + 1)
                    keys = rt[s][:, ATT_H:, :, :, :].rearrange("p h a b f -> p h (a b f)")
                if t >= 2:
                    act.wait_ge(turned, rounds(t - 1))
                nc.scalar.copy(kd[s][:], keys.unsqueeze(2).to_broadcast([P, ATT_KV, 2, HD])).then_inc(kd_ready, 1)
            if t > 0:
                u = t - 1
                for g in ((2,) if u < CT else (0, 1, 2)):
                    r = rounds(u) + (g if u >= CT else 0)
                    act.wait_ge(turned, r + 1)
                    nc.scalar.copy(out[u % 2][:, 4 * g:4 * g + 4, :].rearrange("p c n -> p (c n)"),
                                   k.bank[6 + r % 2][:]).then_inc(taken, 1)

    def halves(t):
        s = t % 2
        u = z[s][:, 0:QW + KW].rearrange("p (h a b f) -> p h a b f", a=2, b=2, f=NF)
        cos, sin = (rope[:, t - CT, n].unsqueeze(1).to_broadcast([P, RH, 2, NF]) for n in R2)
        return u[:, :, :, 0, :], u[:, :, :, 1, :], cos, sin

    @block.vector
    def _(dve):
        dve.wait_ge(rope_in, 16)
        st = Steps(dve, dve_order)
        for t in range(CT, NT):
            dve.wait_ge(z_copied, t + 1)
            dve.wait_ge(turned, rounds(t - 1))
            a, b, cos, sin = halves(t)
            nc.vector.tensor_tensor(t1[:], a, cos, ALU.mult)
            st.link(nc.vector.tensor_tensor(t2[:], b, sin, ALU.mult))
            nc.vector.tensor_tensor(rt[t % 2][:, :, :, 0, :], t1[:], t2[:], ALU.subtract).then_inc(first_ready, 1)

    @block.gpsimd
    def _(pool):
        nc.gpsimd.memset(pad[:], 0.0).then_inc(pad_set, 1)
        pool.wait_ge(rope_in, 16)
        st = Steps(pool, pool_order)
        for t in range(CT, NT):
            pool.wait_ge(z_copied, t + 1)
            pool.wait_ge(turned, rounds(t - 1))
            a, b, cos, sin = halves(t)
            nc.gpsimd.tensor_tensor(t3[:], a, sin, ALU.mult)
            st.link(nc.gpsimd.tensor_tensor(t4[:], b, cos, ALU.mult))
            nc.gpsimd.tensor_tensor(rt[t % 2][:, :, :, 1, :], t3[:], t4[:], ALU.add).then_inc(second_ready, 1)


def attend(k, att):
    nc, dr = k.nc, k.dram
    R2 = range(2)
    W, C = 3 * P, CTX
    PAIRS, KVS = ATT_H // 2, ATT_KV
    M, KM = 2 * PAIRS, 2 * KVS
    PASSES = LT // 2
    SCALE = HD ** -0.5
    q, kw = [k.sb(f"q{u}", [P, PAIRS, P]) for u in R2], [k.sb(f"k_win{u}", [P, 3, KVS, P]) for u in R2]
    vw, band = [k.sb(f"v_win{u}", [P, 3, KVS * HD]) for u in R2], [k.sb(f"band{u}", [P, W]) for u in R2]
    kc, vc = k.sb("k_ctx", [P, KVS, C]), k.sb("v_ctx", [P, CT, KVS * HD])
    sink, sink8 = k.sb("sink", [P, ATT_H]), k.sb("sink_scaled", [P, ATT_H])
    sm, pr = [k.sb(f"masked{s}", [P, 2, W]) for s in R2], [k.sb(f"probs{s}", [P, 2, W + C]) for s in R2]
    pt = [k.sb(f"probsT{s}", [P, 5, 2, 2, P]) for s in R2]
    small = [{n: k.sb(f"{n}{s}", [P, 2]) for n in ("max_win", "max_ctx", "neg_max", "sum_win", "sum_ctx",
                                                      "sink_part", "den")} for s in R2]
    ctx_in, blk_in = k.sem("ctx_in"), [k.sem(f"blk_in{u}") for u in R2]
    ctx0_ready = k.sem("ctx0_ready")
    s_ready, max_ready, p_ready, order = k.sem("s_ready"), k.sem("max_ready"), k.sem("p_ready"), k.sem("dve_order")
    inv_ready, scaled0, scaled1, sink_set = k.sem("inv_ready"), k.sem("scaled0"), k.sem("scaled1"), k.sem("sink_set")
    turned, pt_act, pt_dve = k.sem("turned"), k.sem("pt_act"), k.sem("pt_dve")
    o_ready, o_taken, den_order = k.sem("o_ready"), k.sem("o_taken"), k.sem("den_order")
    block = k.block()

    def logit_banks(m):
        return [k.bank[3 * (m % 2) + n] for n in range(3)]

    def fill(m, r):
        return 7 * (m // 2) + 3 * (m % 2) + r

    def wait_fill(pe, n, f):
        g, x = (f - 2) // 7, (f - 2) % 7
        if f < 2:
            pe.wait_ge(pt_dve, n * M)
            pe.wait_ge(o_taken, n * KM)
        elif x == 6:
            pe.wait_ge(o_taken, n * KM + g + 1)
        elif x % 3 == 2:
            pe.wait_ge(pt_dve, n * M + 2 * g + x // 3 + 1)
        else:
            pe.wait_ge(pt_act, n * 2 * M + 4 * g + 2 * (x // 3) + x % 3 + 1)

    @block.sync
    def _(sp):
        for t in range(CT):
            sp.dma_start(kc[:, :, t * P:(t + 1) * P], dr["att_k"][LT + 2 + t].rearrange("p (h n) -> p h n", h=KVS)).then_inc(ctx_in, 16)
        sp.dma_start(vc[:], dr["att_v"][LT + 2:].rearrange("t p n -> p t n")).then_inc(ctx_in, 16)
        sp.dma_start(sink[:], dr["at_sink"].to_broadcast([P, ATT_H])).then_inc(ctx_in, 16)

        def load(b, u):
            sp.dma_start(q[u][:].rearrange("p c n -> p (c n)"), dr["att_q"][ds(b, 1)].rearrange("a p n -> p (a n)")).then_inc(blk_in[u], 16)
            sp.dma_start(kw[u][:].rearrange("p t h n -> p t (h n)"), dr["att_k"][ds(b, 3)].rearrange("t p n -> p t n")).then_inc(blk_in[u], 16)
            sp.dma_start(vw[u][:], dr["att_v"][ds(b, 3)].rearrange("t p n -> p t n")).then_inc(blk_in[u], 16)
            sp.dma_start(band[u][:], dr["const_band"][ds(b, 1)].rearrange("a p n -> p (a n)")).then_inc(blk_in[u], 16)

        for u in R2:
            load(u, u)
        with sp.Fori(1, PASSES) as i:
            for u in R2:
                sp.wait_ge(o_ready, (i - 1) * KM + (u + 1) * KVS)
                load(i * 2 + u, u)

    @block.tensor
    def _(pe):
        pe.wait_ge(ctx_in, 64)

        def scores(n, m):
            u, kv, c = m // PAIRS, (m % PAIRS) // 2, m % PAIRS
            b = logit_banks(m)
            pe.wait_ge(p_ready, n * M + m - 1 if m >= 2 else n * M)
            if m % PAIRS == 0:
                pe.wait_ge(blk_in[u], n * 64 + 64)
            for h in R2:
                on = slice(HD * h, HD * h + HD)
                pe.matmul(b[h][:, 0:W], q[u][on, c, :], kw[u][on, :, kv, :], start=True, stop=True)
                if h:
                    pe.wait_ge(ctx0_ready, n * M + m + 1)
                mm = pe.matmul(b[2][:, h * C:(h + 1) * C], q[u][on, c, :], kc[on, kv, :], start=True, stop=True)
                mm.then_inc(s_ready if h else ctx0_ready, 1)

        def turn(n, m):
            for r in range(3):
                f = fill(m, r)
                wait_fill(pe, n, f)
                for h in ((r,) if r < 2 else R2):
                    pe.wait_ge((scaled0, scaled1)[h], n * M + m + 1)
                    for c in (range(4) if r < 2 else (4,)):
                        at = c * P if r < 2 else h * P
                        mm = pe.transpose(k.bank[6 + f % 2][:, at:at + P], pr[m % 2][:, h, c * P:(c + 1) * P], k.eye[:])
                mm.then_inc(turned, 1)

        def output(n, m):
            g = m // 2
            u, kv = g // KVS, g % KVS
            f = fill(m, 3)
            wait_fill(pe, n, f)
            pe.wait_ge(pt_act, n * 2 * M + 2 * m + 2)
            pe.wait_ge(pt_dve, n * M + m + 1)
            to = k.bank[6 + f % 2]
            for h in R2:
                for c in range(5):
                    v = vw[u][:, c, kv * HD:(kv + 1) * HD] if c < 3 else vc[:, c - 3, kv * HD:(kv + 1) * HD]
                    mm = pe.matmul(to[HD * h:HD * h + HD, 0:2 * P], v, pt[g % 2][:, c, h, :, :],
                                   start=(c == 0), stop=(c == 4))
            mm.then_inc(o_ready, 1)

        with pe.Fori(0, PASSES) as n:
            scores(n, 0)
            for m in range(M):
                if m + 1 < M:
                    scores(n, m + 1)
                turn(n, m)
                if m % 2:
                    output(n, m)

    @block.scalar
    def _(act):
        act.wait_ge(ctx_in, 64)
        with act.Fori(0, PASSES) as n:
            for m in range(M):
                s, x = m % 2, small[m % 2]
                b = logit_banks(m)
                act.wait_ge(max_ready, n * M + m + 1)
                act.wait_ge(turned, 3 * (n * M) + 3 * (m - 1) if m >= 2 else n * (3 * M))
                act.wait_ge(inv_ready, n * M + m - 1 if m >= 2 else n * M)
                nc.scalar.activation(x["sink_part"][:], x["sink_part"][:], ACT.Exp)
                for h in R2:
                    nc.scalar.activation(pr[s][:, h, 0:W], sm[s][:, h, :], ACT.Exp, bias=x["neg_max"][:, h:h + 1],
                                         scale=SCALE, accum_out=x["sum_win"][:, h:h + 1])
                    e = nc.scalar.activation(pr[s][:, h, W:], b[2][:, h * C:(h + 1) * C], ACT.Exp,
                                             bias=x["neg_max"][:, h:h + 1], scale=SCALE, accum_out=x["sum_ctx"][:, h:h + 1])
                e.then_inc(p_ready, 1)
                for h in R2:
                    act.wait_ge(turned, n * (3 * M) + 3 * m + h + 1)
                    g = m // 2
                    if m % 2 == 0 and h == 0:
                        act.wait_ge(o_ready, n * KM + g - 1 if g >= 2 else n * KM)
                    nc.scalar.copy(pt[g % 2][:, 0:4, h, m % 2, :],
                                   k.bank[6 + fill(m, h) % 2][:].rearrange("p (c n) -> p c n", c=4)).then_inc(pt_act, 1)

    @block.gpsimd
    def _(pool):
        with pool.Fori(0, PASSES) as n:
            for m in range(M):
                pool.wait_ge(inv_ready, n * M + m + 1)
                nc.gpsimd.tensor_tensor(pr[m % 2][:, 0, :], pr[m % 2][:, 0, :],
                                        small[m % 2]["den"][:, 0:1].to_broadcast([P, W + C]), ALU.mult).then_inc(scaled0, 1)

    @block.vector
    def _(dve):
        V = nc.vector
        dve.wait_ge(ctx_in, 64)
        V.tensor_scalar(sink8[:], sink[:], 1.0 / SCALE, None, ALU.mult).then_inc(sink_set, 1)
        dve.wait_ge(sink_set, 1)
        st = Steps(dve, order, M * 4)

        def maxima(n, m):
            u, x, b = m // PAIRS, small[m % 2], logit_banks(m)
            if m % PAIRS == 0:
                dve.wait_ge(blk_in[u], n * 64 + 64)
            dve.wait_ge(s_ready, n * M + m + 1)
            heads = slice(2 * (m % PAIRS), 2 * (m % PAIRS) + 2)
            V.tensor_reduce(x["max_ctx"][:], b[2][:].rearrange("p (h n) -> p h n", h=2), AX.X, ALU.max)
            for h in R2:
                r = V.tensor_tensor_reduce(out=sm[m % 2][:, h, :], in0=b[h][:, 0:W], in1=band[u][:], scale=1.0,
                                           scalar=-3e38, op0=ALU.add, op1=ALU.max, accum_out=x["max_win"][:, h:h + 1])
            st.link(r)
            st.link(V.tensor_tensor(x["max_ctx"][:], x["max_ctx"][:], x["max_win"][:], ALU.max))
            st.link(V.tensor_tensor(x["max_ctx"][:], x["max_ctx"][:], sink8[:, heads], ALU.max))
            st.link(V.tensor_scalar(x["neg_max"][:], x["max_ctx"][:], -SCALE, None, ALU.mult))
            V.tensor_tensor(x["sink_part"][:], sink[:, heads], x["neg_max"][:], ALU.add).then_inc(max_ready, 1)

        def divide(n, m):
            x = small[m % 2]
            dve.wait_ge(p_ready, n * M + m + 1)
            V.tensor_tensor(x["den"][:], x["sum_win"][:], x["sum_ctx"][:], ALU.add).then_inc(den_order, 1)
            dve.wait_ge(den_order, (n * M + m) * 2 + 1)
            V.tensor_tensor(x["den"][:], x["den"][:], x["sink_part"][:], ALU.add).then_inc(den_order, 1)
            dve.wait_ge(den_order, (n * M + m) * 2 + 2)
            V.reciprocal(x["den"][:], x["den"][:]).then_inc(inv_ready, 1)
            dve.wait_ge(inv_ready, n * M + m + 1)
            V.tensor_scalar(pr[m % 2][:, 1, :], pr[m % 2][:, 1, :], x["den"][:, 1:2], None, ALU.mult).then_inc(scaled1, 1)

        with dve.Fori(0, PASSES) as n:
            st.at(n)
            maxima(n, 0)
            for m in range(M):
                g = m // 2
                u, kv = g // KVS, g % KVS
                divide(n, m)
                if m + 1 < M:
                    maxima(n, m + 1)
                dve.wait_ge(turned, n * (3 * M) + 3 * m + 3)
                if m % 2 == 0:
                    dve.wait_ge(o_ready, n * KM + g - 1 if g >= 2 else n * KM)
                V.tensor_copy(pt[g % 2][:, 4, :, m % 2, :],
                              k.bank[6 + fill(m, 2) % 2][:, 0:2 * P].rearrange("p (h n) -> p h n", h=2)).then_inc(pt_dve, 1)
                if m % 2:
                    dve.wait_ge(o_ready, n * KM + g + 1)
                    V.tensor_copy(att[:, 2 * kv:2 * kv + 2, ds(n * (2 * P) + u * P, P)],
                                  k.bank[6 + fill(m, 3) % 2][:, 0:2 * P].rearrange("p (c n) -> p c n", c=2)).then_inc(o_taken, 1)
            st.end()


def final_norm(k):
    nc, dr, H = k.nc, k.dram, k.H
    R2 = range(2)
    w = k.sb("norm_rows", [P, D])
    sq, y = k.sb("squares", [P, 2, D]), [k.sb(f"y{u}", [P, D]) for u in R2]
    r = k.sb("rstd", [P, 2])
    w_in, sum_ready, mean_ready, root_ready = k.sem("w_in"), k.sem("sum_ready"), k.sem("mean_ready"), k.sem("root_ready")
    y_ready, order = k.sem("y_ready"), k.sem("order")
    y_stored = [k.sem(f"y_stored{u}") for u in R2]
    block = k.block()

    @block.sync
    def _(sp):
        sp.dma_start(w[:], dr["norm_final"].rearrange("(a n) -> a n", a=1).to_broadcast([P, D])).then_inc(w_in, 16)
        out = dr["out"].rearrange("a t d -> (a t) d")
        with sp.Fori(0, LT // 2) as i:
            for u in R2:
                sp.wait_ge(y_ready, i * 2 + u + 1)
                sp.dma_start(out[ds(i * (2 * P) + u * P, P), :], y[u][:]).then_inc(y_stored[u], 16)
        for u in R2:
            sp.wait_ge(y_stored[u], 16 * (LT // 2))

    @block.scalar
    def _(act):
        with act.Fori(0, LT // 2) as i:
            act.wait_ge(y_ready, i * 2)
            for u in R2:
                nc.scalar.activation(sq[:, u, :], H[:, ds(i * 2 + (CT + u), 1), :].rearrange("p a d -> p (a d)"),
                                     ACT.Square, accum_out=r[:, u:u + 1]).then_inc(sum_ready, 1)
            for u in R2:
                act.wait_ge(mean_ready, i * 2 + u + 1)
                nc.scalar.activation(r[:, u:u + 1], r[:, u:u + 1], ACT.Sqrt).then_inc(root_ready, 1)

    @block.vector
    def _(dve):
        dve.wait_ge(w_in, 16)
        st = Steps(dve, order, 2)
        with dve.Fori(0, LT // 2) as i:
            st.at(i)
            for u in R2:
                f = r[:, u:u + 1]
                dve.wait_ge(sum_ready, i * 2 + u + 1)
                nc.vector.tensor_scalar(f, f, 1.0 / D, EPS, ALU.mult, ALU.add).then_inc(mean_ready, 1)
                dve.wait_ge(root_ready, i * 2 + u + 1)
                st.link(nc.vector.reciprocal(f, f))
                dve.wait_ge(y_stored[u], i * 16)
                nc.vector.scalar_tensor_tensor(out=y[u][:], in0=H[:, ds(i * 2 + (CT + u), 1), :].rearrange("p a d -> p (a d)"),
                                               scalar=f, in1=w[:], op0=ALU.mult, op1=ALU.mult).then_inc(y_ready, 1)
            st.end()


def constants():
    i = np.arange(P)
    tri = np.stack([i[:, None] <= i[None, :], i[:, None] >= i[None, :]]).astype(np.float32)
    merge = np.zeros((2, LEVELS, P, P), np.float32)
    for n in range(LEVELS):
        pair = (i[:, None] >> (n + 1)) == (i[None, :] >> (n + 1))
        for d, low in enumerate((i[:, None] > i[None, :], i[:, None] < i[None, :])):
            merge[d, n] = pair & low & ((i[:, None] >> n) != (i[None, :] >> n))
    nf = HD // 4
    inv = np.power(np.float32(10000.0), -np.arange(nf, dtype=np.float32) / np.float32(nf)).astype(np.float32)
    pos = np.arange(SEQ)
    angle = np.stack([(pos // 64).astype(np.float32)[:, None] * inv, (pos % 64).astype(np.float32)[:, None] * inv], 1)
    rope = np.stack([np.cos(angle), np.sin(angle)], 1).astype(np.float32)
    key = np.arange(3 * P)[None, :] - P
    near = np.abs(i[:, None] - key) <= WIN
    band = np.where(np.stack([near & (key >= 0)] + [near] * (LT - 2) + [near & (key < P)]), 0.0, -1e30).astype(np.float32)
    return {
        "const_eye": np.eye(P, dtype=np.float32),
        "const_tri": tri,
        "const_merge": merge,
        "const_rope": rope,
        "const_band": band,
        "const_ramp": np.arange(P, dtype=np.float32)[None, :],
    }


def build(nc, dram):
    k = Kernel(nc, dram)
    with k.scope():
        k.bank = [k.scopes[-1].enter_context(nc.psum_tensor(f"bank{b}", [P, 512], F32)) for b in range(8)]
        k.H = k.sb("H", [P, NT, D])
        k.eye = k.sb("eye", [P, P])
        k.tri = k.sb("tri", [P, 2, P])
        for l in range(2):
            with k.scope():
                modulation(k, l)
        with k.scope():
            k.gate = k.sb("gate", [P, NH, TOK])
            k.short = k.sb("short", [P, NH, TOK])
            k.ab = k.sb("ab", [P, NT, 4 * NH])
            with k.scope():
                aT = k.sb("aT", [P, KC, TOK])
                with k.scope():
                    norm_mod(k, 0, 0, 0, aT=aT)
                with k.scope():
                    project0(k, aT)
            with k.scope():
                oT = k.sb("oT", [P, NH, TOK])
                with k.scope():
                    delta_scan(k, oT)
                with k.scope():
                    gate_heads(k, oT)
                with k.scope():
                    project_out(k, 0, 0, lambda c, t: (oT if c < NH else k.short)[:, c % NH, t * P:(t + 1) * P],
                                "ab_w_out")
        moe(k, 0, 0)
        with k.scope():
            aT = k.sb("aT", [P, KC, TOK])
            with k.scope():
                norm_mod(k, 1, 0, 0, aT=aT)
            with k.scope():
                project1(k, aT)
        with k.scope():
            att = k.sb("att", [P, KC, SEQ])
            with k.scope():
                attend(k, att)
            with k.scope():
                project_out(k, 1, CT, lambda c, t: att[:, c, (t - CT) * P:(t - CT + 1) * P], "at_w_out")
        moe(k, 1, CT)
        with k.scope():
            final_norm(k)


INPUTS = ("x", "c", "ctx", "c_ctx", "ada_w", "ada_b", "norm_mix", "norm_ffn", "norm_final", "ab_w_in",
          "ab_conv_qkv", "ab_conv_sc", "ab_a_log", "ab_dt_bias", "ab_out_norm", "ab_w_out", "at_w_in",
          "at_sink", "at_w_out", "moe_w_group", "moe_w_expert", "moe_w1", "moe_w3", "moe_w2")


def kernel(**inputs):
    import concourse.bacc as bacc
    from concourse.bass_utils import run_bass_kernel_spmd

    nc = bacc.Bacc("TRN2", target_bir_lowering=False, num_devices=1)
    arrays, dram = {}, {}
    for name, a in [(n, np.ascontiguousarray(inputs[n])) for n in INPUTS] + list(constants().items()):
        arrays[f"in_{name}"] = a
        dram[name] = nc.dram_tensor(f"in_{name}", a.shape, mybir.dt.from_np(a.dtype), kind="ExternalInput").ap()
    for name, shape, dt in (
        ("mods", (2, 2, MODS * D), F32),
        ("heads", (4, NT, P, W0), F32),
        ("moe_x", (TOK, D), F32),
        ("att_q", (LT, P, ATT_H // 2 * P), F32),
        ("att_k", (NT + 2, P, ATT_KV * P), F32),
        ("att_v", (NT + 2, P, ATT_KV * HD), F32),
        ("moe_y", (SLOTS, D), F32),
        ("slot_token", (SLOTS + P, 1), I32),
    ):
        dram[name] = nc.dram_tensor(name, shape, dt).ap()
    dram["out"] = nc.dram_tensor("out", (1, SEQ, D), F32, kind="ExternalOutput").ap()
    build(nc, dram)
    r = run_bass_kernel_spmd(nc, [arrays], core_ids=[0])
    return r.results[0]["out"]
```

```python
from contextlib import ExitStack, contextmanager

import numpy as np

import concourse.bass as bass
import concourse.mybir as mybir

F32 = mybir.dt.float32
I32 = mybir.dt.int32
ACT = mybir.ActivationFunctionType
ALU = mybir.AluOpType
AX = mybir.AxisListType

P = 128
D = 1024
KC = D // P
SEQ, CTX = 1024, 256
TOK = SEQ + CTX
NT = TOK // P
CT = CTX // P
LT = SEQ // P
EPS = 1e-6
NH = 4
W0 = NH * P
ATT_H, ATT_KV, HD = 16, 4, 64
ATT_COLS = (ATT_H + 2 * ATT_KV) * HD
WIN = 128
GROUPS, PER = 4, 8
NE = GROUPS * PER
FF = 512
FC = FF // P
LEVELS = 7
MODS = 6
UNIT = P // 2
MAXP = ((2 * TOK + NE * (UNIT - 1)) // UNIT + 1) // 2
SLOTS = MAXP * P
RING = 3
PRIME = 1


def primed(n):
    return n + PRIME

PADTOK = TOK + 4
LAT0 = CTX + 2
SPANS = ((0, CTX), (CTX, 512), (CTX + 512, 512))


class Steps:

    def __init__(self, eng, sem, per=0):
        self.eng, self.sem, self.per, self.base, self.n = eng, sem, per, 0, 0

    def at(self, i):
        self.base, self.n = i * self.per, 0

    def link(self, ins):
        self.n += 1
        ins.then_inc(self.sem, 1)
        self.eng.wait_ge(self.sem, primed(self.base + self.n))

    def end(self):
        assert self.n == self.per, f"{self.n} links in a pass, not {self.per}"


class Kernel:

    def __init__(self, nc, dram):
        self.nc, self.dram, self.ids = nc, dram, 0
        self.scopes, self.sems, self.unprimed = [], [], []

    @contextmanager
    def scope(self):
        with ExitStack() as stack:
            self.scopes.append(stack)
            self.sems.append([])
            yield stack
            self.scopes.pop()
        if sems := self.sems.pop():
            self.nc.clear_and_free_semaphores(sems)

    def sb(self, name, shape, dt=F32):
        self.ids += 1
        return self.scopes[-1].enter_context(self.nc.sbuf_tensor(f"{name}_{self.ids}", list(shape), dt))

    def sem(self, name, start=PRIME):
        self.ids += 1
        sem = self.nc.alloc_semaphore(f"{name}_{self.ids}")
        self.sems[-1].append(sem)
        if start:
            self.unprimed.append(sem)
        return sem

    def block(self):
        for sem in self.unprimed:
            self.nc.gpsimd.sem_inc(sem, PRIME)
        self.unprimed = []
        self.nc.all_engine_barrier()
        return self.scopes[-1].enter_context(self.nc.Block())


class Early:

    def __init__(self, k, name, order):
        self.src, self.order = k.dram[name][0].rearrange("(j p) n -> p j n", p=P), order
        self.w = k.sb(name, [P, KC, 512 * len(order)])
        self.w_in = k.sem(f"{name}_in")
        self.all_in = 16 * len(order)

    def load(self, sp):
        for g in self.order:
            at = slice(g * 512, (g + 1) * 512)
            sp.dma_start(self.w[:, :, at], self.src[:, :, at]).then_inc(self.w_in, 16)


def ds(i, n):
    return bass.ds(i, n)


def modulation(k, l, block=None, banks_free=None):
    nc, dr = k.nc, k.dram
    Q, NW = 4, 512
    GR = MODS * D // (Q * NW)
    RQ = range(Q)
    c = k.sb("c", [P, 2, KC])
    sc = k.sb("silu_c", [P, KC, 2])
    w = k.sb("ada_w", [P, KC, Q * NW])
    rows, bias, norms = k.sb("rows", [P, GR, NW]), k.sb("bias", [P, GR, NW]), k.sb("norms", [P, NW])
    c_in, c_silu, consts_in = k.sem("c_in", 0), k.sem("c_silu", 0), k.sem("consts_in", 0)
    w_in = [k.sem(f"ada_w_in{j}", 0) for j in range(KC)]
    piece_used = k.sem("piece_used", 0)
    run_taken, scaled, rows_out, h_in = k.sem("run_taken", 0), k.sem("scaled", 0), k.sem("rows_out", 0), k.sem("h_in", 0)
    scales = [((1 + 3 * n) * D // NW + half, n, half) for n in range(2) for half in range(2)]
    scales = {(run // Q, run % Q): (n, half) for run, n, half in scales}
    assert len({q for _, q in scales}) == Q
    block = block or k.block()

    @block.sync
    def _(sp):
        sp.dma_start(c[:, 0, :], dr["c_ctx"].rearrange("(p j) -> p j", p=P)).then_inc(c_in, 16)
        sp.dma_start(c[:, 1, :], dr["c"].rearrange("a (p j) -> (a p) j", p=P)).then_inc(c_in, 16)
        src = dr["ada_w"].rearrange("l (p j) (g n) -> l g p j n", p=P, g=GR)
        for g in range(GR):
            for j in range(KC):
                if g:
                    sp.wait_ge(piece_used, (g - 1) * KC + j + 1)
                sp.dma_start(w[:, j, :], src[l, g, :, j, :]).then_inc(w_in[j], 16)

    if l == 0:
        @block.gpsimd
        def _(pool):
            pool.dma_start(k.eye[:], dr["const_eye"]).then_inc(h_in, 16)
            pool.dma_start(k.tri[:], dr["const_tri"].rearrange("d p n -> p d n")).then_inc(h_in, 16)
            pool.dma_start(k.H[:, 0:CT, :], dr["ctx"].rearrange("b (t p) d -> p (b t) d", p=P)).then_inc(h_in, 16)
            pool.dma_start(k.H[:, CT:NT, :], dr["x"].rearrange("b (t p) d -> p (b t) d", p=P)).then_inc(h_in, 16)
            pool.wait_ge(h_in, 64)

    def bank(g, q):
        return k.bank[4 * ((g + 1) % 2) + q]

    @block.tensor
    def _(pe):
        pe.wait_ge(c_silu, 1)
        for g in range(GR):
            if g >= 2:
                pe.wait_ge(run_taken, Q * (g - 1))
            elif g == 1 and banks_free:
                pe.wait_ge(banks_free, primed(1))
            for j in range(KC):
                pe.wait_ge(w_in[j], (g + 1) * 16)
                for q in RQ:
                    mm = pe.matmul(bank(g, q)[32 * q:32 * q + 2, :], sc[:, j, :],
                                   w[:, j, q * NW:(q + 1) * NW], start=(j == 0), stop=(j == KC - 1))
                mm.then_inc(piece_used, 1)

    @block.scalar
    def _(act):
        act.wait_ge(c_in, 32)
        nc.scalar.activation(sc[:].rearrange("p j v -> p v j"), c[:], ACT.Silu).then_inc(c_silu, 1)
        b = dr["ada_b"][l:l + 1].rearrange("l (g q n) -> q l g n", q=Q, n=NW)
        for v in range(2):
            for q in RQ:
                act.dma_start(bias[32 * q + v:32 * q + v + 1], b[q]).then_inc(consts_in, 16)
            for (g, q), (n, half) in scales.items():
                act.dma_start(norms[32 * q + v:32 * q + v + 1, :],
                              dr[("norm_mix", "norm_ffn")[n]][l:l + 1, half * NW:(half + 1) * NW]).then_inc(consts_in, 16)
        mods = dr["mods"].rearrange("l v (g q n) -> l q v g n", q=Q, n=NW)
        act.wait_ge(scaled, Q)
        act.wait_ge(run_taken, Q * GR)
        for q in RQ:
            act.dma_start(mods[l, q], rows[32 * q:32 * q + 2]).then_inc(rows_out, 16)
        act.wait_ge(rows_out, Q * 16)

    @block.vector
    def _(dve):
        dve.wait_ge(consts_in, 16 * 16)
        for g in range(GR):
            dve.wait_ge(piece_used, (g + 1) * KC)
            for q in RQ:
                on = slice(32 * q, 32 * q + 2)
                nc.vector.tensor_tensor(rows[on, g, :], bank(g, q)[on, :], bias[on, g, :], ALU.add).then_inc(run_taken, 1)
            for q in RQ:
                if (g, q) in scales:
                    on = slice(32 * q, 32 * q + 2)
                    dve.wait_ge(run_taken, Q * g + q + 1)
                    nc.vector.scalar_tensor_tensor(out=rows[on, g, :], in0=rows[on, g, :], scalar=1.0,
                                                   in1=norms[on, :], op0=ALU.add, op1=ALU.mult).then_inc(scaled, 1)


def spread_row(k, eng, dst, l, v, m, done):
    row = k.dram["mods"][l, v:v + 1, m * D:(m + 1) * D]
    eng.dma_start(dst, row.to_broadcast([P, D])).then_inc(done, 16)


def norm_mod(k, l, which, first, aT=None, logits=None, early=None):
    nc, dr, H = k.nc, k.dram, k.H
    vs = (0, 1) if first == 0 else (1,)
    A = k.sb("scale_rows", [P, 2, D])
    S = k.sb("shift_rows", [P, 2, D])
    sq = k.sb("squares", [P, 3, D])
    rstd = k.sb("rstd", [P, NT])
    a = [k.sb(f"a{u}", [P, D]) for u in range(2)]
    rows_in, sumsq_ready, a_ready = k.sem("rows_in"), k.sem("sumsq_ready"), k.sem("a_ready")
    a_turned, aT_ready = k.sem("a_turned"), k.sem("aT_ready")
    a_stored = [k.sem(f"a_stored{u}") for u in range(2)]
    order, mean_ready, root_ready = k.sem("dve_order"), k.sem("mean_ready"), k.sem("root_ready")
    dve_sums, rstd_ready = k.sem("dve_sums"), k.sem("rstd_ready")
    moe = logits is not None
    NL = GROUPS + NE
    if moe:
        wr = k.sb("w_route", [P, KC, NL])
        fT = k.sb("fT", [P, 2, KC, P])
        logits_ready, logits_taken = k.sem("logits_ready"), k.sem("logits_taken")
    block = k.block()

    def passes(eng, body):
        if first == 0:
            body(0, 0, 0)
        with eng.Fori(1, NT // 2) as i:
            body(i, i if first == 0 else i - 1, 1)

    @block.sync
    def _(sp):
        for v in vs:
            spread_row(k, sp, A[:, v, :], l, v, 1 + 3 * which, rows_in)
            spread_row(k, sp, S[:, v, :], l, v, 3 * which, rows_in)
        if early:
            early.load(sp)
        if moe:
            sp.dma_start(wr[:, :, 0:GROUPS],
                         dr["moe_w_group"][l].rearrange("(j p) n -> p j n", p=P)).then_inc(rows_in, 16)
            sp.dma_start(wr[:, :, GROUPS:],
                         dr["moe_w_expert"][l].rearrange("(j p) n -> p j n", p=P)).then_inc(rows_in, 16)

            def body(i, n, v):
                for u in range(2):
                    sp.wait_ge(a_ready, primed(2 * n + u + 1))
                    sp.dma_start(dr["moe_x"][ds(i * 2 * P + u * P, P), :], a[u][:]).then_inc(a_stored[u], 16)
            passes(sp, body)
            for u in range(2):
                sp.wait_ge(a_stored[u], primed(8 * (NT - first)))

    @block.scalar
    def _(act):
        for n, t in enumerate(t for t in range(first, NT) if t % 3 != 2):
            if n >= 2:
                act.wait_ge(sumsq_ready, primed(n - 1))
            nc.scalar.activation(sq[:, n % 2, :], H[:, t, :], ACT.Square, accum_out=rstd[:, t:t + 1]).then_inc(sumsq_ready, 1)
        act.wait_ge(mean_ready, primed(1))
        nc.scalar.activation(rstd[:, first:], rstd[:, first:], ACT.Sqrt).then_inc(root_ready, 1)

        def body(i, n, v):
            for u in range(2):
                act.wait_ge(a_turned, primed(2 + 2 * n + u + 1))
                if moe:
                    act.wait_ge(logits_ready, primed(2 + 2 * n + u - 1))
                for half in range(2):
                    src = k.bank[2 * u + half][:].rearrange("p (c q) -> p c q", c=4)
                    if moe:
                        dst = fT[:, u, 4 * half:4 * half + 4, :]
                    else:
                        dst = aT[:, 4 * half:4 * half + 4, ds(i * (2 * P) + u * P, P)]
                    nc.scalar.copy(dst, src).then_inc(aT_ready, 1)
            if moe:
                for u in range(2):
                    act.wait_ge(logits_ready, primed(2 + 2 * n + u + 1))
                    nc.scalar.copy(logits[:, ds(i * 2 + u - first, 1), :].rearrange("p a e -> p (a e)"),
                                   k.bank[4 + u][:, 0:NL]).then_inc(logits_taken, 1)
        passes(act, body)

    @block.vector
    def _(dve):
        mine = [t for t in range(first, NT) if t % 3 == 2]
        for n, t in enumerate(mine):
            if n:
                dve.wait_ge(dve_sums, primed(n))
            nc.vector.tensor_tensor_reduce(out=sq[:, 2, :], in0=H[:, t, :], in1=H[:, t, :], scale=1.0, scalar=0.0,
                                           op0=ALU.mult, op1=ALU.add, accum_out=rstd[:, t:t + 1]).then_inc(dve_sums, 1)
        dve.wait_ge(dve_sums, primed(len(mine)))
        dve.wait_ge(sumsq_ready, primed(NT - first - len(mine)))
        nc.vector.tensor_scalar(rstd[:, first:], rstd[:, first:], 1.0 / D, EPS, ALU.mult, ALU.add).then_inc(mean_ready, 1)
        dve.wait_ge(root_ready, primed(1))
        nc.vector.reciprocal(rstd[:, first:], rstd[:, first:]).then_inc(rstd_ready, 1)
        dve.wait_ge(rstd_ready, primed(1))
        dve.wait_ge(rows_in, primed(16 * (2 * len(vs) + 2 * moe)))
        st = Steps(dve, order, 2)

        def body(i, n, v):
            st.at(n)
            for u in range(2):
                r = rstd[:, ds(i * 2 + u, 1)]
                dve.wait_ge(a_turned, primed(2 + 2 * n + u - 1))
                if moe:
                    dve.wait_ge(a_stored[u], primed(n * 16))
                st.link(nc.vector.scalar_tensor_tensor(
                    out=a[u][:], in0=H[:, ds(i * 2 + u, 1), :].rearrange("p a d -> p (a d)"), scalar=r,
                    in1=A[:, v, :], op0=ALU.mult, op1=ALU.mult))
                nc.vector.tensor_tensor(a[u][:], a[u][:], S[:, v, :], ALU.add).then_inc(a_ready, 1)
            st.end()
        passes(dve, body)

    @block.tensor
    def _(pe):
        pe.sem_inc(a_turned, 2)
        if moe:
            pe.sem_inc(logits_ready, 2)

        def body(i, n, v):
            pe.wait_ge(aT_ready, primed(4 * n))
            for u in range(2):
                pe.wait_ge(a_ready, primed(2 * n + u + 1))
                for c in range(KC):
                    t = pe.transpose(k.bank[2 * u + c // 4][:, (c % 4) * P:(c % 4 + 1) * P],
                                     a[u][:, c * P:(c + 1) * P], k.eye[:])
                t.then_inc(a_turned, 1)
            if moe:
                pe.wait_ge(logits_taken, primed(2 * n))
                for u in range(2):
                    pe.wait_ge(aT_ready, primed(4 * n + 2 * u + 2))
                    for c in range(KC):
                        mm = pe.matmul(k.bank[4 + u][:, 0:NL], fT[:, u, c, :], wr[:, c, :],
                                       start=(c == 0), stop=(c == KC - 1))
                    mm.then_inc(logits_ready, 1)
        passes(pe, body)


def project0(k, aT):
    nc, dr = k.nc, k.dram
    PARTS = 7
    QC, ALPHA = 3 * W0, 4 * W0
    SC = ALPHA + 4 * NH
    COLS = (0, W0, 2 * W0, QC, SC + W0, SC + 2 * W0, SC)
    w = [k.sb(f"w{j}", [P, KC, P]) for j in range(PARTS)]
    wab = k.sb("w_ab", [P, KC, 4 * NH])
    cq = k.sb("conv_qkv", [P, 3, 3 * NH])
    csc = k.sb("conv_sc", [P, 3, NH])
    x = k.sb("x_raw", [P, PADTOK])
    y = k.sb("y", [P, PADTOK])
    z = k.sb("z", [P, PADTOK])
    bt = k.sb("by_token", [P, NT, P])
    ones, zero = k.sb("ones", [P, P]), k.sb("zero", [P, D])
    zero_set, cleared = k.sem("zero_set"), k.sem("cleared", 0)
    r = k.sb("inv_norm", [P, 2, 512])
    w_in = [k.sem(f"w_in{j}") for j in range(PARTS)]
    w_used = [k.sem(f"w_used{j}") for j in range(PARTS)]
    wab_in = k.sem("w_ab_in")
    consts_in, ones_set, pads_set = k.sem("consts_in"), k.sem("ones_set"), k.sem("pads_set")
    z_ready = [k.sem(f"z_ready{s}") for s in range(2)]
    z_copied = [k.sem(f"z_copied{s}") for s in range(2)]
    z_gated = [k.sem(f"z_gated{s}") for s in range(2)]
    ab_ready, ab_taken = k.sem("ab_ready"), k.sem("ab_taken")
    conv_ready, silu_ready = k.sem("conv_ready"), k.sem("silu_ready")
    sq_ready, norm_ready, norm_taken = k.sem("sq_ready"), k.sem("norm_ready"), k.sem("norm_taken")
    y_ready, y_stored = k.sem("y_ready"), k.sem("y_stored", 0)
    bt_free = k.sem("bt_free")
    turn_taken, bt_stored = k.sem("turn_taken"), k.sem("bt_stored", 0)
    order, root_ready = k.sem("dve_order"), k.sem("root_ready")
    block = k.block()

    def use(j):
        return j // 2

    CNT = (4, 3)
    COPIED = (3, 2)
    AUX = 12

    @block.sync
    def _(sp):
        sp.dma_start(wab[:], dr["ab_w_in"][0, :, ALPHA:SC].rearrange("(j p) n -> p j n", p=P)).then_inc(wab_in, 16)
        src = dr["ab_w_in"][0].rearrange("(j p) n -> p j n", p=P)
        for j in range(PARTS):
            sp.dma_start(w[j][:], src[:, :, COLS[j]:COLS[j] + P]).then_inc(w_in[j], 16)
            if j == 1:
                for t in range(3):
                    sp.dma_start(cq[:, t, :], dr["ab_conv_qkv"][0, t].rearrange("(c p) -> p c", p=P),
                                 allow_slow_non_contiguous=True).then_inc(consts_in, 16)
                    sp.dma_start(csc[:, t, :], dr["ab_conv_sc"][0, t].rearrange("(c p) -> p c", p=P),
                                 allow_slow_non_contiguous=True).then_inc(consts_in, 16)
        with sp.Fori(1, NH) as h:
            for j in range(PARTS):
                sp.wait_ge(z_ready[j % 2], primed((h - 1) * CNT[j % 2] + use(j) + 1))
                sp.dma_start(w[j][:], src[:, :, ds(h * P + COLS[j], P)]).then_inc(w_in[j], 16)

    def store_channels(eng, part, h):
        out = dr["heads"][part]
        eng.dma_start(out[0:CT, :, ds(h * P, P)].rearrange("t p n -> p t n"),
                      z[:, 0:CTX].rearrange("p (t n) -> p t n", n=P)).then_inc(y_stored, 16)
        eng.dma_start(out[CT:NT, :, ds(h * P, P)].rearrange("t p n -> p t n"),
                      z[:, LAT0:LAT0 + SEQ].rearrange("p (t n) -> p t n", n=P)).then_inc(y_stored, 16)

    @block.gpsimd
    def _(pool):
        nc.gpsimd.memset(ones[:], 1.0).then_inc(ones_set, 1)
        nc.gpsimd.memset(zero[:], 0.0).then_inc(zero_set, 1)
        pool.wait_ge(zero_set, primed(1))
        more = dr["moe_y"][2 * NT * P:SLOTS, :].rearrange("(b p) d -> p b d", p=P)
        pool.dma_start(more, zero[:].unsqueeze(1).to_broadcast([P, MAXP - 2 * NT, D])).then_inc(cleared, 16)
        with pool.Fori(0, NH) as h:
            for n, part in enumerate((0, 1)):
                pool.wait_ge(y_ready, primed(h * 2 + n + 1))
                store_channels(pool, part, h)
            for n, part in enumerate((2, 3)):
                pool.wait_ge(turn_taken, primed(h * 6 + 3 * n + 3))
                pool.dma_start(dr["heads"][part, :, :, ds(h * P, P)].rearrange("t p n -> p t n"),
                               bt[:]).then_inc(bt_stored, 16)
                pool.wait_ge(bt_stored, h * 32 + 16 * n + 16)
                pool.sem_inc(bt_free, 1)
        pool.wait_ge(y_stored, NH * 64)
        pool.wait_ge(bt_stored, NH * 32)
        pool.wait_ge(cleared, 16)

    @block.tensor
    def _(pe):
        pe.wait_ge(wab_in, primed(16))
        pe.wait_ge(ones_set, primed(1))
        for t in range(NT):
            for j in range(KC):
                mm = pe.matmul(k.bank[7][:, t * 4 * NH:(t + 1) * 4 * NH], aT[:, j, t * P:(t + 1) * P], wab[:, j, :],
                               start=(j == 0), stop=(j == KC - 1))
        mm.then_inc(ab_ready, 1)
        pe.wait_ge(ab_taken, primed(1))

        def part(h, j):
            s = j % 2
            pe.wait_ge(w_in[j], primed((h + 1) * 16))
            pe.wait_ge(z_copied[s], primed(h * COPIED[s] + use(j)))
            pe.wait_ge(z_gated[s], primed(h))
            for n, (at, width) in enumerate(SPANS):
                for c in range(KC):
                    mm = pe.matmul(k.bank[3 * s + n][:, 0:width], w[j][:, c, :], aT[:, c, at:at + width],
                                   start=(c == 0), stop=(c == KC - 1))
            mm.then_inc(z_ready[s], 1)

        def aux(h, m):
            pe.wait_ge(norm_taken, primed(h * 6 + min(max(m - 1, 0), 6)))
            pe.wait_ge(turn_taken, primed(h * 6 + max(m - 7, 0)))
            return k.bank[6 + m % 2]

        def norms(h, n):
            pe.wait_ge(sq_ready, primed(h * 2 + n + 1))
            for s, (at, width) in enumerate(SPANS):
                at += 2 if s else 0
                pe.matmul(aux(h, 3 * n + s)[:, 0:width], ones[:], y[:, at:at + width],
                          start=True, stop=True).then_inc(norm_ready, 1)

        def turns(h, n):
            if n == 0:
                pe.wait_ge(y_ready, primed(h * 2 + 2))
            else:
                pe.wait_ge(silu_ready, primed(h * 3 + 3))
            for g in range(3):
                to = aux(h, 6 + 3 * n + g)
                for q in range(min(4, NT - 4 * g)):
                    t = 4 * g + q
                    at = t * P + (2 if t >= CT else 0)
                    mm = pe.transpose(to[:, q * P:(q + 1) * P], z[:, at:at + P], k.eye[:])
                mm.then_inc(norm_ready, 1)

        with pe.Fori(0, NH) as h:
            part(h, 0)
            part(h, 1)
            norms(h, 0)
            part(h, 2)
            norms(h, 1)
            part(h, 3)
            turns(h, 0)
            part(h, 4)
            turns(h, 1)
            part(h, 5)
            part(h, 6)

    @block.scalar
    def _(act):
        act.wait_ge(ab_ready, primed(1))
        nc.scalar.copy(k.ab[:].rearrange("p t n -> p (t n)"), k.bank[7][:, 0:NT * 4 * NH]).then_inc(ab_taken, 1)
        act.wait_ge(pads_set, primed(1))

        def raw(h, j, dst):
            s = j % 2
            act.wait_ge(z_ready[s], primed(h * CNT[s] + use(j) + 1))
            for n, (at, width) in enumerate(SPANS):
                at += 3 if n else 1
                c = nc.scalar.copy(dst[:, at:at + width], k.bank[3 * s + n][:, 0:width])
            c.then_inc(z_copied[s], 1)

        def silu(h, n):
            act.wait_ge(conv_ready, primed(h * 4 + n + 1))
            nc.scalar.activation(z[:, 0:PADTOK - 2], y[:, 0:PADTOK - 2], ACT.Silu).then_inc(silu_ready, 1)

        def square(h, n):
            act.wait_ge(silu_ready, primed(h * 3 + n + 1))
            nc.scalar.activation(y[:, 0:PADTOK - 2], z[:, 0:PADTOK - 2], ACT.Square).then_inc(sq_ready, 1)
            for s, (_, width) in enumerate(SPANS):
                m = 3 * n + s
                act.wait_ge(norm_taken, primed(h * 6 + m + 1))
                nc.scalar.activation(r[:, m % 2, 0:width], r[:, m % 2, 0:width], ACT.Sqrt).then_inc(root_ready, 1)

        def take_turns(h, n):
            act.wait_ge(bt_free, primed(h * 2 + n))
            for g in range(3):
                act.wait_ge(norm_ready, primed(h * AUX + 6 + 3 * n + g + 1))
                tiles = min(4, NT - 4 * g)
                nc.scalar.copy(bt[:, 4 * g:4 * g + tiles, :].rearrange("p t n -> p (t n)"),
                               k.bank[6 + g % 2 if n == 0 else 7 - g % 2][:, 0:tiles * P]).then_inc(turn_taken, 1)

        with act.Fori(0, NH) as h:
            raw(h, 0, x)
            act.wait_ge(z_gated[1], primed(h))
            silu(h, 0)
            square(h, 0)
            act.wait_ge(conv_ready, primed(h * 4 + 1))
            raw(h, 1, x)
            act.wait_ge(y_stored, h * 64 + 32)
            silu(h, 1)
            square(h, 1)
            raw(h, 2, x)
            act.wait_ge(z_ready[1], primed(h * CNT[1] + use(3) + 1))
            for m, (at, width) in enumerate(SPANS):
                c = nc.scalar.activation(k.gate[:, ds(h, 1), at:at + width].rearrange("p a n -> p (a n)"),
                                         k.bank[3 + m][:, 0:width], ACT.Silu)
            c.then_inc(z_copied[1], 1)
            take_turns(h, 0)
            act.wait_ge(y_stored, h * 64 + 64)
            silu(h, 2)
            take_turns(h, 1)
            raw(h, 4, z)

    @block.vector
    def _(dve):
        for at in (0, CTX + 1, PADTOK - 1):
            m = nc.vector.memset(x[:, at:at + (2 if at == CTX + 1 else 1)], 0.0)
        m.then_inc(pads_set, 1)
        dve.wait_ge(consts_in, primed(16 * 6))
        st = Steps(dve, order, 4 * 2 + 2 * 5)
        N = PADTOK - 2

        def conv(h, taps, col):
            c = taps[:, :, ds(h + col, 1)].rearrange("p t a -> p (t a)")
            st.link(nc.vector.tensor_scalar(y[:, 0:N], x[:, 0:N], c[:, 0:1], None, ALU.mult))
            st.link(nc.vector.scalar_tensor_tensor(out=y[:, 0:N], in0=x[:, 1:N + 1], scalar=c[:, 1:2],
                                                   in1=y[:, 0:N], op0=ALU.mult, op1=ALU.add))
            nc.vector.scalar_tensor_tensor(out=y[:, 0:N], in0=x[:, 2:N + 2], scalar=c[:, 2:3],
                                           in1=y[:, 0:N], op0=ALU.mult, op1=ALU.add).then_inc(conv_ready, 1)

        def normalise(h, n, scale):
            for s, (at, width) in enumerate(SPANS):
                at += 2 if s else 0
                m = 3 * n + s
                dve.wait_ge(norm_ready, primed(h * AUX + m + 1))
                nc.vector.tensor_scalar(r[:, m % 2, 0:width], k.bank[6 + m % 2][:, 0:width], EPS, None,
                                        ALU.add).then_inc(norm_taken, 1)
                dve.wait_ge(root_ready, primed(h * 6 + m + 1))
                st.link(nc.vector.reciprocal(r[:, m % 2, 0:width], r[:, m % 2, 0:width]))
                c = nc.vector.scalar_tensor_tensor(out=z[:, at:at + width], in0=z[:, at:at + width],
                                                   scalar=scale, in1=r[:, m % 2, 0:width], op0=ALU.mult, op1=ALU.mult)
                if s < 2:
                    st.link(c)
            c.then_inc(y_ready, 1)

        with dve.Fori(0, NH) as h:
            st.at(h)
            dve.wait_ge(z_copied[0], primed(h * 3 + 1))
            conv(h, cq, 0)
            normalise(h, 0, P ** -0.5)
            dve.wait_ge(z_copied[1], primed(h * 2 + 1))
            conv(h, cq, NH)
            normalise(h, 1, 1.0)
            dve.wait_ge(z_copied[0], primed(h * 3 + 2))
            conv(h, cq, 2 * NH)
            dve.wait_ge(z_copied[0], primed(h * 3 + 3))
            dve.wait_ge(z_ready[1], primed(h * CNT[1] + 3))
            for n, (at, width) in enumerate(SPANS):
                at += 3 if n else 1
                c = nc.vector.tensor_tensor(x[:, at:at + width], z[:, at:at + width],
                                            k.bank[3 + n][:, 0:width], ALU.mult)
            c.then_inc(z_gated[1], 1)
            dve.wait_ge(z_gated[1], primed(h + 1))
            dve.wait_ge(silu_ready, primed(h * 3 + 3))
            conv(h, csc, 0)
            dve.wait_ge(conv_ready, primed(h * 4 + 4))
            dve.wait_ge(z_ready[0], primed(h * CNT[0] + 4))
            for n, (at, width) in enumerate(SPANS):
                c = nc.vector.tensor_tensor(k.short[:, ds(h, 1), at:at + width].rearrange("p a n -> p (a n)"),
                                            y[:, at + (2 if n else 0):at + (2 if n else 0) + width],
                                            k.bank[n][:, 0:width], ALU.mult)
            c.then_inc(z_gated[0], 1)
            st.end()


def delta_scan(k, oT):
    nc, dr = k.nc, k.dram
    R2 = range(2)
    merge = k.sb("merge", [P, 2, LEVELS, P])
    ones = k.sb("ones", [P, P])
    alog = k.sb("a_log", [P, 2 * NH])
    dtb = k.sb("dt_bias", [P, 2 * NH])
    ST = [P, NT, 2 * NH]
    la, beta, g, tot = k.sb("log_a", ST), k.sb("beta", ST), k.sb("g", ST), k.sb("g_total", ST)
    beg, kdec, egl, tmp = k.sb("beta_eg", ST), k.sb("k_decay", ST), k.sb("eg_total", ST), k.sb("tmp", ST)

    def per_dir(name):
        return [k.sb(f"{name}{d}", [P, NH, P]) for d in R2]

    def per_step(name):
        return [[k.sb(f"{name}{d}{u}", [P, NH, P]) for u in R2] for d in R2]

    KT, QT, K, V = per_step("KT"), per_step("QT"), per_step("K"), per_dir("V")
    GU, BI, Dc, EG = per_dir("g_rows_in"), per_dir("b_rows_in"), per_dir("decay"), per_dir("eg_rows")
    Dm, AT, KQ = per_dir("decay_masked"), per_dir("AT"), per_dir("KQ")
    DB = k.sb("decay_beta", [P, NH, P])
    T, TT, Pm, QTd = per_dir("T"), per_dir("TT"), per_dir("A_T_off"), per_dir("QT_decayed")
    VB, R, VN, VD, S = per_dir("V_beta"), per_dir("R"), per_dir("v_new"), per_dir("v_decayed"), per_dir("S")

    consts_in, ones_set, state_set, stats = k.sem("consts_in"), k.sem("ones_set"), k.sem("state_set"), k.sem("stats")
    prep_act, prep_pe, prep_order = k.sem("prep_act"), k.sem("prep_pe"), k.sem("prep_order")

    def sems(name):
        return [k.sem(f"{name}{d}") for d in R2]

    tile_in, rows_in = [[k.sem(f"tile_in{d}{u}") for u in R2] for d in R2], sems("rows_in")
    v_in = sems("v_in")
    g_rows, kk_ready, a_turned, p_ready, dt_ready = (sems(n) for n in ("g_rows", "kk_ready", "a_turned", "p_ready", "dt_ready"))
    ks_ready, vn_ready, o_ready, ds_ready = (sems(n) for n in ("ks_ready", "vn_ready", "o_ready", "ds_ready"))
    e_ready, at_ready, kq_ready, t_ready, pm_ready = (sems(n) for n in ("e_ready", "at_ready", "kq_ready", "t_ready", "pm_ready"))
    tt_ready, r_ready, vd_ready, o_added, s_ready = (sems(n) for n in ("tt_ready", "r_ready", "vd_ready", "o_added", "s_ready"))
    eg_ready, d_ready, vn_copied = (sems(n) for n in ("eg_ready", "d_ready", "vn_copied"))
    dm_ready, qtd_ready, vb_ready, tt0_ready, s_scaled = (sems(n) for n in ("dm_ready", "qtd_ready", "vb_ready", "tt0_ready", "s_scaled"))
    order, pool_order = k.sem("dve_order"), k.sem("pool_order")
    MERGES = LEVELS - 1
    bank = [[k.bank[4 * d + n][:].rearrange("p (h n) -> p h n", h=NH) for n in range(4)] for d in R2]
    flat = [[k.bank[4 * d + n] for n in range(4)] for d in R2]
    block = k.block()

    assert CT == 2

    def passes(eng, body):
        for s in range(CT):
            body(s, 0, s, (s, CT - 1 - s))
        with eng.Fori(1, NT // 2) as i:
            for u in R2:
                s = eng.snap(i * 2 + u, min_val=CT, max_val=NT - 1)
                body(s, i, u, (s, eng.snap(i * -2 + (NT + CT - 1 - u), min_val=CT, max_val=NT - 1)))

    def stat(x, t, d):
        return (x[:, ds(t, 1), NH * d:NH * d + NH].rearrange("p a h -> p (a h)").unsqueeze(2)
                .to_broadcast([P, NH, P]))

    def all_heads(x):
        return x.unsqueeze(1).to_broadcast([P, NH, P])

    def half(x, n, second):
        return x.rearrange("p h (b t s) -> p (h b) t s", t=2, s=2 << n)[:, :, second, :]

    @block.sync
    def _(sp):
        sp.dma_start(merge[:], dr["const_merge"].rearrange("d l p n -> p d l n")).then_inc(consts_in, 16)
        sp.dma_start(alog[:], dr["ab_a_log"].rearrange("a d h -> a (d h)").to_broadcast([P, 2 * NH])).then_inc(consts_in, 16)
        sp.dma_start(dtb[:], dr["ab_dt_bias"].rearrange("a d h -> a (d h)").to_broadcast([P, 2 * NH])).then_inc(consts_in, 16)

        def body(s, i, u, tiles):
            for d in R2:
                if not isinstance(s, int):
                    sp.wait_ge(ds_ready[d], primed(s - 1))
                    sp.wait_ge(qtd_ready[d], primed(s - 1))
                for part, dst in enumerate((QT, KT, K)):
                    sp.dma_start(dst[d][u][:].rearrange("p h n -> p (h n)"),
                                 dr["heads"][part, ds(tiles[d], 1)].rearrange("a p n -> p (a n)")).then_inc(tile_in[d][u], 16)
            for d in R2:
                sp.wait_ge(vb_ready[d], primed(s))
                sp.dma_start(V[d][:].rearrange("p h n -> p (h n)"),
                             dr["heads"][3, ds(tiles[d], 1)].rearrange("a p n -> p (a n)")).then_inc(v_in[d], 16)
        passes(sp, body)

    @block.gpsimd
    def _(pool):
        nc.gpsimd.memset(ones[:], 1.0).then_inc(ones_set, 1)
        nc.gpsimd.memset(oT[:], 0.0).then_inc(state_set, 1)
        for d in R2:
            nc.gpsimd.memset(S[d][:], 0.0).then_inc(state_set, 1)
        pool.wait_ge(stats, primed(1))

        def body(s, i, u, tiles):
            for d in R2:
                pool.wait_ge(g_rows[d], primed(s))
                nc.gpsimd.tensor_tensor(GU[d][:], all_heads(k.tri[:, d, :]), stat(la, tiles[d], d), ALU.mult).then_inc(rows_in[d], 1)
                nc.gpsimd.tensor_tensor(BI[d][:], all_heads(k.eye[:]), stat(beta, tiles[d], d), ALU.mult).then_inc(rows_in[d], 1)
            for d in R2:
                pool.wait_ge(d_ready[d], primed(s + 1))
                pool.wait_ge(kq_ready[d], primed(s))
                nc.gpsimd.tensor_tensor(Dm[d][:], Dc[d][:], all_heads(k.tri[:, d, :]), ALU.mult).then_inc(dm_ready[d], 1)
            for d in R2:
                pool.wait_ge(at_ready[d], primed(s + 1))
                pool.wait_ge(vn_ready[d], primed(s))
                nc.gpsimd.tensor_tensor(TT[d][:], AT[d][:], all_heads(merge[:, 1 - d, 0, :]), ALU.mult).then_inc(pool_order, 1)
                pool.wait_ge(pool_order, primed(s * 2 + d + 1))
                nc.gpsimd.tensor_tensor(TT[d][:], all_heads(k.eye[:]), TT[d][:], ALU.subtract).then_inc(tt0_ready[d], 1)
            for d in R2:
                pool.wait_ge(tile_in[d][u], primed((i + 1) * 48))
                pool.wait_ge(v_in[d], primed((s + 1) * 16))
                pool.wait_ge(eg_ready[d], primed(s + 1))
                pool.wait_ge(r_ready[d], primed(s))
                pool.wait_ge(o_ready[d], primed(s))
                nc.gpsimd.tensor_tensor(QTd[d][:], QT[d][u][:], EG[d][:], ALU.mult).then_inc(qtd_ready[d], 1)
                nc.gpsimd.tensor_tensor(VB[d][:], V[d][:], stat(beta, tiles[d], d), ALU.mult).then_inc(vb_ready[d], 1)
            for d in R2:
                pool.wait_ge(o_ready[d], primed(s + 1))
                nc.gpsimd.tensor_tensor(S[d][:], S[d][:], stat(egl, tiles[d], d), ALU.mult).then_inc(s_scaled[d], 1)
        passes(pool, body)

    @block.scalar
    def _(act):
        act.wait_ge(prep_order, primed(1))
        nc.scalar.activation(tmp[:], la[:], ACT.Abs).then_inc(prep_act, 1)
        act.wait_ge(prep_act, primed(1))
        nc.scalar.activation(tmp[:], tmp[:], ACT.Exp, scale=-1.0).then_inc(prep_act, 1)
        act.wait_ge(prep_act, primed(2))
        nc.scalar.activation(tmp[:], tmp[:], ACT.Ln, bias=1.0).then_inc(prep_act, 1)
        nc.scalar.activation(beta[:], k.ab[:, :, 2 * NH:], ACT.Sigmoid).then_inc(prep_act, 1)
        act.wait_ge(consts_in, primed(48))
        nc.scalar.activation(alog[:], alog[:], ACT.Exp).then_inc(prep_act, 1)
        act.wait_ge(prep_order, primed(6))
        nc.scalar.activation(kdec[:], kdec[:], ACT.Exp).then_inc(prep_act, 1)
        nc.scalar.activation(egl[:], tot[:], ACT.Exp).then_inc(prep_act, 1)
        nc.scalar.activation(tmp[:], g[:], ACT.Exp).then_inc(prep_act, 1)

        def body(s, i, u, tiles):
            for d in R2:
                act.wait_ge(g_rows[d], primed(s + 1))
                act.wait_ge(qtd_ready[d], primed(s))
                nc.scalar.activation(EG[d][:], bank[d][0], ACT.Exp).then_inc(eg_ready[d], 1)
            for d in R2:
                act.wait_ge(e_ready[d], primed(s + 1))
                nc.scalar.activation(Dc[d][:], Dc[d][:], ACT.Exp).then_inc(d_ready[d], 1)
            for d in R2:
                act.wait_ge(vn_ready[d], primed(s + 1))
                act.wait_ge(o_ready[d], primed(s))
                nc.scalar.copy(VN[d][:], bank[d][1]).then_inc(vn_copied[d], 1)
        passes(act, body)

    @block.vector
    def _(dve):
        dve.wait_ge(consts_in, primed(48))
        prep = Steps(dve, prep_order)
        bias = dtb[:].unsqueeze(1).to_broadcast(ST)
        prep.link(nc.vector.tensor_tensor(la[:], k.ab[:, :, 0:2 * NH], bias, ALU.add))
        dve.wait_ge(prep_act, primed(3))
        prep.link(nc.vector.scalar_tensor_tensor(out=la[:], in0=la[:], scalar=0.0, in1=tmp[:], op0=ALU.max, op1=ALU.add))
        dve.wait_ge(prep_act, primed(5))
        prep.link(nc.vector.scalar_tensor_tensor(out=la[:], in0=la[:], scalar=-1.0,
                                                 in1=alog[:].unsqueeze(1).to_broadcast(ST), op0=ALU.mult, op1=ALU.mult))
        dve.wait_ge(prep_pe, primed(1))
        for d in R2:
            prep_copy = nc.vector.tensor_copy(g[:, :, NH * d:NH * d + NH],
                                              flat[0][d][:, 0:NT * NH].rearrange("p (t h) -> p t h", t=NT))
            if d == 1:
                prep.link(prep_copy)
        prep.link(nc.vector.tensor_copy(tot[:], flat[0][2][:, 0:2 * NT * NH].rearrange("p (t h) -> p t h", t=NT)))
        prep.link(nc.vector.tensor_tensor(kdec[:], tot[:], g[:], ALU.subtract))
        dve.wait_ge(prep_act, primed(8))
        prep.link(nc.vector.tensor_tensor(beg[:], tmp[:], beta[:], ALU.mult))
        dve.sem_inc(stats, 1)
        dve.wait_ge(state_set, primed(3))
        st = Steps(dve, order, 2 * (1 + 1 + 1 + 1))

        def body(s, i, u, tiles):
            st.at(s)
            for d in R2:
                dve.wait_ge(eg_ready[d], primed(s + 1))
                dve.wait_ge(dm_ready[d], primed(s))
                st.link(nc.vector.tensor_tensor(Dc[d][:], bank[d][0], stat(g, tiles[d], d), ALU.subtract))
                nc.vector.tensor_scalar(Dc[d][:], Dc[d][:], 0.0, None, ALU.min).then_inc(e_ready[d], 1)
            for d in R2:
                dve.wait_ge(d_ready[d], primed(s + 1))
                dve.wait_ge(at_ready[1 - d], primed(s + d))
                st.link(nc.vector.tensor_tensor(DB[:], Dc[d][:], bank[d][1], ALU.mult))
                dve.wait_ge(kk_ready[d], primed(s + 1))
                nc.vector.tensor_tensor(AT[d][:], DB[:], bank[d][2], ALU.mult).then_inc(at_ready[d], 1)
                dve.wait_ge(dm_ready[d], primed(s + 1))
                nc.vector.tensor_tensor(KQ[d][:], Dm[d][:], bank[d][3], ALU.mult).then_inc(kq_ready[d], 1)
            for d in R2:
                dve.wait_ge(a_turned[d], primed(s + 1))
                st.link(nc.vector.tensor_tensor(T[d][:], bank[d][0], all_heads(merge[:, d, 0, :]), ALU.mult))
                nc.vector.tensor_tensor(T[d][:], all_heads(k.eye[:]), T[d][:], ALU.subtract).then_inc(t_ready[d], 1)
            for n in range(MERGES):
                for d in R2:
                    dve.wait_ge(p_ready[d], primed(s * MERGES + n + 1))
                    nc.vector.tensor_tensor(Pm[d][:], bank[d][1], all_heads(merge[:, d, n + 1, :]),
                                            ALU.mult).then_inc(pm_ready[d], 1)
                for d in R2:
                    dve.wait_ge(dt_ready[d], primed(s * MERGES + n + 1))
                    if n == 0:
                        dve.wait_ge(tt0_ready[d], primed(s + 1))
                        dve.wait_ge(t_ready[d], primed(s + 1))
                    else:
                        dve.wait_ge(tt_ready[d], primed(s * MERGES + n))
                    if n < MERGES - 1:
                        t = half(T[d][:], n, d)
                        nc.vector.tensor_tensor(t, t, half(bank[d][2], n, d), ALU.subtract)
                    t = half(TT[d][:], n, 1 - d)
                    nc.vector.tensor_tensor(t, t, half(bank[d][3], n, 1 - d), ALU.subtract).then_inc(tt_ready[d], 1)
            for d in R2:
                dve.wait_ge(ks_ready[d], primed(s + 1))
                st.link(nc.vector.tensor_tensor(R[d][:], bank[d][0], stat(beg, tiles[d], d), ALU.mult))
                dve.wait_ge(vb_ready[d], primed(s + 1))
                nc.vector.tensor_tensor(R[d][:], VB[d][:], R[d][:], ALU.subtract).then_inc(r_ready[d], 1)
            for d in R2:
                dve.wait_ge(vn_copied[d], primed(s + 1))
                nc.vector.tensor_tensor(VD[d][:], bank[d][1], stat(kdec, tiles[d], d), ALU.mult).then_inc(vd_ready[d], 1)
            for d in R2:
                o = oT[:, :, ds(tiles[d] * P, P)]
                dve.wait_ge(o_ready[d], primed(s + 1))
                dve.wait_ge(o_added[1 - d], primed(s + d))
                nc.vector.tensor_tensor(o, o, bank[d][2], ALU.add).then_inc(o_added[d], 1)
                dve.wait_ge(ds_ready[d], primed(s + 1))
                dve.wait_ge(s_scaled[d], primed(s + 1))
                nc.vector.tensor_tensor(S[d][:], S[d][:], bank[d][3], ALU.add).then_inc(s_ready[d], 1)
            st.end()
        passes(dve, body)

    @block.tensor
    def _(pe):
        pe.wait_ge(ones_set, primed(1))
        pe.wait_ge(prep_order, primed(3))
        for d in R2:
            pe.matmul(flat[0][d][:, 0:NT * NH], k.tri[:, d, :], la[:, :, NH * d:NH * d + NH], start=True, stop=True)
        pe.matmul(flat[0][2][:, 0:2 * NT * NH], ones[:], la[:].rearrange("p t h -> p (t h)"),
                  start=True, stop=True).then_inc(prep_pe, 1)
        pe.wait_ge(stats, primed(1))
        pe.wait_ge(state_set, primed(3))

        def heads(to, lhs, rhs, start=True, stop=True):
            for h in range(NH):
                mm = pe.matmul(to[:, h, :], lhs[:, h, :], rhs[:, h, :], start=start, stop=stop)
            return mm

        def body(s, i, u, tiles):
            for d in R2:
                pe.wait_ge(rows_in[d], primed(2 * s + 2))
                pe.wait_ge(r_ready[d], primed(s))
                pe.wait_ge(vd_ready[d], primed(s))
                pe.wait_ge(vn_copied[d], primed(s))
                pe.matmul(flat[d][0][:], ones[:], GU[d][:].rearrange("p h n -> p (h n)"), start=True, stop=True)
                pe.matmul(flat[d][1][:], ones[:], BI[d][:].rearrange("p h n -> p (h n)"), start=True,
                          stop=True).then_inc(g_rows[d], 1)
            for d in R2:
                pe.wait_ge(tile_in[d][u], primed((i + 1) * 48))
                pe.wait_ge(o_added[d], primed(s))
                pe.wait_ge(s_ready[d], primed(s))
                heads(bank[d][2], KT[d][u], KT[d][u])
                heads(bank[d][3], KT[d][u], QT[d][u]).then_inc(kk_ready[d], 1)
            for d in R2:
                pe.wait_ge(at_ready[d], primed(s + 1))
                pe.wait_ge(eg_ready[d], primed(s + 1))
                for h in range(NH):
                    mm = pe.transpose(bank[d][0][:, h, :], AT[d][:, h, :], k.eye[:])
                mm.then_inc(a_turned[d], 1)
            for n in range(MERGES):
                for d in R2:
                    if n == 0:
                        pe.wait_ge(t_ready[d], primed(s + 1))
                    else:
                        pe.wait_ge(tt_ready[d], primed(s * MERGES + n))
                    heads(bank[d][1], AT[d], T[d]).then_inc(p_ready[d], 1)
                for d in R2:
                    pe.wait_ge(pm_ready[d], primed(s * MERGES + n + 1))
                    if n == 0:
                        pe.wait_ge(tt0_ready[d], primed(s + 1))
                        pe.wait_ge(kq_ready[d], primed(s + 1))
                    if n < MERGES - 1:
                        heads(bank[d][2], TT[d], Pm[d])
                    heads(bank[d][3], Pm[d], TT[d]).then_inc(dt_ready[d], 1)
            for d in R2:
                pe.wait_ge(s_ready[d], primed(s))
                heads(bank[d][0], KT[d][u], S[d]).then_inc(ks_ready[d], 1)
            for d in R2:
                pe.wait_ge(r_ready[d], primed(s + 1))
                pe.wait_ge(tt_ready[d], primed((s + 1) * MERGES))
                heads(bank[d][1], TT[d], R[d]).then_inc(vn_ready[d], 1)
            for d in R2:
                pe.wait_ge(vn_copied[d], primed(s + 1))
                pe.wait_ge(qtd_ready[d], primed(s + 1))
                for h in range(NH):
                    pe.matmul(bank[d][2][:, h, :], S[d][:, h, :], QTd[d][:, h, :], start=True, stop=False)
                    mm = pe.matmul(bank[d][2][:, h, :], VN[d][:, h, :], KQ[d][:, h, :], start=False, stop=True)
                mm.then_inc(o_ready[d], 1)
            for d in R2:
                pe.wait_ge(vd_ready[d], primed(s + 1))
                heads(bank[d][3], K[d][u], VD[d]).then_inc(ds_ready[d], 1)
        passes(pe, body)


def gate_heads(k, oT, early):
    nc, dr = k.nc, k.dram
    ones, wn = k.sb("ones", [P, P]), k.sb("out_norm", [P, 1])
    sq, r = k.sb("squares", [P, 3, 512]), k.sb("rstd", [P, 3, 512])
    w_in, ones_set, sq_ready, sum_ready = k.sem("w_in"), k.sem("ones_set"), k.sem("sq_ready"), k.sem("sum_ready")
    mean_ready, root_ready, gated, order = k.sem("mean_ready"), k.sem("root_ready"), k.sem("gated"), k.sem("dve_order")
    normed = k.sem("normed")
    block = k.block()

    def span(x, h, at, width):
        return x[:, ds(h, 1), at:at + width].rearrange("p a n -> p (a n)")

    @block.sync
    def _(sp):
        sp.dma_start(wn[:], dr["ab_out_norm"].rearrange("a p -> p a")).then_inc(w_in, 16)
        early.load(sp)

    @block.gpsimd
    def _(pool):
        nc.gpsimd.memset(ones[:], 1.0).then_inc(ones_set, 1)
        with pool.Fori(0, NH) as h:
            for n, (at, width) in enumerate(SPANS):
                pool.wait_ge(normed, primed(h * 3 + n + 1))
                o = span(oT, h, at, width)
                nc.gpsimd.tensor_tensor(o, o, span(k.gate, h, at, width), ALU.mult).then_inc(gated, 1)

    @block.scalar
    def _(act):
        with act.Fori(0, NH) as h:
            for n, (at, width) in enumerate(SPANS):
                act.wait_ge(sum_ready, primed(h * 3))
                nc.scalar.activation(sq[:, n, 0:width], span(oT, h, at, width), ACT.Square).then_inc(sq_ready, 1)
            for n, (at, width) in enumerate(SPANS):
                act.wait_ge(mean_ready, primed(h * 3 + n + 1))
                nc.scalar.activation(r[:, n, 0:width], r[:, n, 0:width], ACT.Sqrt).then_inc(root_ready, 1)

    @block.tensor
    def _(pe):
        pe.wait_ge(ones_set, primed(1))
        with pe.Fori(0, NH) as h:
            for n, (at, width) in enumerate(SPANS):
                pe.wait_ge(sq_ready, primed(h * 3 + n + 1))
                pe.wait_ge(mean_ready, primed(h * 3))
                pe.matmul(k.bank[n][:, 0:width], ones[:], sq[:, n, 0:width], start=True, stop=True).then_inc(sum_ready, 1)

    @block.vector
    def _(dve):
        dve.wait_ge(w_in, primed(16))
        st = Steps(dve, order, 3)
        with dve.Fori(0, NH) as h:
            st.at(h)
            for n, (at, width) in enumerate(SPANS):
                dve.wait_ge(sum_ready, primed(h * 3 + n + 1))
                dve.wait_ge(normed, primed(h * 3))
                nc.vector.tensor_scalar(r[:, n, 0:width], k.bank[n][:, 0:width], 1.0 / P, EPS, ALU.mult,
                                        ALU.add).then_inc(mean_ready, 1)
            for n, (at, width) in enumerate(SPANS):
                dve.wait_ge(root_ready, primed(h * 3 + n + 1))
                st.link(nc.vector.reciprocal(r[:, n, 0:width], r[:, n, 0:width]))
                o = span(oT, h, at, width)
                nc.vector.scalar_tensor_tensor(out=o, in0=o, scalar=wn[:], in1=r[:, n, 0:width],
                                               op0=ALU.mult, op1=ALU.mult).then_inc(normed, 1)
            st.end()


def project_out(k, l, first, lhs, weights):
    nc, dr = k.nc, k.dram
    w, w_in, g = weights.w, weights.w_in, k.sb("gate_rows", [P, 2, D])
    y = k.sb("y", [P, 2, D])
    g_in, y_ready, y_scaled, h_added = k.sem("g_in"), k.sem("y_ready"), k.sem("y_scaled"), k.sem("h_added")
    block = k.block()
    tiles = range(first, NT)

    @block.sync
    def _(sp):
        for v in range(2):
            spread_row(k, sp, g[:, v, :], l, v, 2, g_in)

    @block.tensor
    def _(pe):
        pe.wait_ge(w_in, primed(weights.all_in))
        for n, t in enumerate(tiles):
            if n >= 2:
                pe.wait_ge(y_scaled, primed(2 * n - 2))
            for half in range(2):
                for c in range(KC):
                    mm = pe.matmul(k.bank[2 * (n % 2) + half][:], lhs(c, t), w[:, c, half * 512:(half + 1) * 512],
                                   start=(c == 0), stop=(c == KC - 1))
                mm.then_inc(y_ready, 1)

    @block.vector
    def _(dve):
        dve.wait_ge(g_in, primed(32))
        for n, t in enumerate(tiles):
            if n >= 2:
                dve.wait_ge(h_added, primed(n - 1))
            for half in range(2):
                dve.wait_ge(y_ready, primed(2 * n + half + 1))
                nc.vector.tensor_tensor(y[:, n % 2, half * 512:(half + 1) * 512], k.bank[2 * (n % 2) + half][:],
                                        g[:, 0 if t < CT else 1, half * 512:(half + 1) * 512],
                                        ALU.mult).then_inc(y_scaled, 1)

    @block.gpsimd
    def _(pool):
        for n, t in enumerate(tiles):
            pool.wait_ge(y_scaled, primed(2 * n + 2))
            nc.gpsimd.tensor_tensor(k.H[:, t, :], k.H[:, t, :], y[:, n % 2, :], ALU.add).then_inc(h_added, 1)


class Table:
    BLOCKS, LAST, ACTIVE = 0, 1, 2
    EXPERT = 3
    BLOCKS_UPTO = EXPERT + NE
    OF_BLOCK = BLOCKS_UPTO + NE
    PER = 2 + RING + 3
    NEXT = 2 + RING
    SIZE = OF_BLOCK + PER * (MAXP + 1)


def route(k, first, logits, slots, wts, table):
    nc, dr = k.nc, k.dram
    T = NT - first
    ramp = k.sb("ramp", [P, P])
    late = k.sb("ramp_plus_128", [P, P])
    ones, strict = k.sb("ones", [P, P]), k.sb("strict", [P, P])
    gmax, gi, gsum = k.sb("gmax", [P, T]), k.sb("gi", [P, T]), k.sb("gsum", [P, T])
    gx, gc, gh = k.sb("g_shifted", [P, T, GROUPS]), k.sb("g_cand", [P, T, GROUPS]), k.sb("g_hot", [P, T, GROUPS])
    ex = k.sb("in_group", [P, T, PER])
    big = k.sb("big", [P, T, GROUPS, PER])
    em, ei, ec = k.sb("e_max", [P, 2, T]), k.sb("e_index", [P, T]), k.sb("e_cand", [P, T, PER])
    eh = k.sb("e_hot", [P, 2, T, PER])
    hot = k.sb("hot", [P, 2, T, NE])
    cnt, pos, run = k.sb("chosen", [P, T, NE]), k.sb("position", [P, T, NE]), k.sb("running", [P, NE])
    MOST = TOK // UNIT
    U = 2 * (MAXP + 1)
    units, incl, excl = k.sb("units", [P, NE]), k.sb("units_upto", [P, NE]), k.sb("units_before", [P, NE])
    over, thresholds = k.sb("over", [P, NE, MOST]), k.sb("thresholds", [P, MOST])
    active, rank_upto, rank = k.sb("active", [P, NE]), k.sb("active_upto", [P, NE]), k.sb("active_before", [P, NE])
    far, last = k.sb("units_upto_if_active", [P, NE]), k.sb("last_rank", [P, 1])
    cmp, owner = k.sb("compare", [P, U, NE]), k.sb("owner_rank", [P, U])
    triple, rounds = k.sb("multiples_of_ring", [P, NE // RING + 1]), k.sb("rounds", [P, RING, U])
    last_unit, thresholds2 = k.sb("units_upto_rank", [P, NE]), k.sb("even_numbers", [P, MAXP])
    blocks_of = k.sb("blocks_of", [P, NE, MAXP])
    nxt = k.sb("next_rank", [P, MAXP + 1])
    ratio, inv = k.sb("ratio", [P, T]), k.sb("inv", [P, T])
    sf, tf = k.sb("slots_f32", [P, 2, T]), k.sb("table_f32", [P, Table.SIZE])
    tok, zero = k.sb("token", [P, T], I32), k.sb("no_token", [P, MAXP + 1], I32)
    c_in, order, exps, counted, tokens = k.sem("c_in"), k.sem("order"), k.sem("exps"), k.sem("counted"), k.sem("tokens")
    shifted, ratio_set, hot_ready = k.sem("shifted"), k.sem("ratio_set"), k.sem("hot_ready")
    cleared, slots_ready, scattered, consts = k.sem("cleared", 0), k.sem("slots_ready"), k.sem("scattered", 0), k.sem("consts")
    block = k.block()

    @block.sync
    def _(sp):
        sp.dma_start(ramp[:], dr["const_ramp"].to_broadcast([P, P])).then_inc(c_in, 16)

    @block.gpsimd
    def _(pool):
        nc.gpsimd.memset(ones[:], 1.0).then_inc(consts, 1)
        nc.gpsimd.tensor_tensor(strict[:], k.tri[:, 0, :], k.eye[:], ALU.subtract).then_inc(consts, 1)
        nc.gpsimd.iota(tok[:], [[P, T]], base=first * P, channel_multiplier=1).then_inc(tokens, 1)
        nc.gpsimd.memset(zero[:], first * P).then_inc(tokens, 1)
        pool.wait_ge(tokens, primed(2))
        pool.dma_start(dr["slot_token"].rearrange("(p b) a -> p (b a)", p=P), zero[:]).then_inc(cleared, 16)
        pool.wait_ge(cleared, 16)
        pool.wait_ge(slots_ready, primed(1))
        for t in range(T):
            for c in range(2):
                pool.indirect_dma_start(dr["slot_token"], bass.IndirectOffsetOnAxis(ap=slots[:, c, t:t + 1], axis=0),
                                        tok[:, t:t + 1], None).then_inc(scattered, 16)
        pool.wait_ge(scattered, 32 * T)

    @block.scalar
    def _(act):
        act.wait_ge(shifted, primed(1))
        nc.scalar.activation(gx[:], gx[:], ACT.Exp).then_inc(exps, 1)
        act.wait_ge(ratio_set, primed(1))
        nc.scalar.activation(ratio[:], ratio[:], ACT.Exp).then_inc(exps, 1)

    @block.tensor
    def _(pe):
        pe.wait_ge(consts, primed(2))
        pe.wait_ge(hot_ready, primed(1))
        flat = cnt[:].rearrange("p t e -> p (t e)")
        pe.matmul(k.bank[0][:, 0:T * NE], strict[:], flat, start=True, stop=True)
        pe.matmul(k.bank[1][:, 0:T * NE], ones[:], flat, start=True, stop=True).then_inc(counted, 1)

    @block.vector
    def _(dve):
        V = nc.vector
        st = Steps(dve, order)
        G, E = logits[:, :, 0:GROUPS], logits[:, :, GROUPS:].rearrange("p t (g e) -> p t g e", g=GROUPS)

        def cols(x, n):
            return x.unsqueeze(2).to_broadcast([P, T, n])

        def rows(x, n):
            return x[:, 0:n].unsqueeze(1).to_broadcast([P, T, n])

        def first_of(values, best, cand, index, is_it, n):
            st.link(V.tensor_tensor(cand, values, cols(best, n), ALU.is_equal))
            st.link(V.scalar_tensor_tensor(out=cand, in0=cand, scalar=-float(P), in1=rows(late, n), op0=ALU.mult, op1=ALU.add))
            st.link(V.tensor_reduce(index, cand, AX.X, ALU.min))
            st.link(V.tensor_tensor(is_it, rows(ramp, n), cols(index, n), ALU.is_equal))

        dve.wait_ge(c_in, primed(16))
        st.link(V.tensor_scalar(late[:], ramp[:], float(P), None, ALU.add))
        st.link(V.tensor_reduce(gmax[:], G, AX.X, ALU.max))
        st.link(V.tensor_tensor(gx[:], G, cols(gmax[:], GROUPS), ALU.subtract))
        dve.sem_inc(shifted, 1)
        first_of(G, gmax[:], gc[:], gi[:], gh[:], GROUPS)
        st.link(V.tensor_tensor(big[:], E, gh[:].unsqueeze(3).to_broadcast([P, T, GROUPS, PER]), ALU.mult))
        st.link(V.tensor_reduce(ex[:], big[:].rearrange("p t g e -> p t e g"), AX.X, ALU.add))
        for c in range(2):
            if c:
                st.link(V.scalar_tensor_tensor(out=ex[:], in0=eh[:, 0], scalar=-1e30, in1=ex[:], op0=ALU.mult, op1=ALU.add))
            st.link(V.tensor_reduce(em[:, c], ex[:], AX.X, ALU.max))
            if c:
                st.link(V.tensor_tensor(ratio[:], em[:, 1], em[:, 0], ALU.subtract))
                dve.sem_inc(ratio_set, 1)
            first_of(ex[:], em[:, c], ec[:], ei[:], eh[:, c], PER)
        for c in range(2):
            st.link(V.tensor_tensor(hot[:, c].rearrange("p t (g e) -> p t g e", g=GROUPS),
                                    gh[:].unsqueeze(3).to_broadcast([P, T, GROUPS, PER]),
                                    eh[:, c].unsqueeze(2).to_broadcast([P, T, GROUPS, PER]), ALU.mult))
        st.link(V.tensor_tensor(cnt[:], hot[:, 0], hot[:, 1], ALU.add))
        dve.sem_inc(hot_ready, 1)

        dve.wait_ge(exps, primed(2))
        st.link(V.tensor_reduce(gsum[:], gx[:], AX.X, ALU.add))
        st.link(V.reciprocal(gsum[:], gsum[:]))
        st.link(V.tensor_scalar(inv[:], ratio[:], 1.0, None, ALU.add))
        st.link(V.reciprocal(inv[:], inv[:]))
        st.link(V.tensor_tensor(wts[:, 0], gsum[:], inv[:], ALU.mult))
        st.link(V.tensor_tensor(wts[:, 1], wts[:, 0], ratio[:], ALU.mult))

        dve.wait_ge(counted, primed(1))
        st.link(V.memset(run[:], 0.0))
        for t in range(T):
            st.link(V.tensor_tensor(pos[:, t], k.bank[0][:, t * NE:(t + 1) * NE], run[:], ALU.add))
            st.link(V.tensor_tensor(run[:], run[:], k.bank[1][:, t * NE:(t + 1) * NE], ALU.add))
        st.link(V.tensor_scalar(thresholds[:], ramp[:, 0:MOST], float(UNIT), None, ALU.mult))
        st.link(V.tensor_tensor(over[:], run[:].unsqueeze(2).to_broadcast([P, NE, MOST]),
                                thresholds[:].unsqueeze(1).to_broadcast([P, NE, MOST]), ALU.is_gt))
        st.link(V.tensor_reduce(units[:], over[:], AX.X, ALU.add))
        st.link(V.tensor_tensor_scan(incl[:], ones[:, 0:NE], units[:], 0.0, ALU.mult, ALU.add))
        st.link(V.tensor_tensor(excl[:], incl[:], units[:], ALU.subtract))
        st.link(V.tensor_scalar(excl[:], excl[:], float(UNIT), None, ALU.mult))
        st.link(V.tensor_tensor(pos[:], pos[:], excl[:].unsqueeze(1).to_broadcast([P, T, NE]), ALU.add))
        b = big[:].rearrange("p t g e -> p t (g e)")
        for c in range(2):
            st.link(V.tensor_tensor(b, hot[:, c], pos[:], ALU.mult))
            st.link(V.tensor_reduce(sf[:, c], b, AX.X, ALU.add))
        V.tensor_copy(slots[:].rearrange("p c t -> p (c t)"), sf[:].rearrange("p c t -> p (c t)")).then_inc(slots_ready, 1)

        st.link(V.tensor_scalar(active[:], units[:], 1.0, None, ALU.min))
        st.link(V.tensor_tensor_scan(rank_upto[:], ones[:, 0:NE], active[:], 0.0, ALU.mult, ALU.add))
        st.link(V.tensor_tensor(rank[:], rank_upto[:], active[:], ALU.subtract))
        R = slice(0, NE)
        by_rank = ramp[:, R].unsqueeze(2).to_broadcast([P, NE, NE])
        st.link(V.tensor_tensor(cmp[:, R], rank_upto[:].unsqueeze(1).to_broadcast([P, NE, NE]), by_rank, ALU.is_le))
        st.link(V.tensor_reduce(tf[:, Table.EXPERT:Table.EXPERT + NE], cmp[:, R], AX.X, ALU.add))
        st.link(V.tensor_scalar(tf[:, Table.EXPERT:Table.EXPERT + NE], tf[:, Table.EXPERT:Table.EXPERT + NE],
                                float(NE - 1), None, ALU.min))
        st.link(V.tensor_tensor(cmp[:, R], rank[:].unsqueeze(1).to_broadcast([P, NE, NE]), by_rank, ALU.is_le))
        st.link(V.tensor_tensor(cmp[:, R], cmp[:, R], units[:].unsqueeze(1).to_broadcast([P, NE, NE]), ALU.mult))
        st.link(V.tensor_reduce(last_unit[:], cmp[:, R], AX.X, ALU.add))
        st.link(V.tensor_scalar(thresholds2[:], ramp[:, 0:MAXP], 2.0, None, ALU.mult))
        st.link(V.tensor_tensor(blocks_of[:], last_unit[:].unsqueeze(2).to_broadcast([P, NE, MAXP]),
                                thresholds2[:].unsqueeze(1).to_broadcast([P, NE, MAXP]), ALU.is_gt))
        st.link(V.tensor_reduce(tf[:, Table.BLOCKS_UPTO:Table.BLOCKS_UPTO + NE], blocks_of[:], AX.X, ALU.add))
        st.link(V.tensor_copy(tf[:, Table.BLOCKS:Table.BLOCKS + 1], tf[:, Table.BLOCKS_UPTO + NE - 1:Table.BLOCKS_UPTO + NE]))
        st.link(V.tensor_scalar(tf[:, Table.LAST:Table.LAST + 1], tf[:, Table.BLOCKS:Table.BLOCKS + 1], -1.0, None, ALU.add))
        st.link(V.tensor_copy(tf[:, Table.ACTIVE:Table.ACTIVE + 1], rank_upto[:, NE - 1:NE]))
        st.link(V.tensor_scalar(far[:], active[:], -float(2 * U), float(2 * U), ALU.mult, ALU.add))
        st.link(V.tensor_tensor(far[:], far[:], incl[:], ALU.add))
        st.link(V.tensor_tensor(cmp[:], far[:].unsqueeze(1).to_broadcast([P, U, NE]),
                                ramp[:, 0:U].unsqueeze(2).to_broadcast([P, U, NE]), ALU.is_le))
        st.link(V.tensor_reduce(owner[:], cmp[:], AX.X, ALU.add))
        st.link(V.tensor_scalar(last[:], rank_upto[:, NE - 1:NE], -1.0, None, ALU.add))
        st.link(V.tensor_scalar(owner[:], owner[:], last[:, 0:1], None, ALU.min))
        NR = NE // RING + 1
        st.link(V.tensor_scalar(triple[:], ramp[:, 0:NR], float(RING), None, ALU.mult))
        for r in range(RING):
            if r:
                st.link(V.tensor_scalar(triple[:], triple[:], 1.0, None, ALU.add))
            st.link(V.tensor_tensor(cmp[:, :, 0:NR], owner[:].unsqueeze(2).to_broadcast([P, U, NR]),
                                    triple[:].unsqueeze(1).to_broadcast([P, U, NR]), ALU.is_ge))
            st.link(V.tensor_reduce(rounds[:, r], cmp[:, :, 0:NR], AX.X, ALU.add))
        per = tf[:, Table.OF_BLOCK:].rearrange("p (b n) -> p b n", n=Table.PER)
        st.link(V.scalar_tensor_tensor(out=owner[:], in0=rounds[:, 0], scalar=-float(RING), in1=owner[:], op0=ALU.mult, op1=ALU.add))
        st.link(V.tensor_scalar(per[:, :, 0:2], owner[:].rearrange("p (b u) -> p b u", u=2), float(RING), None, ALU.add))
        for r in range(RING):
            st.link(V.tensor_copy(per[:, :, 2 + r], rounds[:, r, 1:U:2]))
        B = MAXP + 1
        st.link(V.tensor_tensor(cmp[:, 0:B], tf[:, Table.BLOCKS_UPTO:Table.BLOCKS_UPTO + NE].unsqueeze(1).to_broadcast([P, B, NE]),
                                ramp[:, 0:B].unsqueeze(2).to_broadcast([P, B, NE]), ALU.is_le))
        st.link(V.tensor_reduce(nxt[:], cmp[:, 0:B], AX.X, ALU.add))
        st.link(V.tensor_scalar(last[:], rank_upto[:, NE - 1:NE], -float(RING), None, ALU.add))
        st.link(V.tensor_scalar(last[:], last[:], 0.0, None, ALU.max))
        st.link(V.tensor_scalar(nxt[:], nxt[:], last[:, 0:1], None, ALU.min))
        st.link(V.tensor_scalar(per[:, :, Table.NEXT], nxt[:], float(RING), None, ALU.add))
        for u in range(2):
            if u:
                st.link(V.tensor_scalar(nxt[:], nxt[:], 1.0, None, ALU.add))
            st.link(V.tensor_scalar(triple[:], ramp[:, 1:NR + 1], float(RING), None, ALU.mult))
            st.link(V.tensor_tensor(cmp[:, 0:B, 0:NR], nxt[:].unsqueeze(2).to_broadcast([P, B, NR]),
                                    triple[:].unsqueeze(1).to_broadcast([P, B, NR]), ALU.is_ge))
            st.link(V.tensor_reduce(rounds[:, 0, 0:B], cmp[:, 0:B, 0:NR], AX.X, ALU.add))
            st.link(V.scalar_tensor_tensor(out=per[:, :, Table.NEXT + 1 + u], in0=rounds[:, 0, 0:B], scalar=-float(RING),
                                           in1=nxt[:], op0=ALU.mult, op1=ALU.add))
        st.link(V.tensor_copy(table[:], tf[:]))

    if first == 0:
        modulation(k, 1, block, banks_free=slots_ready)


def experts(k, l, first, table):
    nc, dr = k.nc, k.dram
    R2, RR = range(2), range(RING)
    LEAST = 2 * (NT - first)
    w13 = k.sb("w13", [P, RING, 2, KC * FF])
    w2 = k.sb("w2", [P, RING, FC * D])
    idx, one = k.sb("idx", [P, MAXP + 1], I32), k.sb("idx_block", [P, 1], I32)
    x, xT = k.sb("x", [P, D]), k.sb("xT", [P, KC, P])
    h, hT, y = k.sb("h", [P, FF]), k.sb("hT", [P, FC, P]), k.sb("y", [P, D])
    idx_in, gather_due, all_stored = k.sem("idx_in", 0), k.sem("gather_due"), k.sem("all_stored")
    w13_in, w2_in = [k.sem(f"w13_in{r}") for r in RR], [k.sem(f"w2_in{r}") for r in RR]
    idx_ready, x_in, x_turned = k.sem("idx_ready"), k.sem("x_in", 0), k.sem("x_turned")
    xT_act, xT_dve = k.sem("xT_act"), k.sem("xT_dve")
    xw1_ready, up_ready, silu_ready = k.sem("xw1_ready"), k.sem("up_ready"), k.sem("silu_ready")
    h_ready, h_turned, hT_ready = k.sem("h_ready"), k.sem("h_turned"), k.sem("hT_ready")
    y0_mm, y_mm, y_dve, y_act, y_stored = (k.sem(n) for n in ("y0_mm", "y_mm", "y_dve", "y_act", "y_stored"))
    block = k.block()

    def passes(eng, body):
        with eng.Fori(1, LEAST) as j:
            body(j)
        count = eng.value_load(table[0:1, Table.BLOCKS:Table.BLOCKS + 1], min_val=LEAST, max_val=MAXP)
        with eng.Fori(LEAST, MAXP) as j:
            with eng.If(j < count):
                body(j)
        return eng.value_load(table[0:1, Table.LAST:Table.LAST + 1], min_val=LEAST - 1, max_val=MAXP - 1)

    @block.sync
    def _(sp):
        def entry(base, m, lo, hi):
            return sp.value_load(table[0:1, ds(m + base, 1)], min_val=lo, max_val=hi)

        def load13(m, r, wait=True):
            e = entry(Table.EXPERT, m, 0, NE - 1)
            used = entry(Table.BLOCKS_UPTO, m - RING, 1, MAXP) if wait else None
            for half, name in enumerate(("moe_w1", "moe_w3")):
                if wait:
                    sp.wait_ge((xw1_ready, up_ready)[half], primed(used))
                sp.dma_start(w13[:, r, half, :], dr[name][l, ds(e, 1)].rearrange("a (p j) n -> p (a j n)", p=P)).then_inc(w13_in[r], 16)

        active = sp.value_load(table[0:1, Table.ACTIVE:Table.ACTIVE + 1], min_val=1, max_val=NE)
        sp.wait_ge(idx_in, 16)
        load13(0, 0, wait=False)
        sp.wait_ge(x_in, 16)
        for m in range(1, RING):
            with sp.If(active > m):
                load13(m, m, wait=False)
        with sp.Fori(1, NE // RING + 1) as i:
            for r in RR:
                with sp.If(i * RING + r < active):
                    load13(i * RING + r, r)

    @block.gpsimd
    def _(pool):
        with nc.allow_non_contiguous_dma(reason="slots of a block over partitions"):
            pool.dma_start(idx[:], dr["slot_token"].rearrange("(b p) a -> p (b a)", p=P)).then_inc(idx_in, 16)
        pool.wait_ge(idx_in, 16)

        def gather(j):
            if not isinstance(j, int) or j:
                pool.wait_ge(x_in, j * 16)
            nc.gpsimd.tensor_copy(one[:], idx[:, ds(j, 1)]).then_inc(idx_ready, 1)
            if not isinstance(j, int) or j:
                pool.wait_ge(x_turned, primed(j))
            pool.wait_ge(idx_ready, primed(j + 1))
            pool.sem_inc(gather_due, 1)
            pool.indirect_dma_start(x[:], None, dr["moe_x"],
                                    bass.IndirectOffsetOnAxis(ap=one[:, 0:1], axis=0)).then_inc(x_in, 16)
        gather(0)
        gather(1)
        passes(pool, lambda j: gather(j + 1))

    X, UP, HT, Y = (0, 1), (2, 3), 4, (5, 6)

    @block.tensor
    def _(pe):
        def entry(j, n, hi):
            return pe.value_load(table[0:1, ds(j * Table.PER + (Table.OF_BLOCK + n), 1)], min_val=0, max_val=hi)

        def by_buffer(buf, products):
            for r in RR:
                with pe.If(buf == r):
                    products(r)

        def turn_x(j):
            pe.wait_ge(x_in, j * 16 + 16)
            if not isinstance(j, int) or j:
                pe.wait_ge(xT_act, primed(j))
                pe.wait_ge(xT_dve, primed(j))
            for c in range(KC):
                t = pe.transpose(k.bank[X[c // 4]][:, (c % 4) * P:(c % 4 + 1) * P], x[:, c:D:KC], k.eye[:])
            t.then_inc(x_turned, 1)

        def turn_h(j):
            pe.wait_ge(h_ready, primed(j + 1))
            for c in range(FC):
                t = pe.transpose(k.bank[HT][:, c * P:(c + 1) * P], h[:, c:FF:FC], k.eye[:])
            t.then_inc(h_turned, 1)

        def owners(j):
            return [entry(j, u, RING - 1) for u in R2], [entry(j, 2 + r, NE) for r in RR]

        def up(j, buf, loads):
            pe.wait_ge(xT_act, primed(j + 1))
            pe.wait_ge(xT_dve, primed(j + 1))
            for r in RR:
                pe.wait_ge(w13_in[r], primed(loads[r] * 32))

            def products(r):
                for half in R2:
                    for c in range(KC):
                        for u in R2:
                            mm = pe.matmul(k.bank[UP[half]][u * UNIT:(u + 1) * UNIT, :], xT[:, c, u * UNIT:(u + 1) * UNIT],
                                           w13[:, r if u else ds(buf[0], 1), half, c * FF:(c + 1) * FF].rearrange(
                                               "p n -> p n" if u else "p a n -> p (a n)"),
                                           start=(c == 0), stop=(c == KC - 1))
                    mm.then_inc((xw1_ready, up_ready)[half], 1)
            by_buffer(buf[1], products)

        def down(j):
            buf, loads = owners(j)
            pe.wait_ge(hT_ready, primed(j + 1))
            pe.wait_ge(y_dve, primed(j))
            pe.wait_ge(y_act, primed(j))
            for r in RR:
                pe.wait_ge(w2_in[r], primed(loads[r] * 16))

            def products(r):
                for half in R2:
                    for c in range(FC):
                        for u in R2:
                            at = c * D + half * 512
                            mm = pe.matmul(k.bank[Y[half]][u * UNIT:(u + 1) * UNIT, :], hT[:, c, u * UNIT:(u + 1) * UNIT],
                                           w2[:, r if u else ds(buf[0], 1), at:at + 512].rearrange(
                                               "p n -> p n" if u else "p a n -> p (a n)"),
                                           start=(c == 0), stop=(c == FC - 1))
                    mm.then_inc((y0_mm, y_mm)[half], 1)
            by_buffer(buf[1], products)

        turn_x(0)
        turn_x(1)
        up(0, *owners(0))

        def body(j):
            of_block = owners(j)
            turn_x(j + 1)
            turn_h(j - 1)
            up(j, *of_block)
            down(j - 1)
        last = passes(pe, body)
        turn_h(last)
        down(last)

    def copy_xT(half):
        return xT[:, 4 * half:4 * half + 4, :], k.bank[X[half]][:].rearrange("p (c q) -> p c q", c=4)

    @block.scalar
    def _(act):
        def first(j):
            act.wait_ge(xw1_ready, primed(j + 1))
            if not isinstance(j, int):
                act.wait_ge(h_turned, primed(j))
            nc.scalar.activation(h[:], k.bank[UP[0]][:], ACT.Silu).then_inc(silu_ready, 1)
            turned(j + 1)

        def turned(j):
            act.wait_ge(x_turned, primed(j + 1))
            if not isinstance(j, int) or j:
                act.wait_ge(up_ready, primed(j))
            nc.scalar.copy(*copy_xT(0)).then_inc(xT_act, 1)

        def second(j):
            act.wait_ge(y_mm, primed(j + 1))
            act.wait_ge(y_stored, primed(j * 16))
            nc.scalar.copy(y[:, 512:], k.bank[Y[1]][:]).then_inc(y_act, 1)
            act.wait_ge(y_act, primed(j + 1))
            act.wait_ge(y_dve, primed(j + 1))
            act.dma_start(dr["moe_y"][ds(j * P, P), :], y[:]).then_inc(y_stored, 16)

        def value(column, lo, hi):
            return act.value_load(table[0:1, ds(column, 1)], min_val=lo, max_val=hi)

        def load2(rank, r):
            e = value(rank + Table.EXPERT, 0, NE - 1)
            act.dma_start(w2[:, r, :], dr["moe_w2"][l, ds(e, 1)].rearrange("a (p j) n -> p (a j n)", p=P)).then_inc(w2_in[r], 16)

        def refill(j):
            per = j * Table.PER + Table.OF_BLOCK
            lo, hi = value(per + Table.NEXT, RING, NE), value(per + (Table.PER + Table.NEXT), RING, NE)
            for u in R2:
                with act.If(lo + u < hi):
                    buf = value(per + (Table.NEXT + 1 + u), 0, RING - 1)
                    for r in RR:
                        with act.If(buf == r):
                            load2(lo + u, r)

        active = value(Table.ACTIVE, 1, NE)
        act.wait_ge(x_in, 16)
        for m in RR:
            with act.If(active > m):
                load2(m, m)
        turned(0)
        first(0)

        def body(j):
            first(j)
            second(j - 1)
            refill(j - 1)
        last = passes(act, body)
        second(last)
        act.wait_ge(y_stored, primed(last * 16 + 16))
        act.sem_inc(all_stored, 1)

    @block.vector
    def _(dve):
        def turned(j):
            dve.wait_ge(x_turned, primed(j + 1))
            if not isinstance(j, int) or j:
                dve.wait_ge(up_ready, primed(j))
            nc.vector.tensor_copy(*copy_xT(1)).then_inc(xT_dve, 1)

        def first(j):
            dve.wait_ge(silu_ready, primed(j + 1))
            dve.wait_ge(up_ready, primed(j + 1))
            nc.vector.tensor_tensor(h[:], h[:], k.bank[UP[1]][:], ALU.mult).then_inc(h_ready, 1)
            turned(j + 1)

        def copy_hT(j):
            dve.wait_ge(h_turned, primed(j + 1))
            dve.wait_ge(y_mm, primed(j))
            nc.vector.tensor_copy(hT[:].rearrange("p c q -> p (c q)"), k.bank[HT][:]).then_inc(hT_ready, 1)

        def second(j):
            dve.wait_ge(y0_mm, primed(j + 1))
            dve.wait_ge(y_stored, primed(j * 16))
            nc.vector.tensor_copy(y[:, 0:512], k.bank[Y[0]][:]).then_inc(y_dve, 1)

        turned(0)
        first(0)

        def body(j):
            copy_hT(j - 1)
            first(j)
            second(j - 1)
        last = passes(dve, body)
        copy_hT(last)
        second(last)


def combine(k, l, first, slots, wts, final=False):
    nc, dr, H = k.nc, k.dram, k.H
    R2 = range(2)
    T = NT - first
    g = k.sb("gate_rows", [P, 2, D])
    y = k.sb("y", [P, T, 2, D])
    g_in, order = k.sem("g_in"), k.sem("order")
    y_in = [k.sem(f"y_in{n}", 0) for n in range(T)]
    scaled, gated, added = k.sem("scaled"), k.sem("gated"), [k.sem(f"added{u}") for u in R2]
    if final:
        w, sq, r = k.sb("norm_rows", [P, D]), k.sb("squares", [P, 2, D]), k.sb("rstd", [P, T])
        w_in, sum_ready, mean_ready, root_ready = k.sem("w_in"), k.sem("sum_ready"), k.sem("mean_ready"), k.sem("root_ready")
        normed, out_stored = k.sem("normed"), k.sem("out_stored")
    block = k.block()

    @block.sync
    def _(sp):
        for v in R2:
            spread_row(k, sp, g[:, v, :], l, v, 5, g_in)
        if final:
            sp.dma_start(w[:], dr["norm_final"].rearrange("(a n) -> a n", a=1).to_broadcast([P, D])).then_inc(w_in, 16)
            out = dr["out"].rearrange("a t d -> (a t) d")
            for n in range(T):
                sp.wait_ge(normed, primed(n + 1))
                sp.dma_start(out[n * P:(n + 1) * P, :], y[:, n, 0, :]).then_inc(out_stored, 16)
            sp.wait_ge(out_stored, primed(16 * T))

    @block.gpsimd
    def _(pool):
        for n in range(T):
            for c in R2:
                pool.indirect_dma_start(y[:, n, c, :], None, dr["moe_y"],
                                        bass.IndirectOffsetOnAxis(ap=slots[:, c, n:n + 1], axis=0)).then_inc(y_in[n], 16)
        for n in range(1, T, 2):
            pool.wait_ge(gated, primed(n + 1))
            nc.gpsimd.tensor_tensor(H[:, first + n, :], H[:, first + n, :], y[:, n, 1, :], ALU.add).then_inc(added[1], 1)

    @block.scalar
    def _(act):
        def root(n):
            act.wait_ge(mean_ready, primed(n + 1))
            nc.scalar.activation(r[:, n:n + 1], r[:, n:n + 1], ACT.Sqrt).then_inc(root_ready, 1)

        for n in range(T):
            act.wait_ge(y_in[n], 32)
            nc.scalar.activation(y[:, n, 0, :], y[:, n, 0, :], ACT.Copy, scale=wts[:, 0, n:n + 1]).then_inc(scaled, 1)
        if final:
            for n in range(T):
                act.wait_ge(added[n % 2], primed(n // 2 + 1))
                nc.scalar.activation(sq[:, n % 2, :], H[:, first + n, :], ACT.Square,
                                     accum_out=r[:, n:n + 1]).then_inc(sum_ready, 1)
                if n:
                    root(n - 1)
            root(T - 1)

    @block.vector
    def _(dve):
        dve.wait_ge(g_in, primed(32))
        st = Steps(dve, order)

        def mean(n):
            dve.wait_ge(sum_ready, primed(n + 1))
            nc.vector.tensor_scalar(r[:, n:n + 1], r[:, n:n + 1], 1.0 / D, EPS, ALU.mult, ALU.add).then_inc(mean_ready, 1)

        for n in range(T):
            dve.wait_ge(scaled, primed(n + 1))
            st.link(nc.vector.scalar_tensor_tensor(out=y[:, n, 1, :], in0=y[:, n, 1, :], scalar=wts[:, 1, n:n + 1],
                                                   in1=y[:, n, 0, :], op0=ALU.mult, op1=ALU.add))
            nc.vector.tensor_tensor(y[:, n, 1, :], y[:, n, 1, :], g[:, 0 if first + n < CT else 1, :],
                                    ALU.mult).then_inc(gated, 1)
            if n % 2 == 0:
                dve.wait_ge(gated, primed(n + 1))
                nc.vector.tensor_tensor(H[:, first + n, :], H[:, first + n, :], y[:, n, 1, :], ALU.add).then_inc(added[0], 1)
        if final:
            dve.wait_ge(w_in, primed(16))
            mean(0)
            for n in range(T):
                if n + 1 < T:
                    mean(n + 1)
                dve.wait_ge(root_ready, primed(n + 1))
                st.link(nc.vector.reciprocal(r[:, n:n + 1], r[:, n:n + 1]))
                nc.vector.scalar_tensor_tensor(out=y[:, n, 0, :], in0=H[:, first + n, :], scalar=r[:, n:n + 1],
                                               in1=w[:], op0=ALU.mult, op1=ALU.mult).then_inc(normed, 1)


def moe(k, l, first):
    with k.scope():
        T = NT - first
        slots, wts = k.sb("slots", [P, 2, T], I32), k.sb("weights", [P, 2, T])
        table = k.sb("table", [P, Table.SIZE], I32)
        with k.scope():
            logits = k.sb("logits", [P, T, GROUPS + NE])
            with k.scope():
                norm_mod(k, l, 1, first, logits=logits)
            with k.scope():
                route(k, first, logits, slots, wts, table)
        with k.scope():
            experts(k, l, first, table)
        with k.scope():
            combine(k, l, first, slots, wts, final=(l == 1))


def project1(k, aT, weights):
    nc, dr = k.nc, k.dram
    R2 = range(2)
    QW, KW = ATT_H * HD, ATT_KV * HD
    RH = (QW + KW) // HD
    NF = HD // 4
    w, w_in = weights.w, weights.w_in
    rope = k.sb("rope", [P, LT, 2, 2, NF])
    z, rt = [k.sb(f"z{s}", [P, ATT_COLS]) for s in R2], [k.sb(f"rotated{s}", [P, RH, 2, 2, NF]) for s in R2]
    kd = [k.sb(f"k_twice{s}", [P, ATT_KV, 2, HD]) for s in R2]
    out = [k.sb(f"turned{s}", [P, 12, P]) for s in R2]
    t1, t2, t3, t4 = (k.sb(f"t{n}", [P, RH, 2, NF]) for n in range(4))
    pad = k.sb("zero", [P, ATT_KV * P])
    rope_in, z_ready, z_copied = k.sem("rope_in"), k.sem("z_ready"), k.sem("z_copied")
    first_ready, second_ready, kd_ready = k.sem("first_ready"), k.sem("second_ready"), k.sem("kd_ready")
    turned, taken, dve_order, pool_order = k.sem("turned"), k.sem("taken"), k.sem("dve_order"), k.sem("pool_order")
    stored, pad_set, padded = [k.sem(f"stored{s}") for s in R2], k.sem("pad_set"), k.sem("padded")
    block = k.block()

    def rounds(t):
        return t if t < CT else CT + 3 * (t - CT)

    def stores(t):
        return sum(48 if x >= CT else 32 for x in range(t % 2, t, 2))

    def place(t):
        return t - CT + 1 if t >= CT else LT + 2 + t

    @block.sync
    def _(sp):
        sp.dma_start(rope[:].rearrange("p t a b f -> p t (a b f)"),
                     dr["const_rope"].rearrange("(t p) a b f -> p t (a b f)", p=P)).then_inc(rope_in, 16)
        sp.wait_ge(pad_set, primed(1))
        for at in (0, LT + 1):
            sp.dma_start(dr["att_k"][at], pad[:]).then_inc(padded, 16)
            sp.dma_start(dr["att_v"][at], pad[:, 0:KW]).then_inc(padded, 16)
        for t in range(NT):
            s = t % 2
            sp.wait_ge(taken, primed(rounds(t + 1)))
            if t >= CT:
                sp.dma_start(dr["att_q"][t - CT], out[s][:, 0:8, :].rearrange("p c n -> p (c n)")).then_inc(stored[s], 16)
            sp.dma_start(dr["att_k"][place(t)], out[s][:, 8:12, :].rearrange("p c n -> p (c n)")).then_inc(stored[s], 16)
            sp.dma_start(dr["att_v"][place(t)], z[s][:, QW + KW:]).then_inc(stored[s], 16)
        for s in R2:
            sp.wait_ge(stored[s], primed(stores(NT + s)))
        sp.wait_ge(padded, primed(64))

    @block.tensor
    def _(pe):
        pe.wait_ge(w_in, primed(weights.all_in))

        def project(t):
            s = t % 2
            if t >= 2:
                pe.wait_ge(z_copied, primed(t - 1))
            for g in ((2,) if t < CT else (0, 1, 2)):
                for c in range(KC):
                    mm = pe.matmul(k.bank[3 * s + g][:], aT[:, c, t * P:(t + 1) * P], w[:, c, g * 512:(g + 1) * 512],
                                   start=(c == 0), stop=(c == KC - 1))
            mm.then_inc(z_ready, 1)

        def turn(t):
            s = t % 2
            pe.wait_ge(kd_ready, primed(t + 1))
            for g in ((2,) if t < CT else (0, 1, 2)):
                r = rounds(t) + (g if t >= CT else 0)
                if r >= 2:
                    pe.wait_ge(taken, primed(r - 1))
                for q in range(4):
                    c = 4 * g + q
                    src = (kd[s][:].rearrange("p h a d -> p (h a d)")[:, (c - 8) * P:(c - 7) * P] if g == 2 else
                           rt[s][:].rearrange("p h a b f -> p (h a b f)")[:, c * P:(c + 1) * P])
                    mm = pe.transpose(k.bank[6 + r % 2][:, q * P:(q + 1) * P], src, k.eye[:])
                mm.then_inc(turned, 1)

        for t in range(NT + 1):
            if t < NT:
                project(t)
            if t > 0:
                turn(t - 1)

    @block.scalar
    def _(act):
        for t in range(NT + 1):
            if t < NT:
                s = t % 2
                act.wait_ge(z_ready, primed(t + 1))
                if t >= 2:
                    act.wait_ge(stored[s], primed(stores(t)))
                for g in ((2,) if t < CT else (0, 1, 2)):
                    c = nc.scalar.copy(z[s][:, g * 512:(g + 1) * 512], k.bank[3 * s + g][:])
                c.then_inc(z_copied, 1)
                if t < CT:
                    act.wait_ge(z_copied, primed(t + 1))
                    keys = z[s][:, QW:QW + KW].rearrange("p (h d) -> p h d", h=ATT_KV)
                else:
                    act.wait_ge(first_ready, primed(t - CT + 1))
                    act.wait_ge(second_ready, primed(t - CT + 1))
                    keys = rt[s][:, ATT_H:, :, :, :].rearrange("p h a b f -> p h (a b f)")
                if t >= 2:
                    act.wait_ge(turned, primed(rounds(t - 1)))
                nc.scalar.copy(kd[s][:], keys.unsqueeze(2).to_broadcast([P, ATT_KV, 2, HD])).then_inc(kd_ready, 1)
            if t > 0:
                u = t - 1
                for g in ((2,) if u < CT else (0, 1, 2)):
                    r = rounds(u) + (g if u >= CT else 0)
                    act.wait_ge(turned, primed(r + 1))
                    nc.scalar.copy(out[u % 2][:, 4 * g:4 * g + 4, :].rearrange("p c n -> p (c n)"),
                                   k.bank[6 + r % 2][:]).then_inc(taken, 1)

    def halves(t):
        s = t % 2
        u = z[s][:, 0:QW + KW].rearrange("p (h a b f) -> p h a b f", a=2, b=2, f=NF)
        cos, sin = (rope[:, t - CT, n].unsqueeze(1).to_broadcast([P, RH, 2, NF]) for n in R2)
        return u[:, :, :, 0, :], u[:, :, :, 1, :], cos, sin

    @block.vector
    def _(dve):
        dve.wait_ge(rope_in, primed(16))
        st = Steps(dve, dve_order)
        for t in range(CT, NT):
            dve.wait_ge(z_copied, primed(t + 1))
            dve.wait_ge(turned, primed(rounds(t - 1)))
            a, b, cos, sin = halves(t)
            nc.vector.tensor_tensor(t1[:], a, cos, ALU.mult)
            st.link(nc.vector.tensor_tensor(t2[:], b, sin, ALU.mult))
            nc.vector.tensor_tensor(rt[t % 2][:, :, :, 0, :], t1[:], t2[:], ALU.subtract).then_inc(first_ready, 1)

    @block.gpsimd
    def _(pool):
        nc.gpsimd.memset(pad[:], 0.0).then_inc(pad_set, 1)
        pool.wait_ge(rope_in, primed(16))
        st = Steps(pool, pool_order)
        for t in range(CT, NT):
            pool.wait_ge(z_copied, primed(t + 1))
            pool.wait_ge(turned, primed(rounds(t - 1)))
            a, b, cos, sin = halves(t)
            nc.gpsimd.tensor_tensor(t3[:], a, sin, ALU.mult)
            st.link(nc.gpsimd.tensor_tensor(t4[:], b, cos, ALU.mult))
            nc.gpsimd.tensor_tensor(rt[t % 2][:, :, :, 1, :], t3[:], t4[:], ALU.add).then_inc(second_ready, 1)


def attend(k, att, early):
    nc, dr = k.nc, k.dram
    R2 = range(2)
    W, C = 3 * P, CTX
    PAIRS, KVS = ATT_H // 2, ATT_KV
    M, KM = 2 * PAIRS, 2 * KVS
    PASSES = LT // 2
    SCALE = HD ** -0.5
    q, kw = [k.sb(f"q{u}", [P, PAIRS, P]) for u in R2], [k.sb(f"k_win{u}", [P, 3, KVS, P]) for u in R2]
    vw, band = [k.sb(f"v_win{u}", [P, 3, KVS * HD]) for u in R2], [k.sb(f"band{u}", [P, W]) for u in R2]
    kc, vc = k.sb("k_ctx", [P, KVS, C]), k.sb("v_ctx", [P, CT, KVS * HD])
    sink, sink8 = k.sb("sink", [P, ATT_H]), k.sb("sink_scaled", [P, ATT_H])
    sm, pr = [k.sb(f"masked{s}", [P, 2, W]) for s in R2], [k.sb(f"probs{s}", [P, 2, W + C]) for s in R2]
    pt = [k.sb(f"probsT{s}", [P, 5, 2, 2, P]) for s in R2]
    small = [{n: k.sb(f"{n}{s}", [P, 2]) for n in ("max_win", "max_ctx", "neg_max", "sum_win", "sum_ctx",
                                                      "sink_part", "den")} for s in R2]
    ctx_in, blk_in = k.sem("ctx_in"), [k.sem(f"blk_in{u}") for u in R2]
    ctx0_ready = k.sem("ctx0_ready")
    s_ready, max_ready, p_ready, order = k.sem("s_ready"), k.sem("max_ready"), k.sem("p_ready"), k.sem("dve_order")
    inv_ready, scaled0, scaled1, sink_set = k.sem("inv_ready"), k.sem("scaled0"), k.sem("scaled1"), k.sem("sink_set")
    turned, pt_act, pt_dve = k.sem("turned"), k.sem("pt_act"), k.sem("pt_dve")
    o_ready, o_taken, den_order = k.sem("o_ready"), k.sem("o_taken"), k.sem("den_order")
    block = k.block()

    def logit_banks(m):
        return [k.bank[3 * (m % 2) + n] for n in range(3)]

    def fill(m, r):
        return 7 * (m // 2) + 3 * (m % 2) + r

    def wait_fill(pe, n, f):
        g, x = (f - 2) // 7, (f - 2) % 7
        if f < 2:
            pe.wait_ge(pt_dve, primed(n * M))
            pe.wait_ge(o_taken, primed(n * KM))
        elif x == 6:
            pe.wait_ge(o_taken, primed(n * KM + g + 1))
        elif x % 3 == 2:
            pe.wait_ge(pt_dve, primed(n * M + 2 * g + x // 3 + 1))
        else:
            pe.wait_ge(pt_act, primed(n * 2 * M + 4 * g + 2 * (x // 3) + x % 3 + 1))

    @block.sync
    def _(sp):
        for t in range(CT):
            sp.dma_start(kc[:, :, t * P:(t + 1) * P], dr["att_k"][LT + 2 + t].rearrange("p (h n) -> p h n", h=KVS)).then_inc(ctx_in, 16)
        sp.dma_start(vc[:], dr["att_v"][LT + 2:].rearrange("t p n -> p t n")).then_inc(ctx_in, 16)
        sp.dma_start(sink[:], dr["at_sink"].to_broadcast([P, ATT_H])).then_inc(ctx_in, 16)

        def load(b, u):
            sp.dma_start(q[u][:].rearrange("p c n -> p (c n)"), dr["att_q"][ds(b, 1)].rearrange("a p n -> p (a n)")).then_inc(blk_in[u], 16)
            sp.dma_start(kw[u][:].rearrange("p t h n -> p t (h n)"), dr["att_k"][ds(b, 3)].rearrange("t p n -> p t n")).then_inc(blk_in[u], 16)
            sp.dma_start(vw[u][:], dr["att_v"][ds(b, 3)].rearrange("t p n -> p t n")).then_inc(blk_in[u], 16)
            sp.dma_start(band[u][:], dr["const_band"][ds(b, 1)].rearrange("a p n -> p (a n)")).then_inc(blk_in[u], 16)

        for u in R2:
            load(u, u)
        early.load(sp)
        with sp.Fori(1, PASSES) as i:
            for u in R2:
                sp.wait_ge(o_ready, primed((i - 1) * KM + (u + 1) * KVS))
                load(i * 2 + u, u)

    @block.tensor
    def _(pe):
        pe.wait_ge(ctx_in, primed(64))

        def scores(n, m):
            u, kv, c = m // PAIRS, (m % PAIRS) // 2, m % PAIRS
            b = logit_banks(m)
            pe.wait_ge(p_ready, primed(n * M + m - 1 if m >= 2 else n * M))
            if m % PAIRS == 0:
                pe.wait_ge(blk_in[u], primed(n * 64 + 64))
            for h in R2:
                on = slice(HD * h, HD * h + HD)
                pe.matmul(b[h][:, 0:W], q[u][on, c, :], kw[u][on, :, kv, :], start=True, stop=True)
                if h:
                    pe.wait_ge(ctx0_ready, primed(n * M + m + 1))
                mm = pe.matmul(b[2][:, h * C:(h + 1) * C], q[u][on, c, :], kc[on, kv, :], start=True, stop=True)
                mm.then_inc(s_ready if h else ctx0_ready, 1)

        def turn(n, m):
            for r in range(3):
                f = fill(m, r)
                wait_fill(pe, n, f)
                for h in ((r,) if r < 2 else R2):
                    pe.wait_ge((scaled0, scaled1)[h], primed(n * M + m + 1))
                    for c in (range(4) if r < 2 else (4,)):
                        at = c * P if r < 2 else h * P
                        mm = pe.transpose(k.bank[6 + f % 2][:, at:at + P], pr[m % 2][:, h, c * P:(c + 1) * P], k.eye[:])
                mm.then_inc(turned, 1)

        def output(n, m):
            g = m // 2
            u, kv = g // KVS, g % KVS
            f = fill(m, 3)
            wait_fill(pe, n, f)
            pe.wait_ge(pt_act, primed(n * 2 * M + 2 * m + 2))
            pe.wait_ge(pt_dve, primed(n * M + m + 1))
            to = k.bank[6 + f % 2]
            for h in R2:
                for c in range(5):
                    v = vw[u][:, c, kv * HD:(kv + 1) * HD] if c < 3 else vc[:, c - 3, kv * HD:(kv + 1) * HD]
                    mm = pe.matmul(to[HD * h:HD * h + HD, 0:2 * P], v, pt[g % 2][:, c, h, :, :],
                                   start=(c == 0), stop=(c == 4))
            mm.then_inc(o_ready, 1)

        with pe.Fori(0, PASSES) as n:
            scores(n, 0)
            scores(n, 1)
            for m in range(M):
                if m + 2 < M:
                    scores(n, m + 2)
                turn(n, m)
                if m % 2:
                    output(n, m)

    @block.scalar
    def _(act):
        act.wait_ge(ctx_in, primed(64))

        def exponentials(n, m):
            s, x = m % 2, small[m % 2]
            b = logit_banks(m)
            act.wait_ge(max_ready, primed(n * M + m + 1))
            act.wait_ge(turned, primed(3 * (n * M) + 3 * (m - 1) if m >= 2 else n * (3 * M)))
            act.wait_ge(inv_ready, primed(n * M + m - 1 if m >= 2 else n * M))
            nc.scalar.activation(x["sink_part"][:], x["sink_part"][:], ACT.Exp)
            for h in R2:
                nc.scalar.activation(pr[s][:, h, 0:W], sm[s][:, h, :], ACT.Exp, bias=x["neg_max"][:, h:h + 1],
                                     scale=SCALE, accum_out=x["sum_win"][:, h:h + 1])
                e = nc.scalar.activation(pr[s][:, h, W:], b[2][:, h * C:(h + 1) * C], ACT.Exp,
                                         bias=x["neg_max"][:, h:h + 1], scale=SCALE, accum_out=x["sum_ctx"][:, h:h + 1])
            e.then_inc(p_ready, 1)

        with act.Fori(0, PASSES) as n:
            exponentials(n, 0)
            for m in range(M):
                if m + 1 < M:
                    exponentials(n, m + 1)
                for h in R2:
                    act.wait_ge(turned, primed(n * (3 * M) + 3 * m + h + 1))
                    g = m // 2
                    if m % 2 == 0 and h == 0:
                        act.wait_ge(o_ready, primed(n * KM + g - 1 if g >= 2 else n * KM))
                    nc.scalar.copy(pt[g % 2][:, 0:4, h, m % 2, :],
                                   k.bank[6 + fill(m, h) % 2][:].rearrange("p (c n) -> p c n", c=4)).then_inc(pt_act, 1)

    @block.gpsimd
    def _(pool):
        with pool.Fori(0, PASSES) as n:
            for m in range(M):
                pool.wait_ge(inv_ready, primed(n * M + m + 1))
                nc.gpsimd.tensor_tensor(pr[m % 2][:, 0, :], pr[m % 2][:, 0, :],
                                        small[m % 2]["den"][:, 0:1].to_broadcast([P, W + C]), ALU.mult).then_inc(scaled0, 1)

    @block.vector
    def _(dve):
        V = nc.vector
        dve.wait_ge(ctx_in, primed(64))
        V.tensor_scalar(sink8[:], sink[:], 1.0 / SCALE, None, ALU.mult).then_inc(sink_set, 1)
        dve.wait_ge(sink_set, primed(1))
        st = Steps(dve, order, M * 4)

        def maxima(n, m):
            u, x, b = m // PAIRS, small[m % 2], logit_banks(m)
            if m % PAIRS == 0:
                dve.wait_ge(blk_in[u], primed(n * 64 + 64))
            dve.wait_ge(s_ready, primed(n * M + m + 1))
            heads = slice(2 * (m % PAIRS), 2 * (m % PAIRS) + 2)
            V.tensor_reduce(x["max_ctx"][:], b[2][:].rearrange("p (h n) -> p h n", h=2), AX.X, ALU.max)
            for h in R2:
                r = V.tensor_tensor_reduce(out=sm[m % 2][:, h, :], in0=b[h][:, 0:W], in1=band[u][:], scale=1.0,
                                           scalar=-3e38, op0=ALU.add, op1=ALU.max, accum_out=x["max_win"][:, h:h + 1])
            st.link(r)
            st.link(V.tensor_tensor(x["max_ctx"][:], x["max_ctx"][:], x["max_win"][:], ALU.max))
            st.link(V.tensor_tensor(x["max_ctx"][:], x["max_ctx"][:], sink8[:, heads], ALU.max))
            st.link(V.tensor_scalar(x["neg_max"][:], x["max_ctx"][:], -SCALE, None, ALU.mult))
            V.tensor_tensor(x["sink_part"][:], sink[:, heads], x["neg_max"][:], ALU.add).then_inc(max_ready, 1)

        def divide(n, m):
            x = small[m % 2]
            dve.wait_ge(p_ready, primed(n * M + m + 1))
            V.tensor_tensor(x["den"][:], x["sum_win"][:], x["sum_ctx"][:], ALU.add).then_inc(den_order, 1)
            dve.wait_ge(den_order, primed((n * M + m) * 2 + 1))
            V.tensor_tensor(x["den"][:], x["den"][:], x["sink_part"][:], ALU.add).then_inc(den_order, 1)
            dve.wait_ge(den_order, primed((n * M + m) * 2 + 2))
            V.reciprocal(x["den"][:], x["den"][:]).then_inc(inv_ready, 1)
            dve.wait_ge(inv_ready, primed(n * M + m + 1))
            V.tensor_scalar(pr[m % 2][:, 1, :], pr[m % 2][:, 1, :], x["den"][:, 1:2], None, ALU.mult).then_inc(scaled1, 1)

        with dve.Fori(0, PASSES) as n:
            st.at(n)
            maxima(n, 0)
            maxima(n, 1)
            for m in range(M):
                g = m // 2
                u, kv = g // KVS, g % KVS
                divide(n, m)
                if m + 2 < M:
                    maxima(n, m + 2)
                dve.wait_ge(turned, primed(n * (3 * M) + 3 * m + 3))
                if m % 2 == 0:
                    dve.wait_ge(o_ready, primed(n * KM + g - 1 if g >= 2 else n * KM))
                V.tensor_copy(pt[g % 2][:, 4, :, m % 2, :],
                              k.bank[6 + fill(m, 2) % 2][:, 0:2 * P].rearrange("p (h n) -> p h n", h=2)).then_inc(pt_dve, 1)
                if m % 2:
                    dve.wait_ge(o_ready, primed(n * KM + g + 1))
                    V.tensor_copy(att[:, 2 * kv:2 * kv + 2, ds(n * (2 * P) + u * P, P)],
                                  k.bank[6 + fill(m, 3) % 2][:, 0:2 * P].rearrange("p (c n) -> p c n", c=2)).then_inc(o_taken, 1)
            st.end()


def constants():
    i = np.arange(P)
    tri = np.stack([i[:, None] <= i[None, :], i[:, None] >= i[None, :]]).astype(np.float32)
    merge = np.zeros((2, LEVELS, P, P), np.float32)
    for n in range(LEVELS):
        pair = (i[:, None] >> (n + 1)) == (i[None, :] >> (n + 1))
        for d, low in enumerate((i[:, None] > i[None, :], i[:, None] < i[None, :])):
            merge[d, n] = pair & low & ((i[:, None] >> n) != (i[None, :] >> n))
    nf = HD // 4
    inv = np.power(np.float32(10000.0), -np.arange(nf, dtype=np.float32) / np.float32(nf)).astype(np.float32)
    pos = np.arange(SEQ)
    angle = np.stack([(pos // 64).astype(np.float32)[:, None] * inv, (pos % 64).astype(np.float32)[:, None] * inv], 1)
    rope = np.stack([np.cos(angle), np.sin(angle)], 1).astype(np.float32)
    key = np.arange(3 * P)[None, :] - P
    near = np.abs(i[:, None] - key) <= WIN
    band = np.where(np.stack([near & (key >= 0)] + [near] * (LT - 2) + [near & (key < P)]), 0.0, -1e30).astype(np.float32)
    return {
        "const_eye": np.eye(P, dtype=np.float32),
        "const_tri": tri,
        "const_merge": merge,
        "const_rope": rope,
        "const_band": band,
        "const_ramp": np.arange(P, dtype=np.float32)[None, :],
    }


def build(nc, dram):
    k = Kernel(nc, dram)
    with k.scope():
        k.bank = [k.scopes[-1].enter_context(nc.psum_tensor(f"bank{b}", [P, 512], F32)) for b in range(8)]
        k.H = k.sb("H", [P, NT, D])
        k.eye = k.sb("eye", [P, P])
        k.tri = k.sb("tri", [P, 2, P])
        with k.scope():
            modulation(k, 0)
        with k.scope():
            k.gate = k.sb("gate", [P, NH, TOK])
            k.short = k.sb("short", [P, NH, TOK])
            k.ab = k.sb("ab", [P, NT, 4 * NH])
            with k.scope():
                aT = k.sb("aT", [P, KC, TOK])
                with k.scope():
                    norm_mod(k, 0, 0, 0, aT=aT)
                with k.scope():
                    project0(k, aT)
            with k.scope():
                oT = k.sb("oT", [P, NH, TOK])
                with k.scope():
                    delta_scan(k, oT)
                with k.scope():
                    w_out = Early(k, "ab_w_out", (0, 1))
                    with k.scope():
                        gate_heads(k, oT, w_out)
                    with k.scope():
                        project_out(k, 0, 0, lambda c, t: (oT if c < NH else k.short)[:, c % NH, t * P:(t + 1) * P], w_out)
        moe(k, 0, 0)
        with k.scope():
            aT = k.sb("aT", [P, KC, TOK])
            w_in = Early(k, "at_w_in", (2, 0, 1))
            with k.scope():
                norm_mod(k, 1, 0, 0, aT=aT, early=w_in)
            with k.scope():
                project1(k, aT, w_in)
        with k.scope():
            att = k.sb("att", [P, KC, SEQ])
            w_out = Early(k, "at_w_out", (0, 1))
            with k.scope():
                attend(k, att, w_out)
            with k.scope():
                project_out(k, 1, CT, lambda c, t: att[:, c, (t - CT) * P:(t - CT + 1) * P], w_out)
        moe(k, 1, CT)


INPUTS = ("x", "c", "ctx", "c_ctx", "ada_w", "ada_b", "norm_mix", "norm_ffn", "norm_final", "ab_w_in",
          "ab_conv_qkv", "ab_conv_sc", "ab_a_log", "ab_dt_bias", "ab_out_norm", "ab_w_out", "at_w_in",
          "at_sink", "at_w_out", "moe_w_group", "moe_w_expert", "moe_w1", "moe_w3", "moe_w2")


def kernel(**inputs):
    import concourse.bacc as bacc
    from concourse.bass_utils import run_bass_kernel_spmd

    nc = bacc.Bacc("TRN2", target_bir_lowering=False, num_devices=1)
    arrays, dram = {}, {}
    for name, a in [(n, np.ascontiguousarray(inputs[n])) for n in INPUTS] + list(constants().items()):
        arrays[f"in_{name}"] = a
        dram[name] = nc.dram_tensor(f"in_{name}", a.shape, mybir.dt.from_np(a.dtype), kind="ExternalInput").ap()
    for name, shape, dt in (
        ("mods", (2, 2, MODS * D), F32),
        ("heads", (4, NT, P, W0), F32),
        ("moe_x", (TOK, D), F32),
        ("att_q", (LT, P, ATT_H // 2 * P), F32),
        ("att_k", (NT + 2, P, ATT_KV * P), F32),
        ("att_v", (NT + 2, P, ATT_KV * HD), F32),
        ("moe_y", (SLOTS, D), F32),
        ("slot_token", (SLOTS + P, 1), I32),
    ):
        dram[name] = nc.dram_tensor(name, shape, dt).ap()
    dram["out"] = nc.dram_tensor("out", (1, SEQ, D), F32, kind="ExternalOutput").ap()
    build(nc, dram)
    r = run_bass_kernel_spmd(nc, [arrays], core_ids=[0])
    return r.results[0]["out"]
```
